# Optimizing a Trainium2 kernel written in Bass

```python
import math
import jax, jax.numpy as jnp
from jax import lax
import numpy as np

D_MODEL = 2048
BATCH = 1
SEQ = 256
DEPTH = 1

CHUNK = 64
N_MEM = 256
BRANCH_WIDTH = D_MODEL // 2
N_BRANCH = 3
GLA_HEADS = 4
GLA_DK = (D_MODEL // 4) // GLA_HEADS
GLA_DV = BRANCH_WIDTH // GLA_HEADS
GLA_RANK = 16
GLA_GATE_NORM = 16.0
DIFF_HEADS = 4
DIFF_DV = BRANCH_WIDTH // DIFF_HEADS
DIFF_DH = DIFF_DV // 2
Q_BLOCK = 128
MEM_HEADS = 4
MEM_DH = BRANCH_WIDTH // MEM_HEADS
_FF_RAW = -(-8 * D_MODEL // 3)
D_FF = -(-_FF_RAW // 256) * 256

NORM_EPS = 1e-6
NEG_INF = -1e30

IN_SIZES = (
    GLA_HEADS * GLA_DK,
    GLA_HEADS * GLA_DK,
    GLA_HEADS * GLA_DV,
    GLA_HEADS * GLA_DV,
    GLA_RANK,
    DIFF_HEADS * 2 * DIFF_DH,
    DIFF_HEADS * 2 * DIFF_DH,
    DIFF_HEADS * DIFF_DV,
    MEM_HEADS * MEM_DH,
)

kernel_name = "hybrid_gla_diffattn_memxattn_swiglu"

def rms_norm(x, g):
    xf = x.astype(jnp.float32)
    y = xf * lax.rsqrt(jnp.mean(xf * xf, axis=-1, keepdims=True) + NORM_EPS)
    return (y * g.astype(jnp.float32)).astype(x.dtype)

def split_cols(z, sizes):
    parts, start = [], 0
    for s in sizes:
        parts.append(z[..., start:start + s])
        start += s
    return parts

def gla_mixer(q, k, v, g, a_low, w_alpha_up, b_alpha, norm_g):
    B, S, _ = q.shape
    N = S // CHUNK
    f32 = jnp.float32
    log_a = jax.nn.log_sigmoid((a_low @ w_alpha_up + b_alpha).astype(f32)) / GLA_GATE_NORM

    def heads(t, d):
        return t.reshape(B, N, CHUNK, GLA_HEADS, d).transpose(0, 3, 1, 2, 4)

    qh = heads(q, GLA_DK).astype(f32) * (GLA_DK ** -0.5)
    kh = heads(k, GLA_DK).astype(f32)
    vh = heads(v, GLA_DV).astype(f32)
    bcum = jnp.cumsum(heads(log_a, GLA_DK), axis=3)
    b_last = bcum[:, :, :, -1:, :]
    q_dec = qh * jnp.exp(bcum)
    k_dec = kh * jnp.exp(-bcum)
    causal = jnp.tril(jnp.ones((CHUNK, CHUNK), dtype=bool))
    att = jnp.where(causal, jnp.einsum('bhnld,bhnmd->bhnlm', q_dec, k_dec), 0.0)
    o_intra = jnp.einsum('bhnlm,bhnmv->bhnlv', att, vh)
    k_tail = kh * jnp.exp(b_last - bcum)
    inc = jnp.einsum('bhnld,bhnlv->nbhdv', k_tail, vh)
    decay = jnp.exp(b_last[:, :, :, 0, :]).transpose(2, 0, 1, 3)

    def step(state, inp):
        dec, add = inp
        return dec[..., None] * state + add, state

    s0 = jnp.zeros((B, GLA_HEADS, GLA_DK, GLA_DV), f32)
    _, s_prev = lax.scan(step, s0, (decay, inc))
    o_inter = jnp.einsum('bhnld,nbhdv->bhnlv', q_dec, s_prev)
    o = (o_intra + o_inter).transpose(0, 2, 3, 1, 4).reshape(B, S, GLA_HEADS, GLA_DV)
    o = rms_norm(o, norm_g).reshape(B, S, GLA_HEADS * GLA_DV)
    return (o * jax.nn.silu(g.astype(f32))).astype(q.dtype)

def diff_mixer(q, k, v, qn_g, kn_g, lq1, lk1, lq2, lk2, subln_g, lam_init):
    B, S, _ = q.shape
    f32 = jnp.float32
    qh = rms_norm(q.reshape(B, S, DIFF_HEADS, 2, DIFF_DH), qn_g).transpose(0, 2, 3, 1, 4)
    kh = rms_norm(k.reshape(B, S, DIFF_HEADS, 2, DIFF_DH), kn_g).transpose(0, 2, 3, 1, 4)
    vh = v.reshape(B, S, DIFF_HEADS, DIFF_DV).transpose(0, 2, 1, 3)
    lam = (jnp.exp(jnp.sum(lq1 * lk1).astype(f32)) - jnp.exp(jnp.sum(lq2 * lk2).astype(f32))
           + lam_init)
    nb = S // Q_BLOCK
    q_blocks = qh.reshape(B, DIFF_HEADS, 2, nb, Q_BLOCK, DIFF_DH).transpose(3, 0, 1, 2, 4, 5)
    k_chunk = jnp.arange(S) // CHUNK
    scale = DIFF_DH ** -0.5

    def one_block(args):
        qb, blk = args
        q_chunk = (blk * Q_BLOCK + jnp.arange(Q_BLOCK)) // CHUNK
        mask = k_chunk[None, :] <= q_chunk[:, None]
        s = jnp.einsum('bhjqd,bhjkd->bhjqk', qb, kh).astype(f32) * scale
        p = jax.nn.softmax(jnp.where(mask, s, NEG_INF), axis=-1)
        a = p[:, :, 0] - lam * p[:, :, 1]
        return jnp.einsum('bhqk,bhkv->bhqv', a.astype(vh.dtype), vh)

    o = lax.map(one_block, (q_blocks, jnp.arange(nb)))
    o = o.transpose(1, 0, 3, 2, 4).reshape(B, S, DIFF_HEADS, DIFF_DV)
    o = rms_norm(o, subln_g) * (1.0 - lam_init)
    return o.reshape(B, S, DIFF_HEADS * DIFF_DV)

def mem_cross_attention(q, mem_n, w_mem_kv, qn_g, kn_g):
    B, S, _ = q.shape
    M = mem_n.shape[1]
    qh = rms_norm(q.reshape(B, S, MEM_HEADS, MEM_DH), qn_g)
    km, vm = jnp.split(mem_n @ w_mem_kv, 2, axis=-1)
    kh = rms_norm(km.reshape(B, M, MEM_HEADS, MEM_DH), kn_g)
    vh = vm.reshape(B, M, MEM_HEADS, MEM_DH)
    s = jnp.einsum('bshd,bmhd->bhsm', qh, kh).astype(jnp.float32) * (MEM_DH ** -0.5)
    p = jax.nn.softmax(s, axis=-1).astype(vh.dtype)
    o = jnp.einsum('bhsm,bmhd->bshd', p, vh)
    return o.reshape(B, S, MEM_HEADS * MEM_DH)

def setup_inputs(seed: int = 0) -> dict:
    key = jax.random.key(seed)
    ks = jax.random.split(key, 32)
    f32 = jnp.float32
    L = DEPTH
    d_in = sum(IN_SIZES)

    def nrm(k, shape, scale):
        return jax.random.normal(k, shape, f32) * scale

    def gain(k, shape):
        return 1.0 + 0.02 * jax.random.normal(k, shape, f32)

    return {
        "x": nrm(ks[0], (BATCH, SEQ, D_MODEL), 1.0),
        "mem": nrm(ks[1], (BATCH, N_MEM, D_MODEL), 1.0),
        "norm_mix_g": gain(ks[2], (L, D_MODEL)),
        "norm_mem_g": gain(ks[3], (L, D_MODEL)),
        "w_in": nrm(ks[4], (L, D_MODEL, d_in), D_MODEL ** -0.5),
        "gla_w_alpha_up": nrm(ks[5], (L, GLA_RANK, GLA_HEADS * GLA_DK), GLA_RANK ** -0.5),
        "gla_b_alpha": nrm(ks[6], (L, GLA_HEADS * GLA_DK), 0.1),
        "gla_norm_g": gain(ks[7], (L, GLA_DV)),
        "diff_q_norm_g": gain(ks[8], (L, DIFF_DH)),
        "diff_k_norm_g": gain(ks[9], (L, DIFF_DH)),
        "diff_lambda_q1": nrm(ks[10], (L, DIFF_DH), 0.1),
        "diff_lambda_k1": nrm(ks[11], (L, DIFF_DH), 0.1),
        "diff_lambda_q2": nrm(ks[12], (L, DIFF_DH), 0.1),
        "diff_lambda_k2": nrm(ks[13], (L, DIFF_DH), 0.1),
        "diff_subln_g": gain(ks[14], (L, DIFF_DV)),
        "mem_q_norm_g": gain(ks[15], (L, MEM_DH)),
        "mem_k_norm_g": gain(ks[16], (L, MEM_DH)),
        "w_mem_kv": nrm(ks[17], (L, D_MODEL, 2 * MEM_HEADS * MEM_DH), D_MODEL ** -0.5),
        "w_branch": nrm(ks[18], (L, N_BRANCH, BRANCH_WIDTH, D_MODEL), BRANCH_WIDTH ** -0.5),
        "w_gate": nrm(ks[19], (L, D_MODEL, N_BRANCH * D_MODEL), D_MODEL ** -0.5),
        "b_gate": nrm(ks[20], (L, N_BRANCH * D_MODEL), 0.02),
        "w_out": nrm(ks[21], (L, D_MODEL, D_MODEL), D_MODEL ** -0.5),
        "norm_ffn_g": gain(ks[22], (L, D_MODEL)),
        "w_ffn_in": nrm(ks[23], (L, D_MODEL, 2 * D_FF), D_MODEL ** -0.5),
        "w_ffn_down": nrm(ks[24], (L, D_FF, D_MODEL), D_FF ** -0.5),
    }

def reference(x, mem, norm_mix_g, norm_mem_g, w_in, gla_w_alpha_up, gla_b_alpha, gla_norm_g,
              diff_q_norm_g, diff_k_norm_g, diff_lambda_q1, diff_lambda_k1, diff_lambda_q2,
              diff_lambda_k2, diff_subln_g, mem_q_norm_g, mem_k_norm_g, w_mem_kv, w_branch,
              w_gate, b_gate, w_out, norm_ffn_g, w_ffn_in, w_ffn_down):
    B, S, D = x.shape
    for l in range(DEPTH):
        lam_init = 0.8 - 0.6 * math.exp(-0.3 * l)
        h = rms_norm(x, norm_mix_g[l])
        z = h @ w_in[l]
        (g_q, g_k, g_v, g_g, g_a, d_q, d_k, d_v, m_q) = split_cols(z, IN_SIZES)
        y_gla = gla_mixer(g_q, g_k, g_v, g_g, g_a, gla_w_alpha_up[l], gla_b_alpha[l], gla_norm_g[l])
        y_diff = diff_mixer(d_q, d_k, d_v, diff_q_norm_g[l], diff_k_norm_g[l],
                            diff_lambda_q1[l], diff_lambda_k1[l], diff_lambda_q2[l],
                            diff_lambda_k2[l], diff_subln_g[l], lam_init)
        y_mem = mem_cross_attention(m_q, rms_norm(mem, norm_mem_g[l]), w_mem_kv[l],
                                    mem_q_norm_g[l], mem_k_norm_g[l])
        y = jnp.stack([y_gla.astype(x.dtype), y_diff.astype(x.dtype), y_mem.astype(x.dtype)],
                      axis=2)
        proj = jnp.einsum('bsiw,iwd->bsid', y, w_branch[l])
        gates = jax.nn.sigmoid((h @ w_gate[l] + b_gate[l]).astype(jnp.float32))
        gates = gates.reshape(B, S, N_BRANCH, D).astype(proj.dtype)
        merged = jnp.sum(gates * proj, axis=2)
        x = x + (merged @ w_out[l]).astype(x.dtype)
        hf = rms_norm(x, norm_ffn_g[l])
        f_gate, f_up = jnp.split(hf @ w_ffn_in[l], 2, axis=-1)
        x = x + ((jax.nn.silu(f_gate) * f_up) @ w_ffn_down[l]).astype(x.dtype)
    return x


_drawn_inputs = setup_inputs


def setup_inputs(seed=0):
    import zlib

    import numpy as np

    out = dict(_drawn_inputs(seed))
    spreads = {}
    factors = {'norm_mem_g': 8.0,
     'gla_b_alpha': 4.127,
     'gla_norm_g': 8.0,
     'diff_q_norm_g': 5.925,
     'diff_k_norm_g': 5.453,
     'diff_subln_g': 6.91,
     'mem_q_norm_g': 8.0,
     'mem_k_norm_g': 8.0,
     'b_gate': 8.0,
     'norm_ffn_g': 4.254}
    for name, (base, spread) in spreads.items():
        noise = np.random.default_rng([zlib.crc32(name.encode()), seed]).standard_normal(out[name].shape)
        drawn = base * np.exp(spread * noise) if base else spread * noise
        out[name] = __import__('jax').numpy.asarray(drawn.astype(out[name].dtype))
    for name, factor in factors.items():
        out[name] = (out[name] * factor).astype(out[name].dtype)
    return out
```

```python
import math
from contextlib import ExitStack

import concourse.bass as bass
from concourse import mybir

FP32 = mybir.dt.float32
FP32R = mybir.dt.float32r
ACT = mybir.ActivationFunctionType
ALU = mybir.AluOpType
AX = mybir.AxisListType

P = 128
HALVES = 2
TILE = 512
KPC = 2
RING = 4
LEAD = 8
CHUNK = 64
HEADS = 4
DH = 256
DK = 128
RANK = 16
EPS = 1e-6
GATE_NORM = 16.0
NEG = -1e30
LAM_INIT = 0.8 - 0.6 * math.exp(0.0)
ACT_HEAD_STEPS = 1
DVE_HEAD_STEPS = 17


class Tally:

    def __init__(self, engine, sem):
        self.engine, self.sem, self.base, self.n, self.loop, self.per = engine, sem, 0, 0, None, 0

    def enter(self, loop, per):
        self.base, self.n, self.loop, self.per = self.base + self.n, 0, loop, per

    def leave(self, times):
        assert self.n == self.per, f"{self.n} steps in a loop's body, {self.per} were stated"
        self.base, self.n, self.loop = self.base + self.per * times, 0, None

    def now(self):
        if self.loop is None:
            return self.base + self.n
        return self.loop * self.per + (self.base + self.n)

    def step(self, instruction):
        instruction.then_inc(self.sem, 1)
        self.n += 1
        self.engine.wait_ge(self.sem, self.now())


def hybrid_layer(nc, x, mem, norm_mix_g, norm_mem_g, w_in, gla_w_alpha_up, gla_b_alpha, gla_norm_g,
                 diff_q_norm_g, diff_k_norm_g, diff_lambda_q1, diff_lambda_k1, diff_lambda_q2,
                 diff_lambda_k2, diff_subln_g, mem_q_norm_g, mem_k_norm_g, w_mem_kv, w_branch,
                 w_gate, b_gate, w_out, norm_ffn_g, w_ffn_in, w_ffn_down, out):
    D = x.shape[2]
    DFF = w_ffn_down.shape[1]
    KT = D // P
    KTB = HEADS * DH // P
    KTF = DFF // P
    COLS = D // TILE
    CPT = KT // KPC
    CPB = KTB // KPC
    CPD = KTF // KPC
    FT = DFF // TILE

    M0, MN, MP = 0, 2, 2 * CPT
    I0, IN, IP = M0 + MN * MP, 4, 2 * CPT
    L0, LN, LP = I0 + IN * IP, 3, 2 * CPT
    G0, GN, GP = L0 + LN * LP, HEADS, 2 * CPT
    B0, BN, BP = G0 + GN * GP, COLS, CPT + 3 * CPB
    O0, ON, OP = B0 + BN * BP, 2, 2 * CPT
    F0, FN, FP = O0 + ON * OP, FT, 2 * CPT
    D0, DN, DP = F0 + FN * FP, 2, 2 * CPD
    END = D0 + DN * DP
    M_T, I_T, L_T, G_T = 0, MN, MN + IN, MN + IN + LN
    B_T = G_T + GN
    O_T = B_T + 2 * BN
    F_T = O_T + ON
    D_T = F_T + FN

    GLA_COLS = 2 * HEADS * DK + 2 * HEADS * DH
    DIFF_COL = GLA_COLS + RANK

    def rows(w):
        return w.rearrange("o (k p) n -> (o p) k n", p=P)

    w_in_v, w_kv_v, w_gate_v, w_out_v = rows(w_in), rows(w_mem_kv), rows(w_gate), rows(w_out)
    w_fin_v, w_down_v = rows(w_ffn_in), rows(w_ffn_down)
    w_br_v = w_branch.rearrange("o i (k p) n -> (o p) i k n", p=P)
    x_v = x.rearrange("o (h p) d -> (o p) h d", p=P)
    mem_v = mem.rearrange("o (h p) d -> (o p) h d", p=P)
    out_v = out.rearrange("o (h p) d -> (o p) h d", p=P)

    ctx = ExitStack()
    with ctx:
        SLOT = KPC * TILE * 4
        CONST = 1152
        BIAS = CONST + 5888
        RAW = BIAS + 2 * TILE * 4
        XT = RAW + 3 * RING * SLOT
        ATT = XT + 2 * KT * HALVES * P * 4
        ZH = ATT + 28672
        ZHEAD = 9 * TILE
        GATE = ZH + HEADS * ZHEAD * 4
        assert GATE + 2 * COLS * HALVES * TILE * 4 <= nc.sbuf_usable_end - 24
        used = [CONST]

        def sb(name, shape, offset, dt=FP32):
            return nc.alloc_sbuf_tensor_at(name, shape, dt, offset=offset)

        def const(name, shape):
            at = used[0]
            n = 4 * math.prod(shape[1:])
            used[0] = at + -(-n // 32) * 32
            assert used[0] <= BIAS
            return sb(name, shape, at)

        ident = const("ident", [P, P])
        upto = const("upto", [P, P])
        after = const("after", [P, P])
        chunk_of = const("chunk_of", [P, 2])
        G_MEM, G_MIX, G_FFN, G_DQ, G_DK, G_MQ, G_MK = 0, KT, 2 * KT, 3 * KT, 3 * KT + 1, 3 * KT + 2, 3 * KT + 4
        NG = 3 * KT + 6
        gains = const("gains", [P, NG])
        gla_gain = const("gla_gain", [P, DH])
        sub_gain = const("sub_gain", [P, DH])
        eps = const("eps", [P, 1])
        lam_dot = const("lam_dot", [P, 2])
        lam_exp = const("lam_exp", [P, 2])
        neg_lam = const("neg_lam", [P, 1])
        ssq_in = const("ssq_in", [P, 2, HALVES])
        rms_in = const("rms_in", [P, 2, HALVES])
        rstd_in = const("rstd_in", [P, 2, HALVES])
        ssq_x1 = const("ssq_x1", [P, HALVES, COLS])
        sum_x1 = const("sum_x1", [P, HALVES])
        rms_x1 = const("rms_x1", [P, HALVES])
        rstd_x1 = const("rstd_x1", [P, HALVES])
        ssq_z = const("ssq_z", [P, HEADS, 6, HALVES * 2])
        ms_z = const("ms_z", [P, HEADS, 12])
        rstd_z = const("rstd_z", [P, HEADS, 12])
        decay = const("decay", [P, HEADS, 4])
        decay_h = const("decay_h", [P, 4])
        rmax = const("rmax", [P, 6])
        nmax = const("nmax", [P, 6])
        psum_exp = const("psum_exp", [P, 6])
        rsum = const("rsum", [P, 6])
        lam_r = const("lam_r", [P, 2])
        ssq_o = const("ssq_o", [P, 4])
        rms_o = const("rms_o", [P, 4])
        rstd_o = const("rstd_o", [P, 4])

        bias = sb("bias", [P, 2, TILE], BIAS)
        raw = sb("raw", [P, RING, KPC, TILE], RAW)
        whi = sb("whi", [P, RING, KPC, TILE], RAW + RING * SLOT, FP32R)
        wlo = sb("wlo", [P, RING, KPC, TILE], RAW + 2 * RING * SLOT, FP32R)
        xt_hi = sb("xt_hi", [P, KT, HALVES * P], XT, FP32R)
        xt_lo = sb("xt_lo", [P, KT, HALVES * P], XT + KT * HALVES * P * 4, FP32R)
        gt_lo = sb("gt_lo", [P, KT, HALVES * P], GATE, FP32R)
        gt_hi = sb("gt_hi", [P, KT, HALVES * P], GATE + KT * HALVES * P * 4, FP32R)
        gates = sb("gates", [P, 2 * COLS, HALVES, TILE], GATE)
        zh = sb("zh", [P, HEADS, ZHEAD], ZH)
        yt = sb("yt", [P, HEADS, ZHEAD], ZH, FP32R)
        MK, MV, DQ, DKO, DV, MQ, GQ, GK, GV, GG = 0, 512, 1024, 1536, 2048, 2560, 3072, 3328, 3584, 4096
        Y_OF = {0: GQ, 1: DQ, 2: MK}
        mem_raw = sb("mem_raw", [P, HALVES, D], ZH)
        x_raw = sb("x_raw", [P, HALVES, D], ZH + HALVES * D * 4)
        junk = sb("junk", [P, 4, D], ZH + 2 * HALVES * D * 4)
        sq = sb("sq", [P, HALVES, TILE], ATT)
        lam_v = sb("lam_v", [P, 4, DK], ATT + 4096)
        up_aug = sb("up_aug", [RANK + 1, HEADS * DK], ATT + 6144)
        low_t = sb("low_t", [RANK + 1, HALVES * P], ATT + 8192)
        wa_raw = sb("wa_raw", [P, KT, RANK], ATT + 9216)
        wa_hi = sb("wa_hi", [P, KT, RANK], ATT + 10240, FP32R)
        wa_lo = sb("wa_lo", [P, KT, RANK], ATT + 11264, FP32R)
        low = sb("low", [P, HALVES, RANK + 1], ATT + 12288)
        gain_rows = sb("gain_rows", [NG, P], ATT + 12800)
        labs = sb("labs", [P, HALVES, HEADS * DK], ATT + 13312)
        lexp = sb("lexp", [P, HALVES, HEADS * DK], ATT + 17408)
        qn = sb("qn", [P, HALVES, DH], ATT)
        kn = sb("kn", [P, HALVES, DH], ATT + 2048)
        q_t = sb("q_t", [P, 2, HALVES * P], ATT + 4096)
        k_t = sb("k_t", [P, 2, HALVES * P], ATT + 6144)
        prob = sb("prob", [P, 768], ATT + 8192)
        prob_t = sb("prob_t", [P, TILE], ATT + 11264)
        qd = sb("qd", [P, HALVES, DK], ATT + 13312)
        kd = sb("kd", [P, HALVES, DK], ATT + 14336)
        sg = sb("sg", [P, HALVES, DH], ATT + 13312)
        k_tail = sb("k_tail", [P, 2, HALVES, DK], ATT + 15360)
        e_tail = sb("e_tail", [P, HALVES, DK], ATT + 17408)
        g_t = sb("g_t", [P, 2, HALVES * P], ATT + 18432)
        att = sb("att", [P, HALVES, P], ATT + 20480)
        state = sb("state", [P, 3, DH], ATT + 21504)
        log_a = sb("log_a", [P, HALVES, HEADS * DK], ATT + 24576)
        res = sb("res", [P, HALVES, TILE], ATT)
        g2 = sb("g2", [P, HALVES, TILE], ATT + 8192)
        x1 = sb("x1", [P, HALVES, D], ATT + 12288)
        xin = sb("xin", [P, 2, HALVES, TILE], ZH)
        sq1 = sb("sq1", [P, HALVES, TILE], ZH + 8192)
        act_hi = sb("act_hi", [P, KTF, HALVES * P], ZH, FP32R)
        act_lo = sb("act_lo", [P, KTF, HALVES * P], ZH + KTF * HALVES * P * 4, FP32R)
        fin = sb("fin", [P, COLS, HALVES, TILE], GATE + 16384)

        acc = [ctx.enter_context(nc.psum_tensor(f"acc{s}", [P, HALVES, TILE], FP32)) for s in range(2)]
        bank = [ctx.enter_context(nc.psum_tensor(f"bank{b}", [P, TILE], FP32)) for b in range(4)]

        def sem(name):
            return ctx.enter_context(nc.semaphore(name))

        chunk_split = sem("chunk_split")
        chunk_used = sem("chunk_used")
        acc_free = [sem(f"acc_free{s}") for s in range(2)]
        bias_used = sem("bias_used")
        raw_landed = [sem(f"raw_landed{s}") for s in range(RING)]
        chunk_hi = sem("chunk_hi")
        bias_landed = [sem(f"bias_landed{s}") for s in range(2)]
        act_step = sem("act_step")
        dve_step = sem("dve_step")
        pool_step = sem("pool_step")
        passed_sp, passed_pool = sem("passed_sp"), sem("passed_pool")
        params_landed = sem("params_landed")
        wa_landed = sem("wa_landed")
        mem_landed = [sem(f"mem_landed{h}") for h in range(HALVES)]
        x_landed = [sem(f"x_landed{h}") for h in range(HALVES)]
        consts_ready = sem("consts_ready")
        gains_turned = sem("gains_turned")
        gains_ready = sem("gains_ready")
        in_turned = sem("in_turned")
        in_hi = sem("in_hi")
        in_lo = sem("in_lo")
        ssq_in_done = sem("ssq_in_done")
        rms_in_done = sem("rms_in_done")
        rstd_in_done = sem("rstd_in_done")
        wa_hi_done = sem("wa_hi_done")
        wa_split = sem("wa_split")
        low_done = sem("low_done")
        low_read = sem("low_read")
        low_turned = sem("low_turned")
        low_t_ready = sem("low_t_ready")
        lgate_done = sem("lgate_done")
        labs_done = sem("labs_done")
        lln_done = sem("lln_done")
        log_a_done = sem("log_a_done")
        decay_sum = sem("decay_sum")
        decay_done = sem("decay_done")
        ms_z_done = sem("ms_z_done")
        rms_z_done = sem("rms_z_done")
        lam_dot_done = sem("lam_dot_done")
        lam_exp_done = sem("lam_exp_done")
        d_turned, m_turned = sem("d_turned"), sem("m_turned")
        d_scores, m_scores = sem("d_scores"), sem("m_scores")
        dp_turned, mp_turned = sem("dp_turned"), sem("mp_turned")
        d_out, m_out = sem("d_out"), sem("m_out")
        dy_turned, my_turned, gy_turned = sem("dy_turned"), sem("my_turned"), sem("gy_turned")
        g_sums, g_turned, g_inc, g_att, g_out = (sem("g_sums"), sem("g_turned"), sem("g_inc"),
                                                 sem("g_att"), sem("g_out"))
        dn_ready, mn_ready = sem("dn_ready"), sem("mn_ready")
        dqt_ready, mqt_ready = sem("dqt_ready"), sem("mqt_ready")
        dkt_ready, mkt_ready = sem("dkt_ready"), sem("mkt_ready")
        dmax_ready, mmax_ready = sem("dmax_ready"), sem("mmax_ready")
        dp_ready, mp_ready = sem("dp_ready"), sem("mp_ready")
        da_ready = sem("da_ready")
        dpt_ready, mpt_ready = sem("dpt_ready"), sem("mpt_ready")
        do_ssq, do_rms = sem("do_ssq"), sem("do_rms")
        dy_ready, my_ready, gy_ready = sem("dy_ready"), sem("my_ready"), sem("gy_ready")
        dy_hi, my_hi, gy_hi = sem("dy_hi"), sem("my_hi"), sem("gy_hi")
        dy_lo, my_lo, gy_lo = sem("dy_lo"), sem("my_lo"), sem("gy_lo")
        ge_ready = sem("ge_ready")
        gd_ready = sem("gd_ready")
        gt_ready = sem("gt_ready")
        gs_ready = sem("gs_ready")
        ga_copied = sem("ga_copied")
        ga_ready = sem("ga_ready")
        gg_exp = sem("gg_exp")
        go_ssq, go_rms = sem("go_ssq"), sem("go_rms")
        sig_g2, sig_g01 = sem("sig_g2"), sem("sig_g01")
        g2_ready = sem("g2_ready")
        g01_free = sem("g01_free")
        res_ready = sem("res_ready")
        res_turned = sem("res_turned")
        res_hi = sem("res_hi")
        res_lo = sem("res_lo")
        xin_landed = [sem(f"xin_landed{s}") for s in range(2)]
        x1_squared = sem("x1_squared")
        x1_sum = sem("x1_sum")
        x1_rms = sem("x1_rms")
        x1_rstd = sem("x1_rstd")
        silu_done = sem("silu_done")
        fin_ready = sem("fin_ready")
        out_stored = sem("out_stored")

        block = ctx.enter_context(nc.Block())

        def nth(base, i, per, u):
            return base + u if i is None else i * per + (base + u)

        @block.sync
        def _(sp):
            for h in range(HALVES):
                sp.dma_start(mem_raw[:, h, :], mem_v[:, h, :]).then_inc(mem_landed[h], 16)
            for h in range(HALVES):
                sp.dma_start(x_raw[:, h, :], x_v[:, h, :]).then_inc(x_landed[h], 16)

            def load(base, i, per, u, source):
                sp.wait_ge(chunk_split, nth(base, i, per, u) + 1)
                sp.sem_inc(passed_sp, 1)
                sp.dma_start(raw[:, u % RING, :, :], source).then_inc(raw_landed[u % RING], 16)

            def load_tile(base, i, per, u0, view, col, chunks):
                for c in range(chunks):
                    load(base, i, per, u0 + c, view[:, KPC * c:KPC * (c + 1), bass.ds(col, TILE)])

            with sp.Fori(0, MN) as i:
                for t in range(2):
                    load_tile(M0, i, MP, t * CPT, w_kv_v, i * (2 * TILE) + t * TILE, CPT)
            with sp.Fori(0, IN) as i:
                for t in range(2):
                    load_tile(I0, i, IP, t * CPT, w_in_v, i * (2 * TILE) + (DIFF_COL + t * TILE), CPT)
            with sp.Fori(0, LN) as i:
                for t in range(2):
                    load_tile(L0, i, LP, t * CPT, w_in_v, i * (2 * TILE) + t * TILE, CPT)
            with sp.Fori(0, GN) as i:
                for t in range(2):
                    sp.wait_ge(bias_used, i * 2 + (t + 1))
                    sp.sem_inc(passed_sp, 1)
                    col = i * (2 * TILE) + t * TILE
                    sp.dma_start(bias[:, t, :], b_gate[:, bass.ds(col, TILE)].partition_broadcast(P)
                                 ).then_inc(bias_landed[t], 16)
                    load_tile(G0, i, GP, t * CPT, w_gate_v, col, CPT)
            with sp.Fori(0, BN) as c:
                load_tile(B0, c, BP, 0, w_gate_v, c * TILE + 2 * D, CPT)
                sp.wait_ge(bias_used, c + (2 * GN + 2))
                sp.sem_inc(passed_sp, 1)
                sp.dma_start(bias[:, 0, :], b_gate[:, bass.ds(c * TILE + 2 * D, TILE)].partition_broadcast(P)
                             ).then_inc(bias_landed[0], 16)
                for b in range(3):
                    load_tile(B0, c, BP, CPT + b * CPB, w_br_v[:, b, :, :], c * TILE, CPB)
            with sp.Fori(0, ON) as i:
                for t in range(2):
                    load_tile(O0, i, OP, t * CPT, w_out_v, i * (2 * TILE) + t * TILE, CPT)
                    sp.wait_ge(chunk_used, nth(O0, i, OP, t * CPT) + RING)
                    sp.sem_inc(passed_sp, 1)
                    sp.wait_ge(res_ready, i * 2 + (BN + t - 1))
                    sp.sem_inc(passed_sp, 1)
                    sp.dma_start(xin[:, t, :, :], x_v[:, :, bass.ds(i * (2 * TILE) + t * TILE, TILE)]
                                 ).then_inc(xin_landed[t], 16)
            with sp.Fori(0, FN) as i:
                for t in range(2):
                    load_tile(F0, i, FP, t * CPT, w_fin_v, i * TILE + t * DFF, CPT)
            with sp.Fori(0, DN) as i:
                for t in range(2):
                    load_tile(D0, i, DP, t * CPD, w_down_v, i * (2 * TILE) + t * TILE, CPD)

        @block.tensor
        def _(pe):
            pe.sem_inc(chunk_used, RING)

            def multiply(base, i, per, u, psum, kt, st_hi, st_lo, first, last):
                slot = u % RING
                pe.wait_ge(chunk_split, nth(base, i, per, u) + (RING + 1))
                for j in range(KPC):
                    for h in range(HALVES):
                        a_hi, a_lo = st_hi(kt + j, h), st_lo(kt + j, h)
                        nc.tensor.matmul(psum[:, h, :], a_hi, whi[:, slot, j, :],
                                         start=first and j == 0, stop=False)
                        nc.tensor.matmul(psum[:, h, :], a_hi, wlo[:, slot, j, :], start=False, stop=False)
                        mm = nc.tensor.matmul(psum[:, h, :], a_lo, whi[:, slot, j, :],
                                              start=False, stop=last and j == KPC - 1)
                mm.then_inc(chunk_used, 1)

            def tokens(tensor):
                return lambda kt, h: tensor[:, kt, h * P:(h + 1) * P]

            X = tokens(xt_hi), tokens(xt_lo)
            GT = tokens(gt_hi), tokens(gt_lo)
            AT = tokens(act_hi), tokens(act_lo)

            def Y(branch):
                def hi(kt, h):
                    o = Y_OF[branch] + (kt % 2) * HALVES * P + h * P
                    return yt[:, kt // 2, o:o + P]

                def lo(kt, h):
                    o = Y_OF[branch] + (2 + kt % 2) * HALVES * P + h * P
                    return yt[:, kt // 2, o:o + P]
                return hi, lo

            def tile(base, i, per, u0, chunks, slot, tiles, st, hook=None):
                pe.wait_ge(acc_free[slot], tiles)
                for c in range(chunks):
                    multiply(base, i, per, u0 + c, acc[slot], KPC * c, *st, c == 0, c == chunks - 1)
                    if hook is not None:
                        hook(c)

            def turn_res(k):
                pe.wait_ge(res_ready, k + 1)
                for b in range(2):
                    for j in range(2):
                        for h in range(HALVES):
                            t = nc.tensor.transpose(bank[b][:, j * 2 * P + h * P:j * 2 * P + (h + 1) * P],
                                                    res[:, h, (2 * b + j) * P:(2 * b + j + 1) * P], ident[:, :])
                t.then_inc(res_turned, 1)

            pe.wait_ge(consts_ready, 1)
            pe.wait_ge(params_landed, 16 * 17)
            nc.tensor.transpose(bank[3][:, 0:NG], gain_rows[:, :], ident[0:NG, 0:NG]).then_inc(gains_turned, 1)
            for g in range(2 * KT // 2):
                source, landed = (mem_raw, mem_landed) if g < KT // 2 else (x_raw, x_landed)
                if g % (KT // 2) == 0:
                    for h in range(HALVES):
                        pe.wait_ge(landed[h], 16)
                if g == 3:
                    pe.wait_ge(gains_ready, 1)
                if g >= 4:
                    pe.wait_ge(in_lo, g - 3)
                for j in range(2):
                    kt = 2 * (g % (KT // 2)) + j
                    for h in range(HALVES):
                        t = nc.tensor.transpose(bank[g % 4][:, j * 2 * P + h * P:j * 2 * P + (h + 1) * P],
                                                source[:, h, kt * P:(kt + 1) * P], ident[:, :])
                t.then_inc(in_turned, 1)
            pe.wait_ge(in_lo, 2 * KT // 2)
            pe.wait_ge(wa_split, 1)
            for h in range(HALVES):
                for kt in range(KT):
                    o = bank[0][:, h * RANK:(h + 1) * RANK]
                    nc.tensor.matmul(o, X[0](kt, h), wa_hi[:, kt, :], start=kt == 0, stop=False)
                    nc.tensor.matmul(o, X[0](kt, h), wa_lo[:, kt, :], start=False, stop=False)
                    m = nc.tensor.matmul(o, X[1](kt, h), wa_hi[:, kt, :], start=False, stop=kt == KT - 1)
            m.then_inc(low_done, 1)

            with pe.Fori(0, MN) as i:
                for t in range(2):
                    tile(M0, i, MP, t * CPT, CPT, t, i + (M_T + 1), GT)
            pe.wait_ge(low_read, 1)
            for h in range(HALVES):
                t = nc.tensor.transpose(bank[1][0:RANK + 1, h * P:(h + 1) * P], low[:, h, :], ident[:, :])
            t.then_inc(low_turned, 1)
            with pe.Fori(0, IN) as i:
                for t in range(2):
                    tile(I0, i, IP, t * CPT, CPT, t, i + (I_T + 1), X)
            pe.wait_ge(low_t_ready, 1)
            for h in range(HALVES):
                m = nc.tensor.matmul(bank[2 + h][:, :], low_t[:, h * P:(h + 1) * P], up_aug[:, :],
                                     start=True, stop=True)
            m.then_inc(lgate_done, 1)
            with pe.Fori(0, LN) as i:
                for t in range(2):
                    tile(L0, i, LP, t * CPT, CPT, t, i + (L_T + 1), X)
            pe.wait_ge(log_a_done, 1)
            for n in range(HEADS):
                for h in range(HALVES):
                    m = nc.tensor.matmul(bank[0][:, n * 4 + 2 * h:n * 4 + 2 * h + 2],
                                         log_a[:, h, n * DK:(n + 1) * DK], chunk_of[:, :], start=True, stop=True)
            m.then_inc(decay_sum, 1)

            with pe.Fori(0, GN) as n:
                def turn_qk(ready, b, done):
                    pe.wait_ge(ready, n + 1)
                    for s, (src, dst) in enumerate(((qn, bank[b[0]]), (kn, bank[b[1]]))):
                        for j in range(2):
                            for h in range(HALVES):
                                t = nc.tensor.transpose(dst[:, j * 2 * P + h * P:j * 2 * P + (h + 1) * P],
                                                        src[:, h, j * P:(j + 1) * P], ident[:, :])
                    t.then_inc(done, 1)

                def turn_y(y, ready, b, done):
                    pe.wait_ge(ready, n + 1)
                    for j in range(2):
                        for h in range(HALVES):
                            t = nc.tensor.transpose(bank[b][:, j * 2 * P + h * P:j * 2 * P + (h + 1) * P],
                                                    y[:, h, j * P:(j + 1) * P], ident[:, :])
                    t.then_inc(done, 1)

                def gla_sums():
                    for h in range(HALVES):
                        nc.tensor.matmul(bank[3][:, h * DK:(h + 1) * DK], upto[:, :],
                                         log_a[:, h, bass.ds(n * DK, DK)], start=True, stop=True)
                    for h in range(HALVES):
                        m = nc.tensor.matmul(bank[3][:, (2 + h) * DK:(3 + h) * DK], after[:, :],
                                             log_a[:, h, bass.ds(n * DK, DK)], start=True, stop=True)
                    m.then_inc(g_sums, 1)

                def gla_turn():
                    pe.wait_ge(gd_ready, n + 1)
                    for s, src in enumerate((qd, kd)):
                        for h in range(HALVES):
                            t = nc.tensor.transpose(bank[2][:, (2 * s + h) * P:(2 * s + h + 1) * P],
                                                    src[:, h, :], ident[:, :])
                    t.then_inc(g_turned, 1)
                    for c in range(2):
                        m = nc.tensor.matmul(bank[3][:, c * DH:(c + 1) * DH], k_tail[:, c, 0, :],
                                             zh[:, n, GV:GV + DH], start=True, stop=True)
                    m.then_inc(g_inc, 1)

                def gla_scores():
                    pe.wait_ge(gt_ready, n + 1)
                    for h in range(HALVES):
                        nc.tensor.matmul(bank[2][:, h * P:(h + 1) * P], g_t[:, 1, h * P:(h + 1) * P],
                                         g_t[:, 0, h * P:(h + 1) * P], start=True, stop=True)
                    m = nc.tensor.matmul(bank[2][:, DH:2 * DH], k_tail[:, 0, 1, :],
                                         zh[:, n, GV + DH:GV + 2 * DH], start=True, stop=True)
                    m.then_inc(g_att, 1)

                def gla_output():
                    pe.wait_ge(ga_ready, n + 1)
                    pe.wait_ge(gs_ready, n + 1)
                    for h in range(HALVES):
                        o = bank[2][:, h * DH:(h + 1) * DH]
                        nc.tensor.matmul(o, att[:, h, :], zh[:, n, GV + h * DH:GV + (h + 1) * DH],
                                         start=True, stop=True, skip_group_check=True)
                        for c in range(2):
                            if 2 * h + c == 0:
                                continue
                            r = slice(c * CHUNK, (c + 1) * CHUNK)
                            m = nc.tensor.matmul(bank[2][r, h * DH:(h + 1) * DH],
                                                 g_t[:, 0, h * P + c * CHUNK:h * P + (c + 1) * CHUNK],
                                                 state[:, 2 * h + c - 1, :], start=False, stop=True,
                                                 skip_group_check=True)
                    m.then_inc(g_out, 1)

                def diff_scores():
                    pe.wait_ge(dqt_ready, n + 1)
                    pe.wait_ge(dkt_ready, n + 1)
                    for j in range(2):
                        nc.tensor.matmul(bank[0][:, j * 2 * P:(j + 1) * 2 * P], q_t[:, j, P:2 * P],
                                         k_t[:, j, :], start=True, stop=True)
                    for j in range(2):
                        m = nc.tensor.matmul(bank[1][:, j * P:(j + 1) * P], q_t[:, j, 0:P],
                                             k_t[:, j, 0:P], start=True, stop=True)
                    m.then_inc(d_scores, 1)

                def diff_turn():
                    pe.wait_ge(da_ready, n + 1)
                    for s, at in enumerate((512, 0, P)):
                        t = nc.tensor.transpose(bank[0][:, s * P:(s + 1) * P], prob[:, at:at + P], ident[:, :])
                    t.then_inc(dp_turned, 1)

                def diff_output():
                    pe.wait_ge(dpt_ready, n + 1)
                    nc.tensor.matmul(bank[0][:, 0:DH], prob_t[:, 0:P], zh[:, n, DV:DV + DH],
                                     start=True, stop=True)
                    nc.tensor.matmul(bank[0][:, DH:2 * DH], prob_t[:, P:2 * P], zh[:, n, DV:DV + DH],
                                     start=True, stop=False)
                    nc.tensor.matmul(bank[0][:, DH:2 * DH], prob_t[:, 2 * P:3 * P],
                                     zh[:, n, DV + DH:DV + 2 * DH], start=False, stop=True).then_inc(d_out, 1)

                def mem_scores():
                    pe.wait_ge(mqt_ready, n + 1)
                    pe.wait_ge(mkt_ready, n + 1)
                    for h in range(HALVES):
                        for j in range(2):
                            m = nc.tensor.matmul(bank[1][:, h * 2 * P:(h + 1) * 2 * P],
                                                 q_t[:, j, h * P:(h + 1) * P], k_t[:, j, :],
                                                 start=j == 0, stop=j == 1)
                    m.then_inc(m_scores, 1)

                def mem_turn():
                    pe.wait_ge(mp_ready, n + 1)
                    for h in range(HALVES):
                        for j in range(2):
                            t = nc.tensor.transpose(bank[1][:, (2 * h + j) * P:(2 * h + j + 1) * P],
                                                    prob[:, (2 * h + j) * P:(2 * h + j + 1) * P], ident[:, :])
                    t.then_inc(mp_turned, 1)

                def mem_output():
                    pe.wait_ge(mpt_ready, n + 1)
                    for h in range(HALVES):
                        for j in range(2):
                            m = nc.tensor.matmul(bank[1][:, h * DH:(h + 1) * DH],
                                                 prob_t[:, (2 * h + j) * P:(2 * h + j + 1) * P],
                                                 zh[:, n, MV + j * DH:MV + (j + 1) * DH],
                                                 start=j == 0, stop=j == 1)
                    m.then_inc(m_out, 1)

                def heads(c):
                    if c == 0:
                        gla_sums()
                    if c == 5:
                        turn_qk(dn_ready, (0, 1), d_turned)
                    if c == 6:
                        gla_turn()
                    if c == 7:
                        diff_scores()
                    if c == 8:
                        gla_scores()
                    if c == 9:
                        diff_turn()
                        turn_qk(mn_ready, (1, 3), m_turned)
                    if c == 10:
                        gla_output()
                    if c == 11:
                        diff_output()
                        mem_scores()
                    if c == 13:
                        mem_turn()
                        turn_y(sg, gy_ready, 2, gy_turned)
                        turn_y(kn, dy_ready, 0, dy_turned)
                    if c == 14:
                        mem_output()
                    if c == 15:
                        turn_y(qn, my_ready, 1, my_turned)

                for t in range(2):
                    tile(G0, n, GP, t * CPT, CPT, t, n + (G_T + 1), X,
                         lambda c, t=t: heads(t * CPT + c))

            def merge_column(c, first):
                def hook(k):
                    if k == 3 and not first:
                        turn_res(c - 1)
                tile(B0, c, BP, 0, CPT, 0, c * 2 + (B_T + 1), X, hook)
                if first:
                    pe.wait_ge(dy_lo, HEADS)
                    pe.wait_ge(my_lo, HEADS)
                    pe.wait_ge(gy_lo, HEADS)
                tile(B0, c, BP, CPT, CPB, 1, c * 2 + (B_T + 1), Y(0))
                tile(B0, c, BP, CPT + CPB, CPB, 0, c * 2 + (B_T + 2), Y(1))
                tile(B0, c, BP, CPT + 2 * CPB, CPB, 1, c * 2 + (B_T + 2), Y(2))

            merge_column(0, True)
            with pe.Fori(1, BN) as c:
                merge_column(c, False)

            with pe.Fori(0, ON) as i:
                for t in range(2):
                    def hook(c, t=t):
                        if c == 3:
                            turn_res(i * 2 + (BN - 1 + t))
                        if c == 5:
                            pe.wait_ge(res_lo, 2 * BN)
                    tile(O0, i, OP, t * CPT, CPT, t, i + (O_T + 1), GT, hook)
            with pe.Fori(0, FN) as i:
                def hook(c):
                    if c == 3:
                        turn_res(i + (BN + COLS - 1))
                    if c == 5:
                        pe.wait_ge(res_lo, 2 * (BN + COLS))
                tile(F0, i, FP, 0, CPT, 0, i + (F_T + 1), X, hook)
                tile(F0, i, FP, CPT, CPT, 1, i + (F_T + 1), X)
            def last_turn(c):
                if c == 3:
                    turn_res(BN + COLS + FT - 1)
                if c == CPD - 3:
                    pe.wait_ge(res_lo, 2 * (BN + COLS + FT))
            for t in range(COLS):
                tile(D0, None, 0, t * CPD, CPD, t % 2, D_T + 1 + t // 2, AT, last_turn if t == 0 else None)

        @block.scalar
        def _(act):
            own = Tally(act, act_step)
            for n, (v, g0) in enumerate(((norm_mem_g, G_MEM), (norm_mix_g, G_MIX), (norm_ffn_g, G_FFN))):
                act.dma_start(gain_rows[g0:g0 + KT, :], v.rearrange("o (k p) -> (o k) p", p=P)
                              ).then_inc(params_landed, 16)
            for v, g0, m in ((diff_q_norm_g, G_DQ, 1), (diff_k_norm_g, G_DK, 1),
                             (mem_q_norm_g, G_MQ, 2), (mem_k_norm_g, G_MK, 2)):
                act.dma_start(gain_rows[g0:g0 + m, :], v.rearrange("o (k p) -> (o k) p", p=P)
                              ).then_inc(params_landed, 16)
            for k, v in enumerate((diff_lambda_q1, diff_lambda_k1, diff_lambda_q2, diff_lambda_k2)):
                act.dma_start(lam_v[:, k, :], v.partition_broadcast(P)).then_inc(params_landed, 16)
            act.dma_start(gla_gain[:, :], gla_norm_g.partition_broadcast(P)).then_inc(params_landed, 16)
            act.dma_start(sub_gain[:, :], diff_subln_g.partition_broadcast(P)).then_inc(params_landed, 16)
            act.dma_start(up_aug[0:RANK, :], gla_w_alpha_up[0, :, :]).then_inc(params_landed, 16)
            act.dma_start(up_aug[RANK:RANK + 1, :], gla_b_alpha).then_inc(params_landed, 16)
            act.dma_start(wa_raw[:, 0:KT // 2, :], w_in_v[:, 0:KT // 2, GLA_COLS:GLA_COLS + RANK]
                          ).then_inc(params_landed, 16)
            act.dma_start(wa_raw[:, KT // 2:KT, :], w_in_v[:, KT // 2:KT, GLA_COLS:GLA_COLS + RANK]
                          ).then_inc(params_landed, 16)

            def split(base, i, per, u):
                s = u % RING
                act.wait_ge(raw_landed[s], 16 * nth(base // RING, i, per // RING, u // RING + 1))
                act.wait_ge(chunk_used, nth(base, i, per, u) + 1)
                nc.scalar.activation(whi[:, s, :, :], raw[:, s, :, :], ACT.Copy).then_inc(chunk_hi, 1)

            for g in range(2 * KT // 2):
                if g == 0:
                    act.wait_ge(gains_ready, 1)
                act.wait_ge(in_turned, g + 1)
                hi, g0 = (gt_hi, G_MEM) if g < KT // 2 else (xt_hi, G_MIX)
                for j in range(2):
                    kt = 2 * (g % (KT // 2)) + j
                    a = nc.scalar.activation(hi[:, kt, :], bank[g % 4][:, j * 2 * P:(j + 1) * 2 * P], ACT.Copy,
                                             scale=gains[:, g0 + kt:g0 + kt + 1])
                a.then_inc(in_hi, 1)
            act.wait_ge(params_landed, 16 * 17)
            nc.scalar.activation(wa_hi[:, :, :], wa_raw[:, :, :], ACT.Copy).then_inc(wa_hi_done, 1)
            for u in range(4):
                split(M0, None, 0, u)
            for k, source in enumerate((mem_raw, x_raw)):
                for h in range(HALVES):
                    a = nc.scalar.activation(junk[:, 2 * k + h, :], source[:, h, :], ACT.Square,
                                             accum_out=ssq_in[:, k, h:h + 1])
            own.step(a)
            act.wait_ge(consts_ready, 1)
            nc.scalar.activation(rms_in[:, :, :], ssq_in[:, :, :], ACT.Sqrt, scale=1.0 / D,
                                 bias=eps[:, :]).then_inc(rms_in_done, 1)
            act.wait_ge(rstd_in_done, 1)
            for u in range(4, LEAD):
                split(M0, None, 0, u)
            act.wait_ge(low_done, 1)
            for h in range(HALVES):
                a = nc.scalar.activation(low[:, h, 0:RANK], bank[0][:, h * RANK:(h + 1) * RANK], ACT.Copy,
                                         scale=rstd_in[:, 1, h:h + 1])
            a.then_inc(low_read, 1)

            def split_some(base, i, per, u, count):
                for k in range(count):
                    split(base, i, per, u + k)

            def store_z(base, i, per, t, src, dest):
                act.wait_ge(chunk_used, nth(base, i, per, (t + 1) * CPT) + RING)
                for h in range(HALVES):
                    a = nc.scalar.activation(dest(h), acc[t][:, h, :].rearrange("p (n c) -> p n c", c=dest(h).shape[2]),
                                             ACT.Copy, scale=rstd_in[:, src, h:h + 1])
                a.then_inc(acc_free[t], 1)

            def two_heads(i, item, t):
                return lambda h: zh[:, 2 * t:2 * t + 2, bass.ds(i * TILE + (item + h * DH), DH)]


            with act.Fori(0, MN) as i:
                for t in range(2):
                    split_some(M0, i, MP, LEAD + t * CPT, 4)
                    store_z(M0, i, MP, t, 0, two_heads(i, MK, t))
                    split_some(M0, i, MP, LEAD + t * CPT + 4, CPT - 4)
            act.wait_ge(low_turned, 1)
            nc.scalar.activation(low_t[:, :], bank[1][0:RANK + 1, 0:HALVES * P], ACT.Copy).then_inc(low_t_ready, 1)
            with act.Fori(0, IN) as i:
                for t in range(2):
                    split_some(I0, i, IP, LEAD + t * CPT, 4)
                    store_z(I0, i, IP, t, 1, two_heads(i, DQ, t))
                    split_some(I0, i, IP, LEAD + t * CPT + 4, CPT - 4)
            act.wait_ge(lgate_done, 1)
            for h in range(HALVES):
                a = nc.scalar.activation(labs[:, h, :], bank[2 + h][:, :], ACT.Abs)
            own.step(a)
            own.step(nc.scalar.activation(lexp[:, :, :], labs[:, :, :], ACT.Exp, scale=-1.0))
            nc.scalar.activation(labs[:, :, :], lexp[:, :, :], ACT.Ln, bias=1.0).then_inc(lln_done, 1)
            act.wait_ge(lam_dot_done, 1)
            nc.scalar.activation(lam_exp[:, :], lam_dot[:, :], ACT.Exp).then_inc(lam_exp_done, 1)
            act.wait_ge(ms_z_done, 1)
            nc.scalar.activation(rstd_z[:, :, :], ms_z[:, :, :], ACT.Sqrt, bias=eps[:, :]).then_inc(rms_z_done, 1)
            for t, item in enumerate((GQ, GK)):
                split_some(L0, None, 0, LEAD + t * CPT, 4)
                store_z(L0, None, 0, t, 1, lambda h: zh[:, :, item + h * DK:item + (h + 1) * DK])
                split_some(L0, None, 0, LEAD + t * CPT + 4, CPT - 4)
            with act.Fori(1, LN) as i:
                for t in range(2):
                    split_some(L0, i, LP, LEAD + t * CPT, 4)
                    store_z(L0, i, LP, t, 1, two_heads(i, GV - TILE, t))
                    split_some(L0, i, LP, LEAD + t * CPT + 4, CPT - 4)
            act.wait_ge(decay_sum, 1)
            nc.scalar.activation(decay[:, :, :], bank[0][:, 0:HEADS * 4].rearrange("p (n c) -> p n c", c=4),
                                 ACT.Exp, scale=1.0 / GATE_NORM).then_inc(decay_done, 1)

            with act.Fori(0, GN) as n:
                own.enter(n, ACT_HEAD_STEPS)

                def gla_decays():
                    act.wait_ge(g_sums, n + 1)
                    nc.scalar.activation(qd[:, :, :], bank[3][:, 0:2 * DK], ACT.Exp, scale=1.0 / GATE_NORM)
                    nc.scalar.activation(kd[:, :, :], bank[3][:, 0:2 * DK], ACT.Exp, scale=-1.0 / GATE_NORM)
                    nc.scalar.activation(e_tail[:, :, :], bank[3][:, 2 * DK:4 * DK], ACT.Exp,
                                         scale=1.0 / GATE_NORM).then_inc(ge_ready, 1)

                def diff_q():
                    act.wait_ge(d_turned, n + 1)
                    nc.scalar.activation(q_t[:, :, :], bank[0][:, :], ACT.Copy,
                                         scale=gains[:, G_DQ:G_DQ + 1]).then_inc(dqt_ready, 1)

                def gla_qk():
                    act.wait_ge(g_turned, n + 1)
                    nc.scalar.activation(g_t[:, :, :], bank[2][:, :], ACT.Copy).then_inc(gt_ready, 1)

                def gla_silu():
                    nc.scalar.activation(sg[:, :, :], zh[:, n, GG:GG + 2 * DH], ACT.Exp, scale=-1.0
                                         ).then_inc(gg_exp, 1)

                def diff_exp():
                    act.wait_ge(dmax_ready, n + 1)
                    for k, (b, at, src, w) in enumerate(((0, 0, 0, 2 * P), (0, 2 * P, 2 * P, 2 * P),
                                                         (1, 4 * P, 0, P), (1, 5 * P, P, P))):
                        a = nc.scalar.activation(prob[:, at:at + w], bank[b][:, src:src + w], ACT.Exp,
                                                 scale=DK ** -0.5, bias=nmax[:, k:k + 1],
                                                 accum_out=psum_exp[:, k:k + 1])
                    a.then_inc(dp_ready, 1)

                def gla_copy():
                    act.wait_ge(g_att, n + 1)
                    scores = bank[2][:, 0:2 * P].rearrange("p (h t) -> p h t", t=P)
                    for c in range(2):
                        r = slice(c * CHUNK, (c + 1) * CHUNK)
                        a = nc.scalar.activation(att[r, :, r], scores[r, :, r], ACT.Copy)
                    a.then_inc(ga_copied, 1)

                def diff_weights():
                    act.wait_ge(dp_turned, n + 1)
                    nc.scalar.activation(prob_t[:, 0:3 * P], bank[0][:, 0:3 * P], ACT.Copy).then_inc(dpt_ready, 1)

                def mem_q():
                    act.wait_ge(m_turned, n + 1)
                    for j in range(2):
                        a = nc.scalar.activation(q_t[:, j, :], bank[1][:, j * 2 * P:(j + 1) * 2 * P], ACT.Copy,
                                                 scale=gains[:, G_MQ + j:G_MQ + j + 1])
                    a.then_inc(mqt_ready, 1)

                def mem_exp():
                    act.wait_ge(mmax_ready, n + 1)
                    for h in range(HALVES):
                        r = slice(h * 2 * P, (h + 1) * 2 * P)
                        a = nc.scalar.activation(prob[:, r], bank[1][:, r], ACT.Exp, scale=DH ** -0.5,
                                                 bias=nmax[:, 4 + h:5 + h], accum_out=psum_exp[:, 4 + h:5 + h])
                    a.then_inc(mp_ready, 1)

                def output_rms():
                    act.wait_ge(g_out, n + 1)
                    for h in range(HALVES):
                        nc.scalar.activation(g_t[:, h, :], bank[2][:, h * DH:(h + 1) * DH], ACT.Square,
                                             accum_out=ssq_o[:, 2 + h:3 + h])
                    act.wait_ge(d_out, n + 1)
                    for h in range(HALVES):
                        a = nc.scalar.activation(kn[:, h, :], bank[0][:, h * DH:(h + 1) * DH], ACT.Square,
                                                 accum_out=ssq_o[:, h:h + 1])
                    own.step(a)
                    nc.scalar.activation(rms_o[:, :], ssq_o[:, :], ACT.Sqrt, scale=1.0 / DH, bias=eps[:, :]
                                         ).then_inc(go_rms, 1)

                def mem_weights():
                    act.wait_ge(mp_turned, n + 1)
                    nc.scalar.activation(prob_t[:, :], bank[1][:, :], ACT.Copy).then_inc(mpt_ready, 1)

                def y_hi(turned, b, place, done):
                    act.wait_ge(turned, n + 1)
                    nc.scalar.activation(yt[:, n, place:place + 2 * DH], bank[b][:, :], ACT.Copy).then_inc(done, 1)

                for s in range(GP):
                    split(G0, n, GP, LEAD + s)
                    if s == 0:
                        gla_decays()
                    if s == 1:
                        diff_q()
                    if s == 2:
                        gla_qk()
                        gla_silu()
                    if s == 3:
                        diff_exp()
                    if s == 4:
                        gla_copy()
                    if s == 5:
                        diff_weights()
                        mem_q()
                    if s == 7:
                        output_rms()
                        mem_exp()
                    if s == 9:
                        mem_weights()
                        y_hi(gy_turned, 2, GQ, gy_hi)
                        y_hi(dy_turned, 0, DQ, dy_hi)
                    if s == 13:
                        y_hi(my_turned, 1, MK, my_hi)
                own.leave(GN)

            def turned_hi(k, write):
                act.wait_ge(res_turned, k + 1)
                for b in range(2):
                    write(b).then_inc(res_hi, 1)

            with act.Fori(0, BN) as c:
                split_some(B0, c, BP, LEAD, 4)
                act.wait_ge(bias_used, 2 * GN + 2)
                for b in range(2):
                    a = nc.scalar.activation(gates[:, c + b * COLS, :, :], gates[:, c + b * COLS, :, :], ACT.Sigmoid)
                a.then_inc(sig_g01, 1)
                split_some(B0, c, BP, LEAD + 4, 4)
                act.wait_ge(g2_ready, c + 1)
                nc.scalar.activation(g2[:, :, :], g2[:, :, :], ACT.Sigmoid).then_inc(sig_g2, 1)
                split_some(B0, c, BP, LEAD + 8, BP - 8)
                turned_hi(c, lambda b: nc.scalar.activation(
                    gt_hi[:, bass.ds(c * 4 + 2 * b, 2), :], bank[b][:, :].rearrange("p (k t) -> p k t", k=2), ACT.Copy))

            for t in range(COLS):
                split_some(O0, None, 0, LEAD + t * CPT, 4)
                k = BN + t
                act.wait_ge(res_ready, k + 1)
                nc.scalar.activation(x1[:, :, t * TILE:(t + 1) * TILE], res[:, :, :], ACT.Copy)
                for h in range(HALVES):
                    a = nc.scalar.activation(sq1[:, h, :], res[:, h, :], ACT.Square,
                                             accum_out=ssq_x1[:, h, t:t + 1])
                a.then_inc(x1_squared, 1)
                if t == COLS - 1:
                    act.wait_ge(x1_sum, 1)
                    nc.scalar.activation(rms_x1[:, :], sum_x1[:, :], ACT.Sqrt, scale=1.0 / D, bias=eps[:, :]
                                         ).then_inc(x1_rms, 1)
                split_some(O0, None, 0, LEAD + t * CPT + 4, 4)
                act.wait_ge(res_turned, k + 1)
                for b in range(2):
                    for j in range(2):
                        kt = 4 * t + 2 * b + j
                        a = nc.scalar.activation(xt_hi[:, kt, :], bank[b][:, j * 2 * P:(j + 1) * 2 * P], ACT.Copy,
                                                 scale=gains[:, G_FFN + kt:G_FFN + kt + 1])
                    a.then_inc(res_hi, 1)
                if t < COLS - 1:
                    act.wait_ge(x1_squared, t + 1)

            act.wait_ge(x1_rstd, 1)
            with act.Fori(0, FN) as i:
                split_some(F0, i, FP, LEAD, 4)
                act.wait_ge(chunk_used, nth(F0, i, FP, CPT) + RING)
                act.wait_ge(res_ready, i + (BN + COLS))
                for h in range(HALVES):
                    a = nc.scalar.activation(g2[:, h, :], acc[0][:, h, :], ACT.Silu, scale=rstd_x1[:, h:h + 1])
                a.then_inc(acc_free[0], 1)
                split_some(F0, i, FP, LEAD + 4, 12)
                turned_hi(i + (BN + COLS), lambda b: nc.scalar.activation(
                    act_hi[:, bass.ds(i * 4 + 2 * b, 2), :], bank[b][:, :].rearrange("p (k t) -> p k t", k=2), ACT.Copy))

            def store(t):
                act.wait_ge(fin_ready, t + 1)
                act.dma_start(out_v[:, :, t * TILE:(t + 1) * TILE], fin[:, t, :, :]).then_inc(out_stored, 16)

            for t in range(COLS):
                u = LEAD + t * CPD
                last = t == COLS - 1
                split_some(D0, None, 0, u, CPD - LEAD if last else CPD - 4)
                if not last:
                    split_some(D0, None, 0, u + CPD - 4, 4)
                store(t)
            act.wait_ge(out_stored, 16 * COLS)

        @block.vector
        def _(dve):
            own = Tally(dve, dve_step)
            V = nc.vector
            dve.sem_inc(chunk_split, RING)
            dve.sem_inc(acc_free[0], 1)
            dve.sem_inc(acc_free[1], 1)
            dve.sem_inc(bias_used, 2)

            def f32(ap):
                return ap.bitcast(FP32)

            def split(base, i, per, u):
                s = u % RING
                dve.wait_ge(chunk_hi, nth(base, i, per, u) + 1)
                V.tensor_tensor(wlo[:, s, :, :], raw[:, s, :, :], f32(whi[:, s, :, :]), ALU.subtract
                                ).then_inc(chunk_split, 1)

            def split_some(base, i, per, u, count):
                for k in range(count):
                    split(base, i, per, u + k)

            V.memset(low[:, :, RANK:RANK + 1], 1.0)
            dve.wait_ge(gains_turned, 1)
            V.tensor_copy(gains[:, :], bank[3][:, 0:NG]).then_inc(gains_ready, 1)
            for g in range(2 * KT // 2):
                if g == 0:
                    own.step(V.memset(lam_dot[:, :], 0.0))
                dve.wait_ge(in_hi, g + 1)
                hi, lo, g0 = (gt_hi, gt_lo, G_MEM) if g < KT // 2 else (xt_hi, xt_lo, G_MIX)
                for j in range(2):
                    kt = 2 * (g % (KT // 2)) + j
                    v = V.scalar_tensor_tensor(lo[:, kt, :], bank[g % 4][:, j * 2 * P:(j + 1) * 2 * P],
                                               gains[:, g0 + kt:g0 + kt + 1], f32(hi[:, kt, :]),
                                               ALU.mult, ALU.subtract)
                v.then_inc(in_lo, 1)
            dve.wait_ge(wa_hi_done, 1)
            V.tensor_tensor(wa_lo[:, :, :], wa_raw[:, :, :], f32(wa_hi[:, :, :]), ALU.subtract).then_inc(wa_split, 1)
            split_some(M0, None, 0, 0, 4)
            dve.wait_ge(rms_in_done, 1)
            V.reciprocal(rstd_in[:, :, :], rms_in[:, :, :]).then_inc(rstd_in_done, 1)
            prod = sq[:, 0, 0:2 * DK].rearrange("p (a b) -> p a b", a=2)
            own.step(V.tensor_tensor(prod, lam_v[:, 0:4:2, :], lam_v[:, 1:4:2, :], ALU.mult))
            V.reduce_sum(lam_dot[:, :], prod, AX.X).then_inc(lam_dot_done, 1)
            own.step(V.tensor_scalar(sub_gain[:, :], sub_gain[:, :], 1.0 - LAM_INIT, None, ALU.mult))
            split_some(M0, None, 0, 4, LEAD - 4)

            def squares(tiles_before, i, t, item):
                dve.wait_ge(acc_free[t], nth(tiles_before, i, 1, 2))
                off = i * TILE + (MK + item * TILE)
                for h in range(HALVES):
                    z = zh[:, 2 * t:2 * t + 2, bass.ds(off + h * DH, DH)]
                    v = V.tensor_tensor(sq[:, h, :].rearrange("p (n c) -> p n c", n=2), z, z, ALU.mult)
                own.step(v)
                for h in range(HALVES):
                    v = V.reduce_sum(ssq_z[:, 2 * t:2 * t + 2, i + item, 2 * h:2 * h + 2],
                                     sq[:, h, :].rearrange("p (n j c) -> p n j c", n=2, c=DK), AX.X)
                own.step(v)

            with dve.Fori(0, MN) as i:
                own.enter(i, 4)
                for t in range(2):
                    split_some(M0, i, MP, LEAD + t * CPT, CPT)
                    squares(M_T, i, t, 0)
                own.leave(MN)
            with dve.Fori(0, IN) as i:
                own.enter(i, 4)
                for t in range(2):
                    split_some(I0, i, IP, LEAD + t * CPT, CPT)
                    squares(I_T, i, t, 2)
                own.leave(IN)

            V.tensor_scalar(ms_z[:, :, 0:8].rearrange("p n (a b) -> p n a b", a=2), ssq_z[:, :, 2:4, :],
                            1.0 / DK, None, ALU.mult)
            for place, item in ((8, 5), (10, 0)):
                v = V.tensor_tensor(ms_z[:, :, place:place + 2], ssq_z[:, :, item, 0:4:2],
                                    ssq_z[:, :, item, 1:4:2], ALU.add)
            own.step(v)
            V.tensor_scalar(ms_z[:, :, 8:12], ms_z[:, :, 8:12], 1.0 / DH, None, ALU.mult).then_inc(ms_z_done, 1)
            dve.wait_ge(lln_done, 1)
            for h in range(HALVES):
                v = V.scalar_tensor_tensor(log_a[:, h, :], bank[2 + h][:, :], 0.0, labs[:, h, :],
                                           ALU.min, ALU.subtract)
            v.then_inc(log_a_done, 1)
            dve.wait_ge(log_a_done, 1)
            V.memset(k_tail[CHUNK:P, 0, :, :], 0.0)
            V.memset(k_tail[0:CHUNK, 1, :, :], 0.0)
            V.memset(att[0:CHUNK, :, CHUNK:P], 0.0)
            own.step(V.memset(att[CHUNK:P, :, 0:CHUNK], 0.0))
            dve.wait_ge(lam_exp_done, 1)
            V.tensor_scalar(neg_lam[:, :], lam_exp[:, 1:2], lam_exp[:, 0:1], -LAM_INIT, ALU.subtract, ALU.add)
            dve.wait_ge(rms_z_done, 1)
            own.step(V.reciprocal(rstd_z[:, :, :], rstd_z[:, :, :]))
            with dve.Fori(0, LN) as i:
                split_some(L0, i, LP, LEAD, LP)
            dve.wait_ge(decay_done, 1)
            dve.wait_ge(acc_free[1], L_T + LN + 1)

            with dve.Fori(0, GN) as n:
                own.enter(n, DVE_HEAD_STEPS)

                def store_gates(t):
                    dve.wait_ge(chunk_used, nth(G0, n, GP, (t + 1) * CPT) + RING)
                    dve.wait_ge(bias_landed[t], 16 * (n + 1))
                    for h in range(HALVES):
                        v = V.scalar_tensor_tensor(gates[:, n * 2 + t, h, :], acc[t][:, h, :],
                                                   rstd_in[:, 1, h:h + 1], bias[:, t, :], ALU.mult, ALU.add)
                    own.step(v)
                    dve.sem_inc(acc_free[t], 1)
                    dve.sem_inc(bias_used, 1)

                def normalise(q, k, at, width, done):
                    m = DH // width
                    for dst, src, r in ((qn, q, at), (kn, k, at + HALVES * m)):
                        z = zh[:, n, src:src + HALVES * DH].rearrange("p (g c) -> p g c", c=width)
                        s = rstd_z[:, n, r:r + HALVES * m].unsqueeze(2).to_broadcast([P, HALVES * m, width])
                        v = V.tensor_tensor(dst[:, :, :].rearrange("p h (m c) -> p (h m) c", m=m), z, s, ALU.mult)
                    v.then_inc(done, 1)

                def gla_decayed():
                    dve.wait_ge(ge_ready, n + 1)
                    zq, zk = zh[:, n, GQ:GQ + 2 * DK], zh[:, n, GK:GK + 2 * DK]
                    flat = lambda a: a.rearrange("p h c -> p (h c)")
                    V.scalar_tensor_tensor(flat(qd[:, :, :]), zq, DK ** -0.5, flat(qd[:, :, :]), ALU.mult, ALU.mult)
                    V.tensor_tensor(flat(kd[:, :, :]), zk, flat(kd[:, :, :]), ALU.mult)
                    V.tensor_copy(decay_h[:, :], decay[:, n, :])
                    for c in range(2):
                        r = slice(c * CHUNK, (c + 1) * CHUNK)
                        v = V.tensor_tensor(flat(k_tail[r, c, :, :]), zk[r, :], flat(e_tail[r, :, :]), ALU.mult)
                    own.step(v)
                    dve.sem_inc(gd_ready, 1)

                def diff_k():
                    dve.wait_ge(d_turned, n + 1)
                    V.tensor_scalar(k_t[:, :, :], bank[1][:, :].rearrange("p (j t) -> p j t", j=2),
                                    gains[:, G_DK:G_DK + 1], None, ALU.mult).then_inc(dkt_ready, 1)

                def gla_states():
                    dve.wait_ge(g_inc, n + 1)
                    own.step(V.tensor_copy(state[:, 0, :], bank[3][:, 0:DH]))
                    own.step(V.scalar_tensor_tensor(state[:, 1, :], state[:, 0, :], decay_h[:, 1:2],
                                                    bank[3][:, DH:2 * DH], ALU.mult, ALU.add))

                def gla_last_state():
                    dve.wait_ge(g_att, n + 1)
                    dve.wait_ge(ga_copied, n + 1)
                    V.scalar_tensor_tensor(state[:, 2, :], state[:, 1, :], decay_h[:, 2:3],
                                           bank[2][:, DH:2 * DH], ALU.mult, ALU.add).then_inc(gs_ready, 1)

                def diff_max():
                    dve.wait_ge(d_scores, n + 1)
                    s1 = bank[0][:, :].rearrange("p (j k) -> p j k", j=2)
                    s0 = bank[1][:, 0:2 * P].rearrange("p (j k) -> p j k", j=2)
                    V.memset(s1[0:CHUNK, :, 3 * CHUNK:4 * CHUNK], NEG)
                    own.step(V.memset(s0[0:CHUNK, :, CHUNK:2 * CHUNK], NEG))
                    V.reduce_max(rmax[:, 0:2], s1, AX.X)
                    own.step(V.reduce_max(rmax[:, 2:4], s0, AX.X))
                    V.tensor_scalar(nmax[:, 0:4], rmax[:, 0:4], -DK ** -0.5, None, ALU.mult).then_inc(dmax_ready, 1)

                def diff_weights():
                    dve.wait_ge(dp_ready, n + 1)
                    own.step(V.reciprocal(rsum[:, 0:4], psum_exp[:, 0:4]))
                    own.step(V.tensor_scalar(lam_r[:, :], rsum[:, 1:4:2], neg_lam[:, :], None, ALU.mult))
                    V.tensor_scalar(prob[:, 2 * P:4 * P], prob[:, 2 * P:4 * P], lam_r[:, 0:1], None, ALU.mult)
                    own.step(V.tensor_scalar(prob[:, 5 * P:6 * P], prob[:, 5 * P:6 * P], lam_r[:, 1:2], None, ALU.mult))
                    V.scalar_tensor_tensor(prob[:, 0:2 * P], prob[:, 0:2 * P], rsum[:, 0:1],
                                           prob[:, 2 * P:4 * P], ALU.mult, ALU.add)
                    V.scalar_tensor_tensor(prob[:, 4 * P:5 * P], prob[:, 4 * P:5 * P], rsum[:, 2:3],
                                           prob[:, 5 * P:6 * P], ALU.mult, ALU.add).then_inc(da_ready, 1)

                def mem_k():
                    dve.wait_ge(m_turned, n + 1)
                    for j in range(2):
                        v = V.tensor_scalar(k_t[:, j, :], bank[3][:, j * 2 * P:(j + 1) * 2 * P],
                                            gains[:, G_MK + j:G_MK + j + 1], None, ALU.mult)
                    v.then_inc(mkt_ready, 1)

                def mem_max():
                    dve.wait_ge(m_scores, n + 1)
                    own.step(V.reduce_max(rmax[:, 4:6], bank[1][:, :].rearrange("p (h k) -> p h k", h=2), AX.X))
                    V.tensor_scalar(nmax[:, 4:6], rmax[:, 4:6], -DH ** -0.5, None, ALU.mult).then_inc(mmax_ready, 1)

                def gla_silu():
                    dve.wait_ge(gg_exp, n + 1)
                    own.step(V.tensor_scalar(sg[:, :, :], sg[:, :, :], 1.0, None, ALU.add))
                    own.step(V.reciprocal(sg[:, :, :], sg[:, :, :]))
                    flat = sg[:, :, :].rearrange("p h c -> p (h c)")
                    own.step(V.tensor_tensor(flat, flat, zh[:, n, GG:GG + 2 * DH], ALU.mult))
                    own.step(V.tensor_tensor(sg[:, :, :], sg[:, :, :],
                                             gla_gain[:, :].unsqueeze(1).to_broadcast([P, HALVES, DH]), ALU.mult))

                def outputs():
                    dve.wait_ge(go_rms, n + 1)
                    own.step(V.reciprocal(rstd_o[:, :], rms_o[:, :]))
                    for h in range(HALVES):
                        v = V.scalar_tensor_tensor(sg[:, h, :], bank[2][:, h * DH:(h + 1) * DH],
                                                   rstd_o[:, 2 + h:3 + h], sg[:, h, :], ALU.mult, ALU.mult)
                    v.then_inc(gy_ready, 1)
                    for h in range(HALVES):
                        v = V.scalar_tensor_tensor(kn[:, h, :], bank[0][:, h * DH:(h + 1) * DH],
                                                   rstd_o[:, h:h + 1], sub_gain[:, :], ALU.mult, ALU.mult)
                    v.then_inc(dy_ready, 1)

                def mem_output():
                    dve.wait_ge(m_out, n + 1)
                    own.step(V.reciprocal(rsum[:, 4:6], psum_exp[:, 4:6]))
                    for h in range(HALVES):
                        v = V.tensor_scalar(qn[:, h, :], bank[1][:, h * DH:(h + 1) * DH], rsum[:, 4 + h:5 + h],
                                            None, ALU.mult)
                    v.then_inc(my_ready, 1)

                def y_lo(hi_done, b, place, done):
                    dve.wait_ge(hi_done, n + 1)
                    V.tensor_tensor(yt[:, n, place + 2 * DH:place + 4 * DH], bank[b][:, :],
                                    f32(yt[:, n, place:place + 2 * DH]), ALU.subtract).then_inc(done, 1)

                for s in range(GP):
                    split(G0, n, GP, LEAD + s)
                    if s == 0:
                        normalise(DQ, DKO, 0, DK, dn_ready)
                        gla_decayed()
                    if s == 1:
                        diff_k()
                        normalise(MQ, MK, 8, DH, mn_ready)
                    if s == 2:
                        gla_states()
                    if s == 3:
                        diff_max()
                        diff_weights()
                        store_gates(0)
                    if s == 4:
                        gla_last_state()
                    if s == 5:
                        mem_k()
                        gla_silu()
                    if s == 7:
                        outputs()
                        mem_max()
                    if s == 9:
                        y_lo(gy_hi, 2, GQ, gy_lo)
                        y_lo(dy_hi, 0, DQ, dy_lo)
                    if s == 10:
                        mem_output()
                    if s == 11:
                        store_gates(1)
                    if s == 13:
                        y_lo(my_hi, 1, MK, my_lo)
                own.leave(GN)

            def turned_lo(k, write):
                for b in range(2):
                    dve.wait_ge(res_hi, k * 2 + (b + 1))
                    write(b).then_inc(res_lo, 1)

            def lo_of(lo, hi, first, b):
                r = bass.ds(first + 2 * b, 2)
                return V.tensor_tensor(lo[:, r, :], bank[b][:, :].rearrange("p (k t) -> p k t", k=2),
                                       f32(hi[:, r, :]), ALU.subtract)

            with dve.Fori(0, BN) as c:
                own.enter(c, 3)
                split_some(B0, c, BP, LEAD, 4)
                dve.wait_ge(chunk_used, nth(B0, c, BP, CPT) + RING)
                dve.wait_ge(bias_landed[0], 16 * (c + (GN + 1)))
                for h in range(HALVES):
                    v = V.scalar_tensor_tensor(g2[:, h, :], acc[0][:, h, :], rstd_in[:, 1, h:h + 1],
                                               bias[:, 0, :], ALU.mult, ALU.add)
                own.step(v)
                dve.sem_inc(g2_ready, 1)
                dve.sem_inc(acc_free[0], 1)
                dve.sem_inc(bias_used, 1)
                for b in range(3):
                    split_some(B0, c, BP, LEAD + 4 * (b + 1), 4)
                    slot = (b + 1) % 2
                    dve.wait_ge(chunk_used, nth(B0, c, BP, CPT + (b + 1) * CPB) + RING)
                    dve.wait_ge((sig_g01, sig_g01, sig_g2)[b], c + 1)
                    g = (gates[:, c, :, :], gates[:, c + COLS, :, :], g2[:, :, :])[b]
                    v = V.tensor_tensor(g, g, acc[slot][:, :, :], ALU.mult)
                    v.then_inc(acc_free[slot], 1)
                    if b > 0:
                        dve.wait_ge(acc_free[slot], nth(B_T, c, 2, 3))
                        sums = gates[:, c, :, :]
                        if b == 1:
                            own.step(V.tensor_tensor(sums, sums, gates[:, c + COLS, :, :], ALU.add))
                        else:
                            own.step(V.tensor_tensor(res[:, :, :], sums, g2[:, :, :], ALU.add))
                            dve.sem_inc(res_ready, 1)
                split_some(B0, c, BP, LEAD + 16, 4)
                turned_lo(c, lambda b: lo_of(gt_lo, gt_hi, c * 4, b))
                own.leave(BN)

            for t in range(COLS):
                split_some(O0, None, 0, LEAD + t * CPT, 4)
                k = BN + t
                s = t % 2
                dve.wait_ge(chunk_used, O0 + (t + 1) * CPT + RING)
                dve.wait_ge(xin_landed[s], 16 * (t // 2 + 1))
                if t > 0:
                    dve.wait_ge(x1_squared, t)
                V.tensor_tensor(res[:, :, :], acc[s][:, :, :], xin[:, s, :, :], ALU.add).then_inc(acc_free[s], 1)
                dve.wait_ge(acc_free[s], O_T + t // 2 + 2)
                dve.sem_inc(res_ready, 1)
                if t == COLS - 1:
                    dve.wait_ge(x1_squared, COLS)
                    V.reduce_sum(sum_x1[:, :], ssq_x1[:, :, :], AX.X).then_inc(x1_sum, 1)
                split_some(O0, None, 0, LEAD + t * CPT + 4, 4)
                for b in range(2):
                    dve.wait_ge(res_hi, 2 * k + b + 1)
                    for j in range(2):
                        kt = 4 * t + 2 * b + j
                        v = V.scalar_tensor_tensor(xt_lo[:, kt, :], bank[b][:, j * 2 * P:(j + 1) * 2 * P],
                                                   gains[:, G_FFN + kt:G_FFN + kt + 1], f32(xt_hi[:, kt, :]),
                                                   ALU.mult, ALU.subtract)
                    v.then_inc(res_lo, 1)
            dve.wait_ge(x1_rms, 1)
            V.reciprocal(rstd_x1[:, :], rms_x1[:, :]).then_inc(x1_rstd, 1)
            dve.wait_ge(x1_rstd, 1)
            with dve.Fori(0, FN) as i:
                split_some(F0, i, FP, LEAD, 12)
                dve.wait_ge(chunk_used, nth(F0, i, FP, FP) + RING)
                dve.wait_ge(acc_free[0], i + (F_T + 2))
                own.enter(i, 1)
                for h in range(HALVES):
                    v = V.scalar_tensor_tensor(res[:, h, :], acc[1][:, h, :], rstd_x1[:, h:h + 1], g2[:, h, :],
                                               ALU.mult, ALU.mult)
                own.step(v)
                dve.sem_inc(acc_free[1], 1)
                dve.sem_inc(res_ready, 1)
                split_some(F0, i, FP, LEAD + 12, 4)
                turned_lo(i + (BN + COLS), lambda b: lo_of(act_lo, act_hi, i * 4, b))
                own.leave(FN)
            for t in range(COLS):
                u = LEAD + t * CPD
                last = t == COLS - 1
                split_some(D0, None, 0, u, CPD - LEAD if last else CPD - 4)
                dve.wait_ge(chunk_used, D0 + (t + 1) * CPD + RING)
                V.tensor_tensor(fin[:, t, :, :], acc[t % 2][:, :, :], x1[:, :, t * TILE:(t + 1) * TILE], ALU.add
                                ).then_inc(acc_free[t % 2], 1)
                dve.wait_ge(acc_free[t % 2], D_T + t // 2 + 2)
                dve.sem_inc(fin_ready, 1)
                if not last:
                    split_some(D0, None, 0, u + CPD - 4, 4)

        @block.gpsimd
        def _(pool):
            own = Tally(pool, pool_step)
            G = nc.gpsimd
            G.memset(eps[:, :], EPS)
            G.memset(chunk_of[:, :], 0.0)
            G.memset(ident[:, :], 0.0)
            G.memset(upto[:, :], 0.0)
            own.step(G.memset(after[:, :], 0.0))
            for c in range(2):
                r = slice(c * CHUNK, (c + 1) * CHUNK)
                G.memset(chunk_of[r, c:c + 1], 1.0)
                G.memset(upto[r, r], 1.0)
                m = G.memset(after[r, r], 1.0)
            own.step(m)
            G.affine_select(out=ident[:, :], in_=ident[:, :], compare_op=ALU.not_equal, fill=1.0, base=0,
                            pattern=[[-1, P]], channel_multiplier=1)
            G.affine_select(out=upto[:, :], in_=upto[:, :], compare_op=ALU.is_ge, fill=0.0, base=0,
                            pattern=[[1, P]], channel_multiplier=-1)
            G.affine_select(out=after[:, :], in_=after[:, :], compare_op=ALU.is_gt, fill=0.0, base=0,
                            pattern=[[-1, P]], channel_multiplier=1).then_inc(consts_ready, 1)
            with pool.Fori(0, GN) as n:
                pool.wait_ge(ga_copied, n + 1)
                pool.sem_inc(passed_pool, 1)
                for c in range(2):
                    r = slice(c * CHUNK, (c + 1) * CHUNK)
                    m = G.affine_select(out=att[r, :, r], in_=att[r, :, r], compare_op=ALU.is_ge, fill=0.0,
                                        base=0, pattern=[[0, HALVES], [1, CHUNK]], channel_multiplier=-1)
                m.then_inc(ga_ready, 1)


_INS = ["x", "mem", "norm_mix_g", "norm_mem_g", "w_in", "gla_w_alpha_up", "gla_b_alpha", "gla_norm_g",
        "diff_q_norm_g", "diff_k_norm_g", "diff_lambda_q1", "diff_lambda_k1", "diff_lambda_q2",
        "diff_lambda_k2", "diff_subln_g", "mem_q_norm_g", "mem_k_norm_g", "w_mem_kv", "w_branch",
        "w_gate", "b_gate", "w_out", "norm_ffn_g", "w_ffn_in", "w_ffn_down"]


def kernel(**inputs):
    import numpy as np
    import concourse.bacc as bacc
    from concourse.bass_utils import run_bass_kernel_spmd

    nc = bacc.Bacc("TRN2", target_bir_lowering=False, num_devices=1, dynamic_dma_scratch_size=1024)
    arrays, args = {}, []
    for name in _INS:
        a = np.ascontiguousarray(inputs[name])
        arrays[f"in_{name}"] = a
        args.append(nc.dram_tensor(f"in_{name}", a.shape, mybir.dt.from_np(a.dtype), kind="ExternalInput").ap())
    shape = inputs["x"].shape
    out = nc.dram_tensor("out", shape, FP32, kind="ExternalOutput").ap()
    hybrid_layer(nc, *args, out)
    result = run_bass_kernel_spmd(nc, [arrays], core_ids=[0])
    return result.results[0]["out"]
```

```python
import math
from contextlib import ExitStack

import concourse.bass as bass
from concourse import mybir

FP32 = mybir.dt.float32
FP32R = mybir.dt.float32r
ACT = mybir.ActivationFunctionType
ALU = mybir.AluOpType
AX = mybir.AxisListType

P = 128
HALVES = 2
TILE = 512
KPC = 2
RING = 4
LOW_AT = 17
LEAD = 8
CHUNK = 64
HEADS = 4
DH = 256
DK = 128
RANK = 16
EPS = 1e-6
GATE_NORM = 16.0
NEG = -1e30
LAM_INIT = 0.8 - 0.6 * math.exp(0.0)
ACT_HEAD_STEPS = 1
DVE_HEAD_STEPS = 17


class Tally:

    def __init__(self, engine, sem):
        self.engine, self.sem, self.base, self.n, self.loop, self.per = engine, sem, 0, 0, None, 0

    def enter(self, loop, per):
        self.base, self.n, self.loop, self.per = self.base + self.n, 0, loop, per

    def leave(self, times):
        assert self.n == self.per, f"{self.n} steps in a loop's body, {self.per} were stated"
        self.base, self.n, self.loop = self.base + self.per * times, 0, None

    def now(self):
        if self.loop is None:
            return self.base + self.n
        return self.loop * self.per + (self.base + self.n)

    def step(self, instruction):
        instruction.then_inc(self.sem, 1)
        self.n += 1
        self.engine.wait_ge(self.sem, self.now())


def hybrid_layer(nc, x, mem, norm_mix_g, norm_mem_g, w_in, gla_w_alpha_up, gla_b_alpha, gla_norm_g,
                 diff_q_norm_g, diff_k_norm_g, diff_lambda_q1, diff_lambda_k1, diff_lambda_q2,
                 diff_lambda_k2, diff_subln_g, mem_q_norm_g, mem_k_norm_g, w_mem_kv, w_branch,
                 w_gate, b_gate, w_out, norm_ffn_g, w_ffn_in, w_ffn_down, out):
    D = x.shape[2]
    DFF = w_ffn_down.shape[1]
    KT = D // P
    KTB = HEADS * DH // P
    KTF = DFF // P
    COLS = D // TILE
    CPT = KT // KPC
    CPB = KTB // KPC
    CPD = KTF // KPC
    FT = DFF // TILE

    M0, MN, MP = 0, 2, 2 * CPT
    I0, IN, IP = M0 + MN * MP, 4, 2 * CPT
    L0, LN, LP = I0 + IN * IP, 3, 2 * CPT
    G0, GN, GP = L0 + LN * LP, HEADS, 2 * CPT
    B0, BN, BP = G0 + GN * GP, COLS, CPT + 3 * CPB
    O0, ON, OP = B0 + BN * BP, 2, 2 * CPT
    F0, FN, FP = O0 + ON * OP, FT, 2 * CPT
    D0, DN, DP = F0 + FN * FP, 2, 2 * CPD
    END = D0 + DN * DP
    PARAMS = 13
    M_T, I_T, L_T, G_T = 0, MN, MN + IN, MN + IN + LN
    B_T = G_T + GN
    O_T = B_T + 2 * BN
    F_T = O_T + ON
    D_T = F_T + FN

    GLA_COLS = 2 * HEADS * DK + 2 * HEADS * DH
    DIFF_COL = GLA_COLS + RANK

    def rows(w):
        return w.rearrange("o (k p) n -> (o p) k n", p=P)

    w_in_v, w_kv_v, w_gate_v, w_out_v = rows(w_in), rows(w_mem_kv), rows(w_gate), rows(w_out)
    w_fin_v, w_down_v = rows(w_ffn_in), rows(w_ffn_down)
    w_br_v = w_branch.rearrange("o i (k p) n -> (o p) i k n", p=P)
    x_v = x.rearrange("o (h p) d -> (o p) h d", p=P)
    mem_v = mem.rearrange("o (h p) d -> (o p) h d", p=P)
    out_v = out.rearrange("o (h p) d -> (o p) h d", p=P)

    ctx = ExitStack()
    with ctx:
        SLOT = KPC * TILE * 4
        CONST = 1152
        BIAS = CONST + 5888
        RAW = BIAS + 2 * TILE * 4
        XT = RAW + 3 * RING * SLOT
        ATT = XT + 2 * KT * HALVES * P * 4
        ZH = ATT + 28672
        ZHEAD = 9 * TILE
        GATE = ZH + HEADS * ZHEAD * 4
        assert GATE + 2 * COLS * HALVES * TILE * 4 <= nc.sbuf_usable_end - 24
        used = [CONST]

        def sb(name, shape, offset, dt=FP32):
            return nc.alloc_sbuf_tensor_at(name, shape, dt, offset=offset)

        def const(name, shape):
            at = used[0]
            n = 4 * math.prod(shape[1:])
            used[0] = at + -(-n // 32) * 32
            assert used[0] <= BIAS
            return sb(name, shape, at)

        ident = const("ident", [P, P])
        upto = const("upto", [P, P])
        after = const("after", [P, P])
        chunk_of = const("chunk_of", [P, 2])
        G_MEM, G_MIX, G_FFN, G_DQ, G_DK, G_MQ, G_MK = 0, KT, 2 * KT, 3 * KT, 3 * KT + 1, 3 * KT + 2, 3 * KT + 4
        NG = 3 * KT + 6
        NG1 = 2 * KT
        gains = const("gains", [P, NG])
        gla_gain = const("gla_gain", [P, DH])
        sub_gain = const("sub_gain", [P, DH])
        eps = const("eps", [P, 1])
        lam_dot = const("lam_dot", [P, 2])
        lam_exp = const("lam_exp", [P, 2])
        neg_lam = const("neg_lam", [P, 1])
        ssq_in = const("ssq_in", [P, 2, HALVES])
        rms_in = const("rms_in", [P, 2, HALVES])
        rstd_in = const("rstd_in", [P, 2, HALVES])
        ssq_x1 = const("ssq_x1", [P, HALVES, COLS])
        sum_x1 = const("sum_x1", [P, HALVES])
        rms_x1 = const("rms_x1", [P, HALVES])
        rstd_x1 = const("rstd_x1", [P, HALVES])
        ssq_z = const("ssq_z", [P, HEADS, 6, HALVES * 2])
        ms_z = const("ms_z", [P, HEADS, 12])
        rstd_z = const("rstd_z", [P, HEADS, 12])
        decay = const("decay", [P, HEADS, 4])
        decay_h = const("decay_h", [P, 4])
        rmax = const("rmax", [P, 6])
        nmax = const("nmax", [P, 6])
        psum_exp = const("psum_exp", [P, 6])
        rsum = const("rsum", [P, 6])
        lam_r = const("lam_r", [P, 2])
        ssq_o = const("ssq_o", [P, 4])
        rms_o = const("rms_o", [P, 4])
        rstd_o = const("rstd_o", [P, 4])

        bias = sb("bias", [P, 2, TILE], BIAS)
        raw = sb("raw", [P, RING, KPC, TILE], RAW)
        whi = sb("whi", [P, RING, KPC, TILE], RAW + RING * SLOT, FP32R)
        wlo = sb("wlo", [P, RING, KPC, TILE], RAW + 2 * RING * SLOT, FP32R)
        xt_hi = sb("xt_hi", [P, KT, HALVES * P], XT, FP32R)
        xt_lo = sb("xt_lo", [P, KT, HALVES * P], XT + KT * HALVES * P * 4, FP32R)
        gt_lo = sb("gt_lo", [P, KT, HALVES * P], GATE, FP32R)
        gt_hi = sb("gt_hi", [P, KT, HALVES * P], GATE + KT * HALVES * P * 4, FP32R)
        gates = sb("gates", [P, 2 * COLS, HALVES, TILE], GATE)
        zh = sb("zh", [P, HEADS, ZHEAD], ZH)
        yt = sb("yt", [P, HEADS, ZHEAD], ZH, FP32R)
        MK, MV, DQ, DKO, DV, MQ, GQ, GK, GV, GG = 0, 512, 1024, 1536, 2048, 2560, 3072, 3328, 3584, 4096
        Y_OF = {0: GQ, 1: DQ, 2: MK}
        x_raw = zh[:, 0:HALVES, DQ:DQ + D]
        mem_raw = zh[:, HALVES:2 * HALVES, DQ:DQ + D]
        junk = sb("junk", [P, D], ATT + 13312)
        sq = sb("sq", [P, HALVES, TILE], ATT)
        lam_v = sb("lam_v", [P, 4, DK], ATT + 4096)
        alpha_up = sb("alpha_up", [RANK, HEADS * DK], ATT + 6144)
        low_t = sb("low_t", [RANK, HALVES * P], ATT + 8192)
        wa_raw = sb("wa_raw", [P, KT, RANK], ATT + 9216)
        wa_hi = sb("wa_hi", [P, KT, RANK], ATT + 10240, FP32R)
        wa_lo = sb("wa_lo", [P, KT, RANK], ATT + 11264, FP32R)
        gain_rows = sb("gain_rows", [NG1, P], ATT + 12288)
        gain_rows2 = sb("gain_rows2", [NG - NG1, P], ATT + 12800)
        alpha_b = sb("alpha_b", [P, HEADS * DK], ATT + 21504)
        labs = sb("labs", [P, HALVES, HEADS * DK], ATT + 13312)
        lexp = sb("lexp", [P, HALVES, HEADS * DK], ATT + 17408)
        qn = sb("qn", [P, HALVES, DH], ATT)
        kn = sb("kn", [P, HALVES, DH], ATT + 2048)
        q_t = sb("q_t", [P, 2, HALVES * P], ATT + 4096)
        k_t = sb("k_t", [P, 2, HALVES * P], ATT + 6144)
        prob = sb("prob", [P, 768], ATT + 8192)
        prob_t = sb("prob_t", [P, TILE], ATT + 11264)
        qd = sb("qd", [P, HALVES, DK], ATT + 13312)
        kd = sb("kd", [P, HALVES, DK], ATT + 14336)
        sg = sb("sg", [P, HALVES, DH], ATT + 13312)
        k_tail = sb("k_tail", [P, 2, HALVES, DK], ATT + 15360)
        e_tail = sb("e_tail", [P, HALVES, DK], ATT + 17408)
        g_t = sb("g_t", [P, 2, HALVES * P], ATT + 18432)
        att = sb("att", [P, HALVES, P], ATT + 20480)
        state = sb("state", [P, 3, DH], ATT + 21504)
        log_a = sb("log_a", [P, HALVES, HEADS * DK], ATT + 24576)
        res = sb("res", [P, HALVES, TILE], ATT)
        g2 = sb("g2", [P, HALVES, TILE], ATT + 8192)
        x1 = sb("x1", [P, HALVES, D], ATT + 12288)
        xin = sb("xin", [P, 2, HALVES, TILE], ZH)
        sq1 = sb("sq1", [P, HALVES, TILE], ZH + 8192)
        act_hi = sb("act_hi", [P, KTF, HALVES * P], ZH, FP32R)
        act_lo = sb("act_lo", [P, KTF, HALVES * P], ZH + KTF * HALVES * P * 4, FP32R)
        fin = sb("fin", [P, COLS, HALVES, TILE], GATE + 16384)

        acc = [ctx.enter_context(nc.psum_tensor(f"acc{s}", [P, HALVES, TILE], FP32)) for s in range(2)]
        bank = [ctx.enter_context(nc.psum_tensor(f"bank{b}", [P, TILE], FP32)) for b in range(4)]

        def sem(name):
            return ctx.enter_context(nc.semaphore(name))

        chunk_split = sem("chunk_split")
        chunk_used = sem("chunk_used")
        acc_free = [sem(f"acc_free{s}") for s in range(2)]
        bias_used = sem("bias_used")
        raw_landed = [sem(f"raw_landed{s}") for s in range(RING)]
        chunk_hi = sem("chunk_hi")
        bias_landed = [sem(f"bias_landed{s}") for s in range(2)]
        act_step = sem("act_step")
        dve_step = sem("dve_step")
        pool_step = sem("pool_step")
        passed_sp, passed_pool = sem("passed_sp"), sem("passed_pool")
        params_landed = sem("params_landed")
        wa_landed = sem("wa_landed")
        gains_landed = sem("gains_landed")
        in_landed = [sem(f"in_landed{k}") for k in range(2 * COLS)]
        eps_ready = sem("eps_ready")
        ident_ready = sem("ident_ready")
        consts_ready = sem("consts_ready")
        gains_turned = sem("gains_turned")
        gains_ready = sem("gains_ready")
        in_turned = sem("in_turned")
        in_hi = sem("in_hi")
        in_lo = sem("in_lo")
        ssq_in_done = sem("ssq_in_done")
        rms_in_done = sem("rms_in_done")
        rstd_in_done = sem("rstd_in_done")
        wa_hi_done = sem("wa_hi_done")
        wa_split = sem("wa_split")
        low_done = sem("low_done")
        low_t_ready = sem("low_t_ready")
        lgate_done = sem("lgate_done")
        larg_done = sem("larg_done")
        labs_done = sem("labs_done")
        lln_done = sem("lln_done")
        log_a_done = sem("log_a_done")
        decay_sum = sem("decay_sum")
        decay_done = sem("decay_done")
        ms_z_done = sem("ms_z_done")
        rms_z_done = sem("rms_z_done")
        lam_dot_done = sem("lam_dot_done")
        lam_exp_done = sem("lam_exp_done")
        d_turned, m_turned = sem("d_turned"), sem("m_turned")
        d_scores, m_scores = sem("d_scores"), sem("m_scores")
        dp_turned, mp_turned = sem("dp_turned"), sem("mp_turned")
        d_out, m_out = sem("d_out"), sem("m_out")
        dy_turned, my_turned, gy_turned = sem("dy_turned"), sem("my_turned"), sem("gy_turned")
        g_sums, g_turned, g_inc, g_att, g_out = (sem("g_sums"), sem("g_turned"), sem("g_inc"),
                                                 sem("g_att"), sem("g_out"))
        dn_ready, mn_ready = sem("dn_ready"), sem("mn_ready")
        dqt_ready, mqt_ready = sem("dqt_ready"), sem("mqt_ready")
        dkt_ready, mkt_ready = sem("dkt_ready"), sem("mkt_ready")
        dmax_ready, mmax_ready = sem("dmax_ready"), sem("mmax_ready")
        dp_ready, mp_ready = sem("dp_ready"), sem("mp_ready")
        da_ready = sem("da_ready")
        dpt_ready, mpt_ready = sem("dpt_ready"), sem("mpt_ready")
        do_ssq, do_rms = sem("do_ssq"), sem("do_rms")
        dy_ready, my_ready, gy_ready = sem("dy_ready"), sem("my_ready"), sem("gy_ready")
        dy_hi, my_hi, gy_hi = sem("dy_hi"), sem("my_hi"), sem("gy_hi")
        dy_lo, my_lo, gy_lo = sem("dy_lo"), sem("my_lo"), sem("gy_lo")
        ge_ready = sem("ge_ready")
        gd_ready = sem("gd_ready")
        gt_ready = sem("gt_ready")
        gs_ready = sem("gs_ready")
        ga_copied = sem("ga_copied")
        ga_ready = sem("ga_ready")
        gg_exp = sem("gg_exp")
        go_ssq, go_rms = sem("go_ssq"), sem("go_rms")
        sig_g2, sig_g01 = sem("sig_g2"), sem("sig_g01")
        g2_ready = sem("g2_ready")
        g01_free = sem("g01_free")
        res_ready = sem("res_ready")
        res_turned = sem("res_turned")
        res_hi = sem("res_hi")
        res_lo = sem("res_lo")
        xin_landed = [sem(f"xin_landed{s}") for s in range(2)]
        x1_squared = sem("x1_squared")
        x1_sum = sem("x1_sum")
        x1_rms = sem("x1_rms")
        x1_rstd = sem("x1_rstd")
        silu_done = sem("silu_done")
        fin_ready = sem("fin_ready")
        out_stored = sem("out_stored")

        block = ctx.enter_context(nc.Block())

        def nth(base, i, per, u):
            return base + u if i is None else i * per + (base + u)

        @block.sync
        def _(sp):
            def load_in(k):
                source, view = (mem_raw, mem_v) if k < COLS else (x_raw, x_v)
                r = slice(k % COLS * TILE, (k % COLS + 1) * TILE)
                sp.dma_start(source[:, :, r], view[:, :, r]).then_inc(in_landed[k], 16)

            def load(base, i, per, u, source):
                sp.wait_ge(chunk_split, nth(base, i, per, u) + 1)
                sp.sem_inc(passed_sp, 1)
                sp.dma_start(raw[:, u % RING, :, :], source).then_inc(raw_landed[u % RING], 16)

            def load_tile(base, i, per, u0, view, col, chunks):
                for c in range(chunks):
                    load(base, i, per, u0 + c, view[:, KPC * c:KPC * (c + 1), bass.ds(col, TILE)])

            wa_v = w_in_v[:, :, GLA_COLS:GLA_COLS + RANK]
            params = [(lam_v[:, k, :], v.partition_broadcast(P)) for k, v in
                      enumerate((diff_lambda_q1, diff_lambda_k1, diff_lambda_q2, diff_lambda_k2))]
            params += [(gla_gain[:, :], gla_norm_g.partition_broadcast(P)),
                       (sub_gain[:, :], diff_subln_g.partition_broadcast(P)),
                       (alpha_up[:, :], gla_w_alpha_up[0, :, :]),
                       (alpha_b[:, :], gla_b_alpha.partition_broadcast(P))]
            params += [(gain_rows2[g0 - NG1:g0 - NG1 + m, :], v.rearrange("o (k p) -> (o k) p", p=P))
                       for v, g0, m in ((norm_ffn_g, G_FFN, KT), (diff_q_norm_g, G_DQ, 1),
                                        (diff_k_norm_g, G_DK, 1), (mem_q_norm_g, G_MQ, 2),
                                        (mem_k_norm_g, G_MK, 2))]
            assert len(params) == PARAMS
            load_in(0)
            for u in range(MN * MP):
                c, col = u % CPT, u // CPT * TILE
                load(M0, None, 0, u, w_kv_v[:, KPC * c:KPC * (c + 1), col:col + TILE])
                if u == 0:
                    load_in(1)
                if u in (2, 3, 4, 5, 6, 7):
                    load_in(u)
                if u in (8, 9):
                    r = slice((u - 8) * KT // 2, (u - 7) * KT // 2)
                    sp.dma_start(wa_raw[:, r, :], wa_v[:, r, :]).then_inc(wa_landed, 16)
                if 10 <= u < 10 + PARAMS:
                    sp.dma_start(*params[u - 10]).then_inc(params_landed, 16)
            with sp.Fori(0, IN) as i:
                for t in range(2):
                    load_tile(I0, i, IP, t * CPT, w_in_v, i * (2 * TILE) + (DIFF_COL + t * TILE), CPT)
            with sp.Fori(0, LN) as i:
                for t in range(2):
                    load_tile(L0, i, LP, t * CPT, w_in_v, i * (2 * TILE) + t * TILE, CPT)
            with sp.Fori(0, GN) as i:
                for t in range(2):
                    sp.wait_ge(bias_used, i * 2 + (t + 1))
                    sp.sem_inc(passed_sp, 1)
                    col = i * (2 * TILE) + t * TILE
                    sp.dma_start(bias[:, t, :], b_gate[:, bass.ds(col, TILE)].partition_broadcast(P)
                                 ).then_inc(bias_landed[t], 16)
                    load_tile(G0, i, GP, t * CPT, w_gate_v, col, CPT)
            with sp.Fori(0, BN) as c:
                load_tile(B0, c, BP, 0, w_gate_v, c * TILE + 2 * D, CPT)
                sp.wait_ge(bias_used, c + (2 * GN + 2))
                sp.sem_inc(passed_sp, 1)
                sp.dma_start(bias[:, 0, :], b_gate[:, bass.ds(c * TILE + 2 * D, TILE)].partition_broadcast(P)
                             ).then_inc(bias_landed[0], 16)
                for b in range(3):
                    load_tile(B0, c, BP, CPT + b * CPB, w_br_v[:, b, :, :], c * TILE, CPB)
            with sp.Fori(0, ON) as i:
                for t in range(2):
                    load_tile(O0, i, OP, t * CPT, w_out_v, i * (2 * TILE) + t * TILE, CPT)
                    sp.wait_ge(chunk_used, nth(O0, i, OP, t * CPT) + RING)
                    sp.sem_inc(passed_sp, 1)
                    sp.wait_ge(res_ready, i * 2 + (BN + t - 1))
                    sp.sem_inc(passed_sp, 1)
                    sp.dma_start(xin[:, t, :, :], x_v[:, :, bass.ds(i * (2 * TILE) + t * TILE, TILE)]
                                 ).then_inc(xin_landed[t], 16)
            with sp.Fori(0, FN) as i:
                for t in range(2):
                    load_tile(F0, i, FP, t * CPT, w_fin_v, i * TILE + t * DFF, CPT)
            with sp.Fori(0, DN) as i:
                for t in range(2):
                    load_tile(D0, i, DP, t * CPD, w_down_v, i * (2 * TILE) + t * TILE, CPD)

        @block.tensor
        def _(pe):
            pe.sem_inc(chunk_used, RING)

            def multiply(base, i, per, u, psum, kt, st_hi, st_lo, first, last):
                slot = u % RING
                pe.wait_ge(chunk_split, nth(base, i, per, u) + (RING + 1))
                for j in range(KPC):
                    for h in range(HALVES):
                        a_hi, a_lo = st_hi(kt + j, h), st_lo(kt + j, h)
                        nc.tensor.matmul(psum[:, h, :], a_hi, whi[:, slot, j, :],
                                         start=first and j == 0, stop=False)
                        nc.tensor.matmul(psum[:, h, :], a_hi, wlo[:, slot, j, :], start=False, stop=False)
                        mm = nc.tensor.matmul(psum[:, h, :], a_lo, whi[:, slot, j, :],
                                              start=False, stop=last and j == KPC - 1)
                mm.then_inc(chunk_used, 1)

            def tokens(tensor):
                return lambda kt, h: tensor[:, kt, h * P:(h + 1) * P]

            X = tokens(xt_hi), tokens(xt_lo)
            GT = tokens(gt_hi), tokens(gt_lo)
            AT = tokens(act_hi), tokens(act_lo)

            def Y(branch):
                def hi(kt, h):
                    o = Y_OF[branch] + (kt % 2) * HALVES * P + h * P
                    return yt[:, kt // 2, o:o + P]

                def lo(kt, h):
                    o = Y_OF[branch] + (2 + kt % 2) * HALVES * P + h * P
                    return yt[:, kt // 2, o:o + P]
                return hi, lo

            def tile(base, i, per, u0, chunks, slot, tiles, st, hook=None):
                pe.wait_ge(acc_free[slot], tiles)
                for c in range(chunks):
                    multiply(base, i, per, u0 + c, acc[slot], KPC * c, *st, c == 0, c == chunks - 1)
                    if hook is not None:
                        hook(c)

            def turn_res(k):
                pe.wait_ge(res_ready, k + 1)
                for b in range(2):
                    for j in range(2):
                        for h in range(HALVES):
                            t = nc.tensor.transpose(bank[b][:, j * 2 * P + h * P:j * 2 * P + (h + 1) * P],
                                                    res[:, h, (2 * b + j) * P:(2 * b + j + 1) * P], ident[:, :])
                t.then_inc(res_turned, 1)

            def turn_gains(rows, n, b, done):
                nc.tensor.transpose(bank[b][:, 0:n], rows[:, :], ident[0:n, 0:n]).then_inc(done, 1)

            def turn_in(g):
                source = mem_raw if g < KT // 2 else x_raw
                if g % 2 == 0:
                    pe.wait_ge(in_landed[g // 2], 16)
                if g == 3:
                    pe.wait_ge(gains_ready, 1)
                if g >= 4:
                    pe.wait_ge(in_lo, g - 3)
                for j in range(2):
                    kt = 2 * (g % (KT // 2)) + j
                    for h in range(HALVES):
                        t = nc.tensor.transpose(bank[g % 4][:, j * 2 * P + h * P:j * 2 * P + (h + 1) * P],
                                                source[:, h, kt * P:(kt + 1) * P], ident[:, :])
                t.then_inc(in_turned, 1)

            def low_rank():
                pe.wait_ge(in_lo, 2 * KT // 2)
                pe.wait_ge(wa_split, 1)
                for kt in range(KT):
                    o = bank[0][0:RANK, 0:HALVES * P]
                    nc.tensor.matmul(o, wa_hi[:, kt, :], xt_hi[:, kt, :], start=kt == 0, stop=False)
                    nc.tensor.matmul(o, wa_hi[:, kt, :], xt_lo[:, kt, :], start=False, stop=False)
                    m = nc.tensor.matmul(o, wa_lo[:, kt, :], xt_hi[:, kt, :], start=False, stop=kt == KT - 1)
                m.then_inc(low_done, 1)

            def low_rank_up():
                pe.wait_ge(low_t_ready, 1)
                pe.wait_ge(params_landed, 16 * PARAMS)
                for h in range(HALVES):
                    m = nc.tensor.matmul(bank[2 + h][:, :], low_t[:, h * P:(h + 1) * P], alpha_up[:, :],
                                         start=True, stop=True)
                m.then_inc(lgate_done, 1)

            pe.wait_ge(ident_ready, 1)
            pe.wait_ge(gains_landed, 16 * 2)
            turn_gains(gain_rows, NG1, 3, gains_turned)
            for g in range(4):
                turn_in(g)

            def start(u):
                if u + 4 < 2 * KT // 2:
                    turn_in(u + 4)
                if u == LOW_AT:
                    low_rank()
                if u == LOW_AT + 6:
                    low_rank_up()
                if u == LOW_AT + 7:
                    turn_gains(gain_rows2, NG - NG1, 1, gains_turned)

            for t in range(2 * MN):
                def hook(c, t=t):
                    if t == 0 and c < CPT - 1:
                        pe.wait_ge(in_lo, c + 2)
                    start(t * CPT + c)
                if t == 0:
                    pe.wait_ge(in_lo, 1)
                tile(M0, None, 0, t * CPT, CPT, t % 2, M_T + 1 + t // 2, GT, hook)
            with pe.Fori(0, IN) as i:
                for t in range(2):
                    tile(I0, i, IP, t * CPT, CPT, t, i + (I_T + 1), X)
            with pe.Fori(0, LN) as i:
                for t in range(2):
                    tile(L0, i, LP, t * CPT, CPT, t, i + (L_T + 1), X)
            pe.wait_ge(log_a_done, 1)
            pe.wait_ge(consts_ready, 1)
            for n in range(HEADS):
                for h in range(HALVES):
                    m = nc.tensor.matmul(bank[0][:, n * 4 + 2 * h:n * 4 + 2 * h + 2],
                                         log_a[:, h, n * DK:(n + 1) * DK], chunk_of[:, :], start=True, stop=True)
            m.then_inc(decay_sum, 1)

            with pe.Fori(0, GN) as n:
                def turn_qk(ready, b, done):
                    pe.wait_ge(ready, n + 1)
                    for s, (src, dst) in enumerate(((qn, bank[b[0]]), (kn, bank[b[1]]))):
                        for j in range(2):
                            for h in range(HALVES):
                                t = nc.tensor.transpose(dst[:, j * 2 * P + h * P:j * 2 * P + (h + 1) * P],
                                                        src[:, h, j * P:(j + 1) * P], ident[:, :])
                    t.then_inc(done, 1)

                def turn_y(y, ready, b, done):
                    pe.wait_ge(ready, n + 1)
                    for j in range(2):
                        for h in range(HALVES):
                            t = nc.tensor.transpose(bank[b][:, j * 2 * P + h * P:j * 2 * P + (h + 1) * P],
                                                    y[:, h, j * P:(j + 1) * P], ident[:, :])
                    t.then_inc(done, 1)

                def gla_sums():
                    for h in range(HALVES):
                        nc.tensor.matmul(bank[3][:, h * DK:(h + 1) * DK], upto[:, :],
                                         log_a[:, h, bass.ds(n * DK, DK)], start=True, stop=True)
                    for h in range(HALVES):
                        m = nc.tensor.matmul(bank[3][:, (2 + h) * DK:(3 + h) * DK], after[:, :],
                                             log_a[:, h, bass.ds(n * DK, DK)], start=True, stop=True)
                    m.then_inc(g_sums, 1)

                def gla_turn():
                    pe.wait_ge(gd_ready, n + 1)
                    for s, src in enumerate((qd, kd)):
                        for h in range(HALVES):
                            t = nc.tensor.transpose(bank[2][:, (2 * s + h) * P:(2 * s + h + 1) * P],
                                                    src[:, h, :], ident[:, :])
                    t.then_inc(g_turned, 1)
                    for c in range(2):
                        m = nc.tensor.matmul(bank[3][:, c * DH:(c + 1) * DH], k_tail[:, c, 0, :],
                                             zh[:, n, GV:GV + DH], start=True, stop=True)
                    m.then_inc(g_inc, 1)

                def gla_scores():
                    pe.wait_ge(gt_ready, n + 1)
                    for h in range(HALVES):
                        nc.tensor.matmul(bank[2][:, h * P:(h + 1) * P], g_t[:, 1, h * P:(h + 1) * P],
                                         g_t[:, 0, h * P:(h + 1) * P], start=True, stop=True)
                    m = nc.tensor.matmul(bank[2][:, DH:2 * DH], k_tail[:, 0, 1, :],
                                         zh[:, n, GV + DH:GV + 2 * DH], start=True, stop=True)
                    m.then_inc(g_att, 1)

                def gla_output():
                    pe.wait_ge(ga_ready, n + 1)
                    pe.wait_ge(gs_ready, n + 1)
                    for h in range(HALVES):
                        o = bank[2][:, h * DH:(h + 1) * DH]
                        nc.tensor.matmul(o, att[:, h, :], zh[:, n, GV + h * DH:GV + (h + 1) * DH],
                                         start=True, stop=True, skip_group_check=True)
                        for c in range(2):
                            if 2 * h + c == 0:
                                continue
                            r = slice(c * CHUNK, (c + 1) * CHUNK)
                            m = nc.tensor.matmul(bank[2][r, h * DH:(h + 1) * DH],
                                                 g_t[:, 0, h * P + c * CHUNK:h * P + (c + 1) * CHUNK],
                                                 state[:, 2 * h + c - 1, :], start=False, stop=True,
                                                 skip_group_check=True)
                    m.then_inc(g_out, 1)

                def diff_scores():
                    pe.wait_ge(dqt_ready, n + 1)
                    pe.wait_ge(dkt_ready, n + 1)
                    for j in range(2):
                        nc.tensor.matmul(bank[0][:, j * 2 * P:(j + 1) * 2 * P], q_t[:, j, P:2 * P],
                                         k_t[:, j, :], start=True, stop=True)
                    for j in range(2):
                        m = nc.tensor.matmul(bank[1][:, j * P:(j + 1) * P], q_t[:, j, 0:P],
                                             k_t[:, j, 0:P], start=True, stop=True)
                    m.then_inc(d_scores, 1)

                def diff_turn():
                    pe.wait_ge(da_ready, n + 1)
                    for s, at in enumerate((512, 0, P)):
                        t = nc.tensor.transpose(bank[0][:, s * P:(s + 1) * P], prob[:, at:at + P], ident[:, :])
                    t.then_inc(dp_turned, 1)

                def diff_output():
                    pe.wait_ge(dpt_ready, n + 1)
                    nc.tensor.matmul(bank[0][:, 0:DH], prob_t[:, 0:P], zh[:, n, DV:DV + DH],
                                     start=True, stop=True)
                    nc.tensor.matmul(bank[0][:, DH:2 * DH], prob_t[:, P:2 * P], zh[:, n, DV:DV + DH],
                                     start=True, stop=False)
                    nc.tensor.matmul(bank[0][:, DH:2 * DH], prob_t[:, 2 * P:3 * P],
                                     zh[:, n, DV + DH:DV + 2 * DH], start=False, stop=True).then_inc(d_out, 1)

                def mem_scores():
                    pe.wait_ge(mqt_ready, n + 1)
                    pe.wait_ge(mkt_ready, n + 1)
                    for h in range(HALVES):
                        for j in range(2):
                            m = nc.tensor.matmul(bank[1][:, h * 2 * P:(h + 1) * 2 * P],
                                                 q_t[:, j, h * P:(h + 1) * P], k_t[:, j, :],
                                                 start=j == 0, stop=j == 1)
                    m.then_inc(m_scores, 1)

                def mem_turn():
                    pe.wait_ge(mp_ready, n + 1)
                    for h in range(HALVES):
                        for j in range(2):
                            t = nc.tensor.transpose(bank[1][:, (2 * h + j) * P:(2 * h + j + 1) * P],
                                                    prob[:, (2 * h + j) * P:(2 * h + j + 1) * P], ident[:, :])
                    t.then_inc(mp_turned, 1)

                def mem_output():
                    pe.wait_ge(mpt_ready, n + 1)
                    for h in range(HALVES):
                        for j in range(2):
                            m = nc.tensor.matmul(bank[1][:, h * DH:(h + 1) * DH],
                                                 prob_t[:, (2 * h + j) * P:(2 * h + j + 1) * P],
                                                 zh[:, n, MV + j * DH:MV + (j + 1) * DH],
                                                 start=j == 0, stop=j == 1)
                    m.then_inc(m_out, 1)

                def heads(c):
                    if c == 0:
                        gla_sums()
                    if c == 5:
                        turn_qk(dn_ready, (0, 1), d_turned)
                    if c == 6:
                        gla_turn()
                    if c == 7:
                        diff_scores()
                    if c == 8:
                        gla_scores()
                    if c == 9:
                        diff_turn()
                        turn_qk(mn_ready, (1, 3), m_turned)
                    if c == 10:
                        gla_output()
                    if c == 11:
                        diff_output()
                        mem_scores()
                    if c == 13:
                        mem_turn()
                        turn_y(sg, gy_ready, 2, gy_turned)
                        turn_y(kn, dy_ready, 0, dy_turned)
                    if c == 14:
                        mem_output()
                    if c == 15:
                        turn_y(qn, my_ready, 1, my_turned)

                for t in range(2):
                    tile(G0, n, GP, t * CPT, CPT, t, n + (G_T + 1), X,
                         lambda c, t=t: heads(t * CPT + c))

            def merge_column(c, first):
                def hook(k):
                    if k == 3 and not first:
                        turn_res(c - 1)
                tile(B0, c, BP, 0, CPT, 0, c * 2 + (B_T + 1), X, hook)
                if first:
                    pe.wait_ge(dy_lo, HEADS)
                    pe.wait_ge(my_lo, HEADS)
                    pe.wait_ge(gy_lo, HEADS)
                tile(B0, c, BP, CPT, CPB, 1, c * 2 + (B_T + 1), Y(0))
                tile(B0, c, BP, CPT + CPB, CPB, 0, c * 2 + (B_T + 2), Y(1))
                tile(B0, c, BP, CPT + 2 * CPB, CPB, 1, c * 2 + (B_T + 2), Y(2))

            merge_column(0, True)
            with pe.Fori(1, BN) as c:
                merge_column(c, False)

            with pe.Fori(0, ON) as i:
                for t in range(2):
                    def hook(c, t=t):
                        if c == 3:
                            turn_res(i * 2 + (BN - 1 + t))
                        if c == 5:
                            pe.wait_ge(res_lo, 2 * BN)
                    tile(O0, i, OP, t * CPT, CPT, t, i + (O_T + 1), GT, hook)
            with pe.Fori(0, FN) as i:
                def hook(c):
                    if c == 3:
                        turn_res(i + (BN + COLS - 1))
                    if c == 5:
                        pe.wait_ge(res_lo, 2 * (BN + COLS))
                tile(F0, i, FP, 0, CPT, 0, i + (F_T + 1), X, hook)
                tile(F0, i, FP, CPT, CPT, 1, i + (F_T + 1), X)
            def last_turn(c):
                if c == 3:
                    turn_res(BN + COLS + FT - 1)
                if c == CPD - 3:
                    pe.wait_ge(res_lo, 2 * (BN + COLS + FT))
            for t in range(COLS):
                tile(D0, None, 0, t * CPD, CPD, t % 2, D_T + 1 + t // 2, AT, last_turn if t == 0 else None)

        @block.scalar
        def _(act):
            own = Tally(act, act_step)
            for v, g0 in ((norm_mem_g, G_MEM), (norm_mix_g, G_MIX)):
                act.dma_start(gain_rows[g0:g0 + KT, :], v.rearrange("o (k p) -> (o k) p", p=P)
                              ).then_inc(gains_landed, 16)

            def split(base, i, per, u):
                s = u % RING
                act.wait_ge(raw_landed[s], 16 * nth(base // RING, i, per // RING, u // RING + 1))
                act.wait_ge(chunk_used, nth(base, i, per, u) + 1)
                nc.scalar.activation(whi[:, s, :, :], raw[:, s, :, :], ACT.Copy).then_inc(chunk_hi, 1)

            def split_some(base, i, per, u, count):
                for k in range(count):
                    split(base, i, per, u + k)

            def store_z(base, i, per, t, src, dest):
                act.wait_ge(chunk_used, nth(base, i, per, (t + 1) * CPT) + RING)
                for h in range(HALVES):
                    a = nc.scalar.activation(dest(h), acc[t][:, h, :].rearrange("p (n c) -> p n c", c=dest(h).shape[2]),
                                             ACT.Copy, scale=rstd_in[:, src, h:h + 1])
                a.then_inc(acc_free[t], 1)

            def two_heads(i, item, t):
                return lambda h: zh[:, 2 * t:2 * t + 2, bass.ds(i * TILE + (item + h * DH), DH)]


            def in_group(g):
                act.wait_ge(in_turned, g + 1)
                hi, g0 = (gt_hi, G_MEM) if g < KT // 2 else (xt_hi, G_MIX)
                for j in range(2):
                    kt = 2 * (g % (KT // 2)) + j
                    a = nc.scalar.activation(hi[:, kt, :], bank[g % 4][:, j * 2 * P:(j + 1) * 2 * P], ACT.Copy,
                                             scale=gains[:, g0 + kt:g0 + kt + 1])
                a.then_inc(in_hi, 1)

            def in_squares(k, h):
                source = (mem_raw, x_raw)[k]
                own.step(nc.scalar.activation(junk[:, :], source[:, h, :], ACT.Square,
                                              accum_out=ssq_in[:, k, h:h + 1]))

            def in_rms(k):
                nc.scalar.activation(rms_in[:, k, :], ssq_in[:, k, :], ACT.Sqrt, scale=1.0 / D,
                                     bias=eps[:, :]).then_inc(rms_in_done, 1)

            act.wait_ge(eps_ready, 1)
            own.step(nc.scalar.activation(rms_o[:, 0:1], eps[:, :], ACT.Sqrt))
            act.wait_ge(gains_ready, 1)
            in_group(0)
            in_group(1)
            split(M0, None, 0, 0)
            in_group(2)
            in_group(3)
            split(M0, None, 0, 1)
            for u in range(2, MN * MP + LEAD):
                split(M0, None, 0, u)
                if u + 2 < 2 * KT // 2:
                    in_group(u + 2)
                if u in (8, 9):
                    in_squares(0, u - 8)
                if u == 10:
                    in_rms(0)
                if u == 12:
                    act.wait_ge(wa_landed, 16 * 2)
                    nc.scalar.activation(wa_hi[:, :, :], wa_raw[:, :, :], ACT.Copy).then_inc(wa_hi_done, 1)
                if u in (14, 15):
                    in_squares(1, u - 14)
                if u == 16:
                    in_rms(1)
                if u == LOW_AT + 4:
                    act.wait_ge(low_done, 1)
                    nc.scalar.activation(low_t[:, :], bank[0][0:RANK, 0:HALVES * P], ACT.Copy
                                         ).then_inc(low_t_ready, 1)
                if u == LOW_AT + 12:
                    act.wait_ge(larg_done, 1)
                    own.step(nc.scalar.activation(labs[:, :, :], log_a[:, :, :], ACT.Abs))
                if u == LOW_AT + 13:
                    own.step(nc.scalar.activation(lexp[:, :, :], labs[:, :, :], ACT.Exp, scale=-1.0))
                if u == LOW_AT + 15:
                    nc.scalar.activation(labs[:, :, :], lexp[:, :, :], ACT.Ln, bias=1.0).then_inc(lln_done, 1)
                if u >= LEAD and (u - LEAD) % CPT == 3:
                    t = (u - LEAD) // CPT
                    if t == 0:
                        act.wait_ge(rstd_in_done, 1)
                    store_z(M0, t // 2, MP, t % 2, 0, two_heads(t // 2, MK, t % 2))
            act.wait_ge(rstd_in_done, 2)
            act.wait_ge(gains_ready, 2)
            with act.Fori(0, IN) as i:
                for t in range(2):
                    split_some(I0, i, IP, LEAD + t * CPT, 4)
                    store_z(I0, i, IP, t, 1, two_heads(i, DQ, t))
                    split_some(I0, i, IP, LEAD + t * CPT + 4, CPT - 4)
            act.wait_ge(lam_dot_done, 1)
            nc.scalar.activation(lam_exp[:, :], lam_dot[:, :], ACT.Exp).then_inc(lam_exp_done, 1)
            for t, item in enumerate((GQ, GK)):
                split_some(L0, None, 0, LEAD + t * CPT, 4)
                if t == 0:
                    act.wait_ge(ms_z_done, 1)
                    nc.scalar.activation(rstd_z[:, :, :], ms_z[:, :, :], ACT.Sqrt, bias=eps[:, :]
                                         ).then_inc(rms_z_done, 1)
                store_z(L0, None, 0, t, 1, lambda h: zh[:, :, item + h * DK:item + (h + 1) * DK])
                split_some(L0, None, 0, LEAD + t * CPT + 4, CPT - 4)
            with act.Fori(1, LN) as i:
                for t in range(2):
                    split_some(L0, i, LP, LEAD + t * CPT, 4)
                    store_z(L0, i, LP, t, 1, two_heads(i, GV - TILE, t))
                    split_some(L0, i, LP, LEAD + t * CPT + 4, CPT - 4)
            act.wait_ge(decay_sum, 1)
            nc.scalar.activation(decay[:, :, :], bank[0][:, 0:HEADS * 4].rearrange("p (n c) -> p n c", c=4),
                                 ACT.Exp, scale=1.0 / GATE_NORM).then_inc(decay_done, 1)

            with act.Fori(0, GN) as n:
                own.enter(n, ACT_HEAD_STEPS)

                def gla_decays():
                    act.wait_ge(g_sums, n + 1)
                    nc.scalar.activation(qd[:, :, :], bank[3][:, 0:2 * DK], ACT.Exp, scale=1.0 / GATE_NORM)
                    nc.scalar.activation(kd[:, :, :], bank[3][:, 0:2 * DK], ACT.Exp, scale=-1.0 / GATE_NORM)
                    nc.scalar.activation(e_tail[:, :, :], bank[3][:, 2 * DK:4 * DK], ACT.Exp,
                                         scale=1.0 / GATE_NORM).then_inc(ge_ready, 1)

                def diff_q():
                    act.wait_ge(d_turned, n + 1)
                    nc.scalar.activation(q_t[:, :, :], bank[0][:, :], ACT.Copy,
                                         scale=gains[:, G_DQ:G_DQ + 1]).then_inc(dqt_ready, 1)

                def gla_qk():
                    act.wait_ge(g_turned, n + 1)
                    nc.scalar.activation(g_t[:, :, :], bank[2][:, :], ACT.Copy).then_inc(gt_ready, 1)

                def gla_silu():
                    nc.scalar.activation(sg[:, :, :], zh[:, n, GG:GG + 2 * DH], ACT.Exp, scale=-1.0
                                         ).then_inc(gg_exp, 1)

                def diff_exp():
                    act.wait_ge(dmax_ready, n + 1)
                    for k, (b, at, src, w) in enumerate(((0, 0, 0, 2 * P), (0, 2 * P, 2 * P, 2 * P),
                                                         (1, 4 * P, 0, P), (1, 5 * P, P, P))):
                        a = nc.scalar.activation(prob[:, at:at + w], bank[b][:, src:src + w], ACT.Exp,
                                                 scale=DK ** -0.5, bias=nmax[:, k:k + 1],
                                                 accum_out=psum_exp[:, k:k + 1])
                    a.then_inc(dp_ready, 1)

                def gla_copy():
                    act.wait_ge(g_att, n + 1)
                    scores = bank[2][:, 0:2 * P].rearrange("p (h t) -> p h t", t=P)
                    for c in range(2):
                        r = slice(c * CHUNK, (c + 1) * CHUNK)
                        a = nc.scalar.activation(att[r, :, r], scores[r, :, r], ACT.Copy)
                    a.then_inc(ga_copied, 1)

                def diff_weights():
                    act.wait_ge(dp_turned, n + 1)
                    nc.scalar.activation(prob_t[:, 0:3 * P], bank[0][:, 0:3 * P], ACT.Copy).then_inc(dpt_ready, 1)

                def mem_q():
                    act.wait_ge(m_turned, n + 1)
                    for j in range(2):
                        a = nc.scalar.activation(q_t[:, j, :], bank[1][:, j * 2 * P:(j + 1) * 2 * P], ACT.Copy,
                                                 scale=gains[:, G_MQ + j:G_MQ + j + 1])
                    a.then_inc(mqt_ready, 1)

                def mem_exp():
                    act.wait_ge(mmax_ready, n + 1)
                    for h in range(HALVES):
                        r = slice(h * 2 * P, (h + 1) * 2 * P)
                        a = nc.scalar.activation(prob[:, r], bank[1][:, r], ACT.Exp, scale=DH ** -0.5,
                                                 bias=nmax[:, 4 + h:5 + h], accum_out=psum_exp[:, 4 + h:5 + h])
                    a.then_inc(mp_ready, 1)

                def output_rms():
                    act.wait_ge(g_out, n + 1)
                    for h in range(HALVES):
                        nc.scalar.activation(g_t[:, h, :], bank[2][:, h * DH:(h + 1) * DH], ACT.Square,
                                             accum_out=ssq_o[:, 2 + h:3 + h])
                    act.wait_ge(d_out, n + 1)
                    for h in range(HALVES):
                        a = nc.scalar.activation(kn[:, h, :], bank[0][:, h * DH:(h + 1) * DH], ACT.Square,
                                                 accum_out=ssq_o[:, h:h + 1])
                    own.step(a)
                    nc.scalar.activation(rms_o[:, :], ssq_o[:, :], ACT.Sqrt, scale=1.0 / DH, bias=eps[:, :]
                                         ).then_inc(go_rms, 1)

                def mem_weights():
                    act.wait_ge(mp_turned, n + 1)
                    nc.scalar.activation(prob_t[:, :], bank[1][:, :], ACT.Copy).then_inc(mpt_ready, 1)

                def y_hi(turned, b, place, done):
                    act.wait_ge(turned, n + 1)
                    nc.scalar.activation(yt[:, n, place:place + 2 * DH], bank[b][:, :], ACT.Copy).then_inc(done, 1)

                for s in range(GP):
                    split(G0, n, GP, LEAD + s)
                    if s == 0:
                        gla_decays()
                    if s == 1:
                        diff_q()
                    if s == 2:
                        gla_qk()
                        gla_silu()
                    if s == 3:
                        diff_exp()
                    if s == 4:
                        gla_copy()
                    if s == 5:
                        diff_weights()
                        mem_q()
                    if s == 7:
                        output_rms()
                        mem_exp()
                    if s == 9:
                        mem_weights()
                        y_hi(gy_turned, 2, GQ, gy_hi)
                        y_hi(dy_turned, 0, DQ, dy_hi)
                    if s == 13:
                        y_hi(my_turned, 1, MK, my_hi)
                own.leave(GN)

            def turned_hi(k, write):
                act.wait_ge(res_turned, k + 1)
                for b in range(2):
                    write(b).then_inc(res_hi, 1)

            with act.Fori(0, BN) as c:
                split_some(B0, c, BP, LEAD, 4)
                act.wait_ge(bias_used, 2 * GN + 2)
                for b in range(2):
                    a = nc.scalar.activation(gates[:, c + b * COLS, :, :], gates[:, c + b * COLS, :, :], ACT.Sigmoid)
                a.then_inc(sig_g01, 1)
                split_some(B0, c, BP, LEAD + 4, 4)
                act.wait_ge(g2_ready, c + 1)
                nc.scalar.activation(g2[:, :, :], g2[:, :, :], ACT.Sigmoid).then_inc(sig_g2, 1)
                split_some(B0, c, BP, LEAD + 8, BP - 8)
                turned_hi(c, lambda b: nc.scalar.activation(
                    gt_hi[:, bass.ds(c * 4 + 2 * b, 2), :], bank[b][:, :].rearrange("p (k t) -> p k t", k=2), ACT.Copy))

            for t in range(COLS):
                split_some(O0, None, 0, LEAD + t * CPT, 4)
                k = BN + t
                act.wait_ge(res_ready, k + 1)
                nc.scalar.activation(x1[:, :, t * TILE:(t + 1) * TILE], res[:, :, :], ACT.Copy)
                for h in range(HALVES):
                    a = nc.scalar.activation(sq1[:, h, :], res[:, h, :], ACT.Square,
                                             accum_out=ssq_x1[:, h, t:t + 1])
                a.then_inc(x1_squared, 1)
                if t == COLS - 1:
                    act.wait_ge(x1_sum, 1)
                    nc.scalar.activation(rms_x1[:, :], sum_x1[:, :], ACT.Sqrt, scale=1.0 / D, bias=eps[:, :]
                                         ).then_inc(x1_rms, 1)
                split_some(O0, None, 0, LEAD + t * CPT + 4, 4)
                act.wait_ge(res_turned, k + 1)
                for b in range(2):
                    for j in range(2):
                        kt = 4 * t + 2 * b + j
                        a = nc.scalar.activation(xt_hi[:, kt, :], bank[b][:, j * 2 * P:(j + 1) * 2 * P], ACT.Copy,
                                                 scale=gains[:, G_FFN + kt:G_FFN + kt + 1])
                    a.then_inc(res_hi, 1)
                if t < COLS - 1:
                    act.wait_ge(x1_squared, t + 1)

            act.wait_ge(x1_rstd, 1)
            with act.Fori(0, FN) as i:
                split_some(F0, i, FP, LEAD, 4)
                act.wait_ge(chunk_used, nth(F0, i, FP, CPT) + RING)
                act.wait_ge(res_ready, i + (BN + COLS))
                for h in range(HALVES):
                    a = nc.scalar.activation(g2[:, h, :], acc[0][:, h, :], ACT.Silu, scale=rstd_x1[:, h:h + 1])
                a.then_inc(acc_free[0], 1)
                split_some(F0, i, FP, LEAD + 4, 12)
                turned_hi(i + (BN + COLS), lambda b: nc.scalar.activation(
                    act_hi[:, bass.ds(i * 4 + 2 * b, 2), :], bank[b][:, :].rearrange("p (k t) -> p k t", k=2), ACT.Copy))

            def store(t):
                act.wait_ge(fin_ready, t + 1)
                act.dma_start(out_v[:, :, t * TILE:(t + 1) * TILE], fin[:, t, :, :]).then_inc(out_stored, 16)

            for t in range(COLS):
                u = LEAD + t * CPD
                last = t == COLS - 1
                split_some(D0, None, 0, u, CPD - LEAD if last else CPD - 4)
                if not last:
                    split_some(D0, None, 0, u + CPD - 4, 4)
                store(t)
            act.wait_ge(out_stored, 16 * COLS)

        @block.vector
        def _(dve):
            own = Tally(dve, dve_step)
            V = nc.vector
            dve.sem_inc(chunk_split, RING)
            dve.sem_inc(acc_free[0], 1)
            dve.sem_inc(acc_free[1], 1)
            dve.sem_inc(bias_used, 2)

            def f32(ap):
                return ap.bitcast(FP32)

            def split(base, i, per, u):
                s = u % RING
                dve.wait_ge(chunk_hi, nth(base, i, per, u) + 1)
                V.tensor_tensor(wlo[:, s, :, :], raw[:, s, :, :], f32(whi[:, s, :, :]), ALU.subtract
                                ).then_inc(chunk_split, 1)

            def split_some(base, i, per, u, count):
                for k in range(count):
                    split(base, i, per, u + k)

            def squares(tiles_before, i, t, item):
                dve.wait_ge(acc_free[t], nth(tiles_before, i, 1, 2))
                off = i * TILE + (MK + item * TILE)
                for h in range(HALVES):
                    z = zh[:, 2 * t:2 * t + 2, bass.ds(off + h * DH, DH)]
                    v = V.tensor_tensor(sq[:, h, :].rearrange("p (n c) -> p n c", n=2), z, z, ALU.mult)
                own.step(v)
                for h in range(HALVES):
                    v = V.reduce_sum(ssq_z[:, 2 * t:2 * t + 2, i + item, 2 * h:2 * h + 2],
                                     sq[:, h, :].rearrange("p (n j c) -> p n j c", n=2, c=DK), AX.X)
                own.step(v)

            def in_group(g):
                dve.wait_ge(in_hi, g + 1)
                hi, lo, g0 = (gt_hi, gt_lo, G_MEM) if g < KT // 2 else (xt_hi, xt_lo, G_MIX)
                for j in range(2):
                    kt = 2 * (g % (KT // 2)) + j
                    v = V.scalar_tensor_tensor(lo[:, kt, :], bank[g % 4][:, j * 2 * P:(j + 1) * 2 * P],
                                               gains[:, g0 + kt:g0 + kt + 1], f32(hi[:, kt, :]),
                                               ALU.mult, ALU.subtract)
                v.then_inc(in_lo, 1)

            V.memset(lam_dot[:, :], 0.0)
            dve.wait_ge(gains_turned, 1)
            own.step(V.tensor_copy(gains[:, 0:NG1], bank[3][:, 0:NG1]))
            dve.sem_inc(gains_ready, 1)
            in_group(0)
            in_group(1)
            split(M0, None, 0, 0)
            in_group(2)
            in_group(3)
            split(M0, None, 0, 1)
            for u in range(2, MN * MP + LEAD):
                split(M0, None, 0, u)
                if u + 2 < 2 * KT // 2:
                    in_group(u + 2)
                if u in (10, 16):
                    k = (u - 10) // 6
                    dve.wait_ge(rms_in_done, k + 1)
                    V.reciprocal(rstd_in[:, k, :], rms_in[:, k, :]).then_inc(rstd_in_done, 1)
                if u == 13:
                    dve.wait_ge(wa_hi_done, 1)
                    V.tensor_tensor(wa_lo[:, :, :], wa_raw[:, :, :], f32(wa_hi[:, :, :]), ALU.subtract
                                    ).then_inc(wa_split, 1)
                if u == LOW_AT + 10:
                    dve.wait_ge(params_landed, 16 * PARAMS)
                    prod = sq[:, 0, 0:2 * DK].rearrange("p (a b) -> p a b", a=2)
                    own.step(V.tensor_tensor(prod, lam_v[:, 0:4:2, :], lam_v[:, 1:4:2, :], ALU.mult))
                    V.reduce_sum(lam_dot[:, :], prod, AX.X).then_inc(lam_dot_done, 1)
                    own.step(V.tensor_scalar(sub_gain[:, :], sub_gain[:, :], 1.0 - LAM_INIT, None, ALU.mult))
                if u == LOW_AT + 11:
                    dve.wait_ge(rstd_in_done, 2)
                    dve.wait_ge(lgate_done, 1)
                    for h in range(HALVES):
                        v = V.scalar_tensor_tensor(log_a[:, h, :], bank[2 + h][:, :], rstd_in[:, 1, h:h + 1],
                                                   alpha_b[:, :], ALU.mult, ALU.add)
                    v.then_inc(larg_done, 1)
                    dve.wait_ge(gains_turned, 2)
                    V.tensor_copy(gains[:, NG1:NG], bank[1][:, 0:NG - NG1]).then_inc(gains_ready, 1)
                if u == LOW_AT + 17:
                    dve.wait_ge(lln_done, 1)
                    V.scalar_tensor_tensor(log_a[:, :, :], log_a[:, :, :], 0.0, labs[:, :, :],
                                           ALU.min, ALU.subtract).then_inc(log_a_done, 1)
                if u >= LEAD and (u - LEAD) % CPT == 7:
                    t = (u - LEAD) // CPT
                    squares(M_T, t // 2, t % 2, 0)
            with dve.Fori(0, IN) as i:
                own.enter(i, 4)
                for t in range(2):
                    split_some(I0, i, IP, LEAD + t * CPT, CPT)
                    squares(I_T, i, t, 2)
                own.leave(IN)

            V.tensor_scalar(ms_z[:, :, 0:8].rearrange("p n (a b) -> p n a b", a=2), ssq_z[:, :, 2:4, :],
                            1.0 / DK, None, ALU.mult)
            for place, item in ((8, 5), (10, 0)):
                v = V.tensor_tensor(ms_z[:, :, place:place + 2], ssq_z[:, :, item, 0:4:2],
                                    ssq_z[:, :, item, 1:4:2], ALU.add)
            own.step(v)
            V.tensor_scalar(ms_z[:, :, 8:12], ms_z[:, :, 8:12], 1.0 / DH, None, ALU.mult).then_inc(ms_z_done, 1)
            dve.wait_ge(log_a_done, 1)
            V.memset(k_tail[CHUNK:P, 0, :, :], 0.0)
            V.memset(k_tail[0:CHUNK, 1, :, :], 0.0)
            V.memset(att[0:CHUNK, :, CHUNK:P], 0.0)
            own.step(V.memset(att[CHUNK:P, :, 0:CHUNK], 0.0))
            dve.wait_ge(lam_exp_done, 1)
            V.tensor_scalar(neg_lam[:, :], lam_exp[:, 1:2], lam_exp[:, 0:1], -LAM_INIT, ALU.subtract, ALU.add)
            split_some(L0, None, 0, LEAD, 6)
            dve.wait_ge(rms_z_done, 1)
            own.step(V.reciprocal(rstd_z[:, :, :], rstd_z[:, :, :]))
            split_some(L0, None, 0, LEAD + 6, LP - 6)
            with dve.Fori(1, LN) as i:
                split_some(L0, i, LP, LEAD, LP)
            dve.wait_ge(decay_done, 1)
            dve.wait_ge(acc_free[1], L_T + LN + 1)

            with dve.Fori(0, GN) as n:
                own.enter(n, DVE_HEAD_STEPS)

                def store_gates(t):
                    dve.wait_ge(chunk_used, nth(G0, n, GP, (t + 1) * CPT) + RING)
                    dve.wait_ge(bias_landed[t], 16 * (n + 1))
                    for h in range(HALVES):
                        v = V.scalar_tensor_tensor(gates[:, n * 2 + t, h, :], acc[t][:, h, :],
                                                   rstd_in[:, 1, h:h + 1], bias[:, t, :], ALU.mult, ALU.add)
                    own.step(v)
                    dve.sem_inc(acc_free[t], 1)
                    dve.sem_inc(bias_used, 1)

                def normalise(q, k, at, width, done):
                    m = DH // width
                    for dst, src, r in ((qn, q, at), (kn, k, at + HALVES * m)):
                        z = zh[:, n, src:src + HALVES * DH].rearrange("p (g c) -> p g c", c=width)
                        s = rstd_z[:, n, r:r + HALVES * m].unsqueeze(2).to_broadcast([P, HALVES * m, width])
                        v = V.tensor_tensor(dst[:, :, :].rearrange("p h (m c) -> p (h m) c", m=m), z, s, ALU.mult)
                    v.then_inc(done, 1)

                def gla_decayed():
                    dve.wait_ge(ge_ready, n + 1)
                    zq, zk = zh[:, n, GQ:GQ + 2 * DK], zh[:, n, GK:GK + 2 * DK]
                    flat = lambda a: a.rearrange("p h c -> p (h c)")
                    V.scalar_tensor_tensor(flat(qd[:, :, :]), zq, DK ** -0.5, flat(qd[:, :, :]), ALU.mult, ALU.mult)
                    V.tensor_tensor(flat(kd[:, :, :]), zk, flat(kd[:, :, :]), ALU.mult)
                    V.tensor_copy(decay_h[:, :], decay[:, n, :])
                    for c in range(2):
                        r = slice(c * CHUNK, (c + 1) * CHUNK)
                        v = V.tensor_tensor(flat(k_tail[r, c, :, :]), zk[r, :], flat(e_tail[r, :, :]), ALU.mult)
                    own.step(v)
                    dve.sem_inc(gd_ready, 1)

                def diff_k():
                    dve.wait_ge(d_turned, n + 1)
                    V.tensor_scalar(k_t[:, :, :], bank[1][:, :].rearrange("p (j t) -> p j t", j=2),
                                    gains[:, G_DK:G_DK + 1], None, ALU.mult).then_inc(dkt_ready, 1)

                def gla_states():
                    dve.wait_ge(g_inc, n + 1)
                    own.step(V.tensor_copy(state[:, 0, :], bank[3][:, 0:DH]))
                    own.step(V.scalar_tensor_tensor(state[:, 1, :], state[:, 0, :], decay_h[:, 1:2],
                                                    bank[3][:, DH:2 * DH], ALU.mult, ALU.add))

                def gla_last_state():
                    dve.wait_ge(g_att, n + 1)
                    dve.wait_ge(ga_copied, n + 1)
                    V.scalar_tensor_tensor(state[:, 2, :], state[:, 1, :], decay_h[:, 2:3],
                                           bank[2][:, DH:2 * DH], ALU.mult, ALU.add).then_inc(gs_ready, 1)

                def diff_max():
                    dve.wait_ge(d_scores, n + 1)
                    s1 = bank[0][:, :].rearrange("p (j k) -> p j k", j=2)
                    s0 = bank[1][:, 0:2 * P].rearrange("p (j k) -> p j k", j=2)
                    V.memset(s1[0:CHUNK, :, 3 * CHUNK:4 * CHUNK], NEG)
                    own.step(V.memset(s0[0:CHUNK, :, CHUNK:2 * CHUNK], NEG))
                    V.reduce_max(rmax[:, 0:2], s1, AX.X)
                    own.step(V.reduce_max(rmax[:, 2:4], s0, AX.X))
                    V.tensor_scalar(nmax[:, 0:4], rmax[:, 0:4], -DK ** -0.5, None, ALU.mult).then_inc(dmax_ready, 1)

                def diff_weights():
                    dve.wait_ge(dp_ready, n + 1)
                    own.step(V.reciprocal(rsum[:, 0:4], psum_exp[:, 0:4]))
                    own.step(V.tensor_scalar(lam_r[:, :], rsum[:, 1:4:2], neg_lam[:, :], None, ALU.mult))
                    V.tensor_scalar(prob[:, 2 * P:4 * P], prob[:, 2 * P:4 * P], lam_r[:, 0:1], None, ALU.mult)
                    own.step(V.tensor_scalar(prob[:, 5 * P:6 * P], prob[:, 5 * P:6 * P], lam_r[:, 1:2], None, ALU.mult))
                    V.scalar_tensor_tensor(prob[:, 0:2 * P], prob[:, 0:2 * P], rsum[:, 0:1],
                                           prob[:, 2 * P:4 * P], ALU.mult, ALU.add)
                    V.scalar_tensor_tensor(prob[:, 4 * P:5 * P], prob[:, 4 * P:5 * P], rsum[:, 2:3],
                                           prob[:, 5 * P:6 * P], ALU.mult, ALU.add).then_inc(da_ready, 1)

                def mem_k():
                    dve.wait_ge(m_turned, n + 1)
                    for j in range(2):
                        v = V.tensor_scalar(k_t[:, j, :], bank[3][:, j * 2 * P:(j + 1) * 2 * P],
                                            gains[:, G_MK + j:G_MK + j + 1], None, ALU.mult)
                    v.then_inc(mkt_ready, 1)

                def mem_max():
                    dve.wait_ge(m_scores, n + 1)
                    own.step(V.reduce_max(rmax[:, 4:6], bank[1][:, :].rearrange("p (h k) -> p h k", h=2), AX.X))
                    V.tensor_scalar(nmax[:, 4:6], rmax[:, 4:6], -DH ** -0.5, None, ALU.mult).then_inc(mmax_ready, 1)

                def gla_silu():
                    dve.wait_ge(gg_exp, n + 1)
                    own.step(V.tensor_scalar(sg[:, :, :], sg[:, :, :], 1.0, None, ALU.add))
                    own.step(V.reciprocal(sg[:, :, :], sg[:, :, :]))
                    flat = sg[:, :, :].rearrange("p h c -> p (h c)")
                    own.step(V.tensor_tensor(flat, flat, zh[:, n, GG:GG + 2 * DH], ALU.mult))
                    own.step(V.tensor_tensor(sg[:, :, :], sg[:, :, :],
                                             gla_gain[:, :].unsqueeze(1).to_broadcast([P, HALVES, DH]), ALU.mult))

                def outputs():
                    dve.wait_ge(go_rms, n + 1)
                    own.step(V.reciprocal(rstd_o[:, :], rms_o[:, :]))
                    for h in range(HALVES):
                        v = V.scalar_tensor_tensor(sg[:, h, :], bank[2][:, h * DH:(h + 1) * DH],
                                                   rstd_o[:, 2 + h:3 + h], sg[:, h, :], ALU.mult, ALU.mult)
                    v.then_inc(gy_ready, 1)
                    for h in range(HALVES):
                        v = V.scalar_tensor_tensor(kn[:, h, :], bank[0][:, h * DH:(h + 1) * DH],
                                                   rstd_o[:, h:h + 1], sub_gain[:, :], ALU.mult, ALU.mult)
                    v.then_inc(dy_ready, 1)

                def mem_output():
                    dve.wait_ge(m_out, n + 1)
                    own.step(V.reciprocal(rsum[:, 4:6], psum_exp[:, 4:6]))
                    for h in range(HALVES):
                        v = V.tensor_scalar(qn[:, h, :], bank[1][:, h * DH:(h + 1) * DH], rsum[:, 4 + h:5 + h],
                                            None, ALU.mult)
                    v.then_inc(my_ready, 1)

                def y_lo(hi_done, b, place, done):
                    dve.wait_ge(hi_done, n + 1)
                    V.tensor_tensor(yt[:, n, place + 2 * DH:place + 4 * DH], bank[b][:, :],
                                    f32(yt[:, n, place:place + 2 * DH]), ALU.subtract).then_inc(done, 1)

                for s in range(GP):
                    split(G0, n, GP, LEAD + s)
                    if s == 0:
                        normalise(DQ, DKO, 0, DK, dn_ready)
                        gla_decayed()
                    if s == 1:
                        diff_k()
                        normalise(MQ, MK, 8, DH, mn_ready)
                    if s == 2:
                        gla_states()
                    if s == 3:
                        diff_max()
                        diff_weights()
                        store_gates(0)
                    if s == 4:
                        gla_last_state()
                    if s == 5:
                        mem_k()
                        gla_silu()
                    if s == 7:
                        outputs()
                        mem_max()
                    if s == 9:
                        y_lo(gy_hi, 2, GQ, gy_lo)
                        y_lo(dy_hi, 0, DQ, dy_lo)
                    if s == 10:
                        mem_output()
                    if s == 11:
                        store_gates(1)
                    if s == 13:
                        y_lo(my_hi, 1, MK, my_lo)
                own.leave(GN)

            def turned_lo(k, write):
                for b in range(2):
                    dve.wait_ge(res_hi, k * 2 + (b + 1))
                    write(b).then_inc(res_lo, 1)

            def lo_of(lo, hi, first, b):
                r = bass.ds(first + 2 * b, 2)
                return V.tensor_tensor(lo[:, r, :], bank[b][:, :].rearrange("p (k t) -> p k t", k=2),
                                       f32(hi[:, r, :]), ALU.subtract)

            with dve.Fori(0, BN) as c:
                own.enter(c, 3)
                split_some(B0, c, BP, LEAD, 4)
                dve.wait_ge(chunk_used, nth(B0, c, BP, CPT) + RING)
                dve.wait_ge(bias_landed[0], 16 * (c + (GN + 1)))
                for h in range(HALVES):
                    v = V.scalar_tensor_tensor(g2[:, h, :], acc[0][:, h, :], rstd_in[:, 1, h:h + 1],
                                               bias[:, 0, :], ALU.mult, ALU.add)
                own.step(v)
                dve.sem_inc(g2_ready, 1)
                dve.sem_inc(acc_free[0], 1)
                dve.sem_inc(bias_used, 1)
                for b in range(3):
                    split_some(B0, c, BP, LEAD + 4 * (b + 1), 4)
                    slot = (b + 1) % 2
                    dve.wait_ge(chunk_used, nth(B0, c, BP, CPT + (b + 1) * CPB) + RING)
                    dve.wait_ge((sig_g01, sig_g01, sig_g2)[b], c + 1)
                    g = (gates[:, c, :, :], gates[:, c + COLS, :, :], g2[:, :, :])[b]
                    v = V.tensor_tensor(g, g, acc[slot][:, :, :], ALU.mult)
                    v.then_inc(acc_free[slot], 1)
                    if b > 0:
                        dve.wait_ge(acc_free[slot], nth(B_T, c, 2, 3))
                        sums = gates[:, c, :, :]
                        if b == 1:
                            own.step(V.tensor_tensor(sums, sums, gates[:, c + COLS, :, :], ALU.add))
                        else:
                            own.step(V.tensor_tensor(res[:, :, :], sums, g2[:, :, :], ALU.add))
                            dve.sem_inc(res_ready, 1)
                split_some(B0, c, BP, LEAD + 16, 4)
                turned_lo(c, lambda b: lo_of(gt_lo, gt_hi, c * 4, b))
                own.leave(BN)

            for t in range(COLS):
                split_some(O0, None, 0, LEAD + t * CPT, 4)
                k = BN + t
                s = t % 2
                dve.wait_ge(chunk_used, O0 + (t + 1) * CPT + RING)
                dve.wait_ge(xin_landed[s], 16 * (t // 2 + 1))
                if t > 0:
                    dve.wait_ge(x1_squared, t)
                V.tensor_tensor(res[:, :, :], acc[s][:, :, :], xin[:, s, :, :], ALU.add).then_inc(acc_free[s], 1)
                dve.wait_ge(acc_free[s], O_T + t // 2 + 2)
                dve.sem_inc(res_ready, 1)
                if t == COLS - 1:
                    dve.wait_ge(x1_squared, COLS)
                    V.reduce_sum(sum_x1[:, :], ssq_x1[:, :, :], AX.X).then_inc(x1_sum, 1)
                split_some(O0, None, 0, LEAD + t * CPT + 4, 4)
                for b in range(2):
                    dve.wait_ge(res_hi, 2 * k + b + 1)
                    for j in range(2):
                        kt = 4 * t + 2 * b + j
                        v = V.scalar_tensor_tensor(xt_lo[:, kt, :], bank[b][:, j * 2 * P:(j + 1) * 2 * P],
                                                   gains[:, G_FFN + kt:G_FFN + kt + 1], f32(xt_hi[:, kt, :]),
                                                   ALU.mult, ALU.subtract)
                    v.then_inc(res_lo, 1)
            dve.wait_ge(x1_rms, 1)
            V.reciprocal(rstd_x1[:, :], rms_x1[:, :]).then_inc(x1_rstd, 1)
            dve.wait_ge(x1_rstd, 1)
            with dve.Fori(0, FN) as i:
                split_some(F0, i, FP, LEAD, 12)
                dve.wait_ge(chunk_used, nth(F0, i, FP, FP) + RING)
                dve.wait_ge(acc_free[0], i + (F_T + 2))
                own.enter(i, 1)
                for h in range(HALVES):
                    v = V.scalar_tensor_tensor(res[:, h, :], acc[1][:, h, :], rstd_x1[:, h:h + 1], g2[:, h, :],
                                               ALU.mult, ALU.mult)
                own.step(v)
                dve.sem_inc(acc_free[1], 1)
                dve.sem_inc(res_ready, 1)
                split_some(F0, i, FP, LEAD + 12, 4)
                turned_lo(i + (BN + COLS), lambda b: lo_of(act_lo, act_hi, i * 4, b))
                own.leave(FN)
            for t in range(COLS):
                u = LEAD + t * CPD
                last = t == COLS - 1
                split_some(D0, None, 0, u, CPD - LEAD if last else CPD - 4)
                dve.wait_ge(chunk_used, D0 + (t + 1) * CPD + RING)
                V.tensor_tensor(fin[:, t, :, :], acc[t % 2][:, :, :], x1[:, :, t * TILE:(t + 1) * TILE], ALU.add
                                ).then_inc(acc_free[t % 2], 1)
                dve.wait_ge(acc_free[t % 2], D_T + t // 2 + 2)
                dve.sem_inc(fin_ready, 1)
                if not last:
                    split_some(D0, None, 0, u + CPD - 4, 4)

        @block.gpsimd
        def _(pool):
            own = Tally(pool, pool_step)
            G = nc.gpsimd
            G.memset(eps[:, :], EPS).then_inc(eps_ready, 1)
            own.step(G.memset(ident[:, :], 0.0))
            G.affine_select(out=ident[:, :], in_=ident[:, :], compare_op=ALU.not_equal, fill=1.0, base=0,
                            pattern=[[-1, P]], channel_multiplier=1).then_inc(ident_ready, 1)
            G.memset(chunk_of[:, :], 0.0)
            G.memset(upto[:, :], 0.0)
            own.step(G.memset(after[:, :], 0.0))
            for c in range(2):
                r = slice(c * CHUNK, (c + 1) * CHUNK)
                G.memset(chunk_of[r, c:c + 1], 1.0)
                G.memset(upto[r, r], 1.0)
                m = G.memset(after[r, r], 1.0)
            own.step(m)
            G.affine_select(out=upto[:, :], in_=upto[:, :], compare_op=ALU.is_ge, fill=0.0, base=0,
                            pattern=[[1, P]], channel_multiplier=-1)
            G.affine_select(out=after[:, :], in_=after[:, :], compare_op=ALU.is_gt, fill=0.0, base=0,
                            pattern=[[-1, P]], channel_multiplier=1).then_inc(consts_ready, 1)
            with pool.Fori(0, GN) as n:
                pool.wait_ge(ga_copied, n + 1)
                pool.sem_inc(passed_pool, 1)
                for c in range(2):
                    r = slice(c * CHUNK, (c + 1) * CHUNK)
                    m = G.affine_select(out=att[r, :, r], in_=att[r, :, r], compare_op=ALU.is_ge, fill=0.0,
                                        base=0, pattern=[[0, HALVES], [1, CHUNK]], channel_multiplier=-1)
                m.then_inc(ga_ready, 1)


_INS = ["x", "mem", "norm_mix_g", "norm_mem_g", "w_in", "gla_w_alpha_up", "gla_b_alpha", "gla_norm_g",
        "diff_q_norm_g", "diff_k_norm_g", "diff_lambda_q1", "diff_lambda_k1", "diff_lambda_q2",
        "diff_lambda_k2", "diff_subln_g", "mem_q_norm_g", "mem_k_norm_g", "w_mem_kv", "w_branch",
        "w_gate", "b_gate", "w_out", "norm_ffn_g", "w_ffn_in", "w_ffn_down"]


def kernel(**inputs):
    import numpy as np
    import concourse.bacc as bacc
    from concourse.bass_utils import run_bass_kernel_spmd

    nc = bacc.Bacc("TRN2", target_bir_lowering=False, num_devices=1, dynamic_dma_scratch_size=1024)
    arrays, args = {}, []
    for name in _INS:
        a = np.ascontiguousarray(inputs[name])
        arrays[f"in_{name}"] = a
        args.append(nc.dram_tensor(f"in_{name}", a.shape, mybir.dt.from_np(a.dtype), kind="ExternalInput").ap())
    shape = inputs["x"].shape
    out = nc.dram_tensor("out", shape, FP32, kind="ExternalOutput").ap()
    hybrid_layer(nc, *args, out)
    result = run_bass_kernel_spmd(nc, [arrays], core_ids=[0])
    return result.results[0]["out"]
```

```python
import math
from contextlib import ExitStack

import concourse.bass as bass
from concourse import mybir

FP32 = mybir.dt.float32
FP32R = mybir.dt.float32r
ACT = mybir.ActivationFunctionType
ALU = mybir.AluOpType
AX = mybir.AxisListType

P = 128
HALVES = 2
TILE = 512
KPC = 2
RING = 4
IN_AHEAD = 3
LOW_AT = 17
LEAD = 8
CHUNK = 64
HEADS = 4
DH = 256
DK = 128
RANK = 16
EPS = 1e-6
GATE_NORM = 16.0
NEG = -1e30
LAM_INIT = 0.8 - 0.6 * math.exp(0.0)
ACT_HEAD_STEPS = 1
DVE_HEAD_STEPS = 17
QK_BACK_AT = (4, 8, 11, 15)


class Tally:

    def __init__(self, engine, sem):
        self.engine, self.sem, self.base, self.n, self.loop, self.per = engine, sem, 0, 0, None, 0

    def enter(self, loop, per):
        self.base, self.n, self.loop, self.per = self.base + self.n, 0, loop, per

    def leave(self, times):
        assert self.n == self.per, f"{self.n} steps in a loop's body, {self.per} were stated"
        self.base, self.n, self.loop = self.base + self.per * times, 0, None

    def now(self):
        if self.loop is None:
            return self.base + self.n
        return self.loop * self.per + (self.base + self.n)

    def step(self, instruction):
        instruction.then_inc(self.sem, 1)
        self.n += 1
        self.engine.wait_ge(self.sem, self.now())


def hybrid_layer(nc, x, mem, norm_mix_g, norm_mem_g, w_in, gla_w_alpha_up, gla_b_alpha, gla_norm_g,
                 diff_q_norm_g, diff_k_norm_g, diff_lambda_q1, diff_lambda_k1, diff_lambda_q2,
                 diff_lambda_k2, diff_subln_g, mem_q_norm_g, mem_k_norm_g, w_mem_kv, w_branch,
                 w_gate, b_gate, w_out, norm_ffn_g, w_ffn_in, w_ffn_down, out):
    D = x.shape[2]
    DFF = w_ffn_down.shape[1]
    KT = D // P
    KTB = HEADS * DH // P
    KTF = DFF // P
    COLS = D // TILE
    CPT = KT // KPC
    CPB = KTB // KPC
    CPD = KTF // KPC
    FT = DFF // TILE

    M0, MN, MP = 0, 2, 2 * CPT
    I0, IN, IP = M0 + MN * MP, 4, 2 * CPT
    L0, LN, LP = I0 + IN * IP, 3, 2 * CPT
    G0, GN, GP = L0 + LN * LP, HEADS, 2 * CPT
    B0, BN, BP = G0 + GN * GP, COLS, CPT + 3 * CPB
    O0, ON, OP = B0 + BN * BP, 2, 2 * CPT
    F0, FN, FP = O0 + ON * OP, FT, 2 * CPT
    D0, DN, DP = F0 + FN * FP, 2, 2 * CPD
    END = D0 + DN * DP
    PARAMS = 13
    M_T, I_T, L_T, G_T = 0, MN, MN + IN, MN + IN + LN
    B_T = G_T + GN
    O_T = B_T + 2 * BN
    F_T = O_T + ON
    D_T = F_T + FN

    GLA_COLS = 2 * HEADS * DK + 2 * HEADS * DH
    DIFF_COL = GLA_COLS + RANK

    def rows(w):
        return w.rearrange("o (k p) n -> (o p) k n", p=P)

    w_in_v, w_kv_v, w_gate_v, w_out_v = rows(w_in), rows(w_mem_kv), rows(w_gate), rows(w_out)
    w_fin_v, w_down_v = rows(w_ffn_in), rows(w_ffn_down)
    w_br_v = w_branch.rearrange("o i (k p) n -> (o p) i k n", p=P)
    x_v = x.rearrange("o (h p) d -> (o p) h d", p=P)
    mem_v = mem.rearrange("o (h p) d -> (o p) h d", p=P)
    out_v = out.rearrange("o (h p) d -> (o p) h d", p=P)

    ctx = ExitStack()
    with ctx:
        SLOT = KPC * TILE * 4
        CONST = 1152
        BIAS = CONST + 5888
        RAW = BIAS + 2 * TILE * 4
        XT = RAW + 3 * RING * SLOT
        ATT = XT + 2 * KT * HALVES * P * 4
        ZH = ATT + 28672
        ZHEAD = 9 * TILE
        GATE = ZH + HEADS * ZHEAD * 4
        assert GATE + 2 * COLS * HALVES * TILE * 4 <= nc.sbuf_usable_end - 24
        used = [CONST]

        def sb(name, shape, offset, dt=FP32):
            return nc.alloc_sbuf_tensor_at(name, shape, dt, offset=offset)

        def const(name, shape):
            at = used[0]
            n = 4 * math.prod(shape[1:])
            used[0] = at + -(-n // 32) * 32
            assert used[0] <= BIAS
            return sb(name, shape, at)

        ident = const("ident", [P, P])
        upto = const("upto", [P, P])
        after = const("after", [P, P])
        chunk_of = const("chunk_of", [P, 2])
        G_MEM, G_MIX, G_FFN, G_DQ, G_DK, G_MQ, G_MK = 0, KT, 2 * KT, 3 * KT, 3 * KT + 1, 3 * KT + 2, 3 * KT + 4
        NG = 3 * KT + 6
        NG1 = 2 * KT
        gains = const("gains", [P, NG])
        gla_gain = const("gla_gain", [P, DH])
        sub_gain = const("sub_gain", [P, DH])
        eps = const("eps", [P, 1])
        lam_dot = const("lam_dot", [P, 2])
        lam_exp = const("lam_exp", [P, 2])
        neg_lam = const("neg_lam", [P, 1])
        ssq_in = const("ssq_in", [P, 2, HALVES])
        rms_in = const("rms_in", [P, 2, HALVES])
        rstd_in = const("rstd_in", [P, 2, HALVES])
        ssq_x1 = const("ssq_x1", [P, HALVES, COLS])
        sum_x1 = const("sum_x1", [P, HALVES])
        rms_x1 = const("rms_x1", [P, HALVES])
        rstd_x1 = const("rstd_x1", [P, HALVES])
        ssq_z = const("ssq_z", [P, HEADS, 6, HALVES * 2])
        ms_z = const("ms_z", [P, HEADS, 12])
        rstd_z = const("rstd_z", [P, HEADS, 12])
        decay = const("decay", [P, HEADS, 4])
        decay_h = const("decay_h", [P, 4])
        rmax = const("rmax", [P, 6])
        nmax = const("nmax", [P, 6])
        psum_exp = const("psum_exp", [P, 6])
        rsum = const("rsum", [P, 6])
        lam_r = const("lam_r", [P, 2])
        ssq_o = const("ssq_o", [P, 4])
        rms_o = const("rms_o", [P, 4])
        rstd_o = const("rstd_o", [P, 4])

        bias = sb("bias", [P, 2, TILE], BIAS)
        raw = sb("raw", [P, RING, KPC, TILE], RAW)
        whi = sb("whi", [P, RING, KPC, TILE], RAW + RING * SLOT, FP32R)
        wlo = sb("wlo", [P, RING, KPC, TILE], RAW + 2 * RING * SLOT, FP32R)
        xt_hi = sb("xt_hi", [P, KT, HALVES * P], XT, FP32R)
        xt_lo = sb("xt_lo", [P, KT, HALVES * P], XT + KT * HALVES * P * 4, FP32R)
        gt_lo = sb("gt_lo", [P, KT, HALVES * P], GATE, FP32R)
        gt_hi = sb("gt_hi", [P, KT, HALVES * P], GATE + KT * HALVES * P * 4, FP32R)
        gates = sb("gates", [P, 2 * COLS, HALVES, TILE], GATE)
        zh = sb("zh", [P, HEADS, ZHEAD], ZH)
        yt = sb("yt", [P, HEADS, ZHEAD], ZH, FP32R)
        DQ, DKO, DV, MQ, MK, MV, GQ, GK, GV, GG = 0, 512, 1024, 1536, 2048, 2560, 3072, 3328, 3584, 4096
        Y_OF = {0: GQ, 1: DQ, 2: MQ}
        x_raw = zh[:, 0:HALVES, DQ:DQ + D]
        mem_raw = zh[:, HALVES:2 * HALVES, DQ:DQ + D]
        junk = sb("junk", [P, D], ATT + 13312)
        sq = sb("sq", [P, HALVES, TILE], ATT)
        lam_v = sb("lam_v", [P, 4, DK], ATT + 4096)
        alpha_up = sb("alpha_up", [RANK, HEADS * DK], ATT + 6144)
        low_t = sb("low_t", [RANK, HALVES * P], ATT + 8192)
        wa_raw = sb("wa_raw", [P, KT, RANK], ATT + 9216)
        wa_hi = sb("wa_hi", [P, KT, RANK], ATT + 10240, FP32R)
        wa_lo = sb("wa_lo", [P, KT, RANK], ATT + 11264, FP32R)
        gain_rows = sb("gain_rows", [NG1, P], ATT + 12288)
        gain_rows2 = sb("gain_rows2", [NG - NG1, P], ATT + 12800)
        alpha_b = sb("alpha_b", [P, HEADS * DK], ATT + 21504)
        labs = sb("labs", [P, HALVES, HEADS * DK], ATT + 13312)
        lexp = sb("lexp", [P, HALVES, HEADS * DK], ATT + 17408)
        qn = sb("qn", [P, HALVES, DH], ATT)
        kn = sb("kn", [P, HALVES, DH], ATT + 2048)
        dq_t = sb("dq_t", [P, HALVES, 2, P], ATT + 4096)
        mq_t = sb("mq_t", [P, HALVES, 2, P], ATT + 6144)
        turned = sb("turned", [P, 2, 4 * DH // P, P], ATT)
        prob = sb("prob", [P, 768], ATT + 8192)
        prob_t = sb("prob_t", [P, TILE], ATT + 11264)
        qd = sb("qd", [P, HALVES, DK], ATT + 13312)
        kd = sb("kd", [P, HALVES, DK], ATT + 14336)
        sg = sb("sg", [P, HALVES, DH], ATT + 13312)
        k_tail = sb("k_tail", [P, 2, HALVES, DK], ATT + 15360)
        e_tail = sb("e_tail", [P, HALVES, DK], ATT + 17408)
        g_t = sb("g_t", [P, 2, HALVES * P], ATT + 18432)
        att = sb("att", [P, HALVES, P], ATT + 20480)
        state = sb("state", [P, 3, DH], ATT + 21504)
        log_a = sb("log_a", [P, HALVES, HEADS * DK], ATT + 24576)
        res = sb("res", [P, HALVES, TILE], ATT)
        res_t = sb("res_t", [P, TILE // P, HALVES * P], ATT + 4096)
        g2 = sb("g2", [P, HALVES, TILE], ATT + 8192)
        x1 = sb("x1", [P, HALVES, D], ATT + 12288)
        xin = sb("xin", [P, 2, HALVES, TILE], ZH)
        sq1 = sb("sq1", [P, HALVES, TILE], ZH + 8192)
        act_hi = sb("act_hi", [P, KTF, HALVES * P], ZH, FP32R)
        act_lo = sb("act_lo", [P, KTF, HALVES * P], ZH + KTF * HALVES * P * 4, FP32R)
        fin = sb("fin", [P, COLS, HALVES, TILE], GATE + 16384)

        acc = [ctx.enter_context(nc.psum_tensor(f"acc{s}", [P, HALVES, TILE], FP32)) for s in range(2)]
        bank = [ctx.enter_context(nc.psum_tensor(f"bank{b}", [P, TILE], FP32)) for b in range(4)]

        def sem(name):
            return ctx.enter_context(nc.semaphore(name))

        chunk_split = sem("chunk_split")
        chunk_used = sem("chunk_used")
        acc_free = [sem(f"acc_free{s}") for s in range(2)]
        bias_used = sem("bias_used")
        raw_landed = [sem(f"raw_landed{s}") for s in range(RING)]
        chunk_hi = sem("chunk_hi")
        bias_landed = [sem(f"bias_landed{s}") for s in range(2)]
        act_step = sem("act_step")
        dve_step = sem("dve_step")
        pool_step = sem("pool_step")
        passed_sp, passed_act, passed_pool = sem("passed_sp"), sem("passed_act"), sem("passed_pool")
        params_landed = sem("params_landed")
        wa_landed = sem("wa_landed")
        gains_landed = sem("gains_landed")
        in_landed = {g: sem(f"in_landed{g}") for g in (0, 1, *range(2, 2 * CPT, 2))}
        eps_ready = sem("eps_ready")
        ident_ready = sem("ident_ready")
        consts_ready = sem("consts_ready")
        gains_turned = sem("gains_turned")
        gains_ready = sem("gains_ready")
        in_turned = sem("in_turned")
        in_hi = sem("in_hi")
        in_lo = sem("in_lo")
        rms_in_done = sem("rms_in_done")
        rstd_in_done = sem("rstd_in_done")
        wa_hi_done = sem("wa_hi_done")
        wa_split = sem("wa_split")
        low_done = sem("low_done")
        low_t_ready = sem("low_t_ready")
        lgate_done = sem("lgate_done")
        larg_done = sem("larg_done")
        lln_done = sem("lln_done")
        log_a_done = sem("log_a_done")
        decay_sum = sem("decay_sum")
        decay_done = sem("decay_done")
        ms_z_done = sem("ms_z_done")
        rms_z_done = sem("rms_z_done")
        lam_dot_done = sem("lam_dot_done")
        lam_exp_done = sem("lam_exp_done")
        qk_turned = sem("qk_turned")
        qk_back = sem("qk_back")
        d_scores, m_scores = sem("d_scores"), sem("m_scores")
        dp_turned, mp_turned = sem("dp_turned"), sem("mp_turned")
        d_out, m_out = sem("d_out"), sem("m_out")
        dy_turned, my_turned, gy_turned = sem("dy_turned"), sem("my_turned"), sem("gy_turned")
        g_sums, g_turned, g_inc, g_att, g_out = (sem("g_sums"), sem("g_turned"), sem("g_inc"),
                                                 sem("g_att"), sem("g_out"))
        dqt_ready, mqt_ready = sem("dqt_ready"), sem("mqt_ready")
        dmax_ready, mmax_ready = sem("dmax_ready"), sem("mmax_ready")
        dp_ready, mp_ready = sem("dp_ready"), sem("mp_ready")
        da_ready = sem("da_ready")
        dpt_ready, mpt_ready = sem("dpt_ready"), sem("mpt_ready")
        dy_ready, my_ready, gy_ready = sem("dy_ready"), sem("my_ready"), sem("gy_ready")
        dy_hi, my_hi, gy_hi = sem("dy_hi"), sem("my_hi"), sem("gy_hi")
        dy_lo, my_lo, gy_lo = sem("dy_lo"), sem("my_lo"), sem("gy_lo")
        ge_ready = sem("ge_ready")
        gd_ready = sem("gd_ready")
        gt_ready = sem("gt_ready")
        gs_ready = sem("gs_ready")
        ga_copied = sem("ga_copied")
        ga_ready = sem("ga_ready")
        gg_exp = sem("gg_exp")
        go_rms = sem("go_rms")
        sig_g2, sig_g01 = sem("sig_g2"), sem("sig_g01")
        g2_ready = sem("g2_ready")
        res_ready = sem("res_ready")
        res_turned = sem("res_turned")
        res_turned_v = sem("res_turned_v")
        res_hi = sem("res_hi")
        res_lo = sem("res_lo")
        xin_landed = [sem(f"xin_landed{s}") for s in range(2)]
        x1_squared = sem("x1_squared")
        x1_sum = sem("x1_sum")
        x1_rms = sem("x1_rms")
        x1_rstd = sem("x1_rstd")
        half_done = sem("half_done")
        fin_ready = sem("fin_ready")
        out_stored = sem("out_stored")

        block = ctx.enter_context(nc.Block())

        def nth(base, i, per, u):
            return base + u if i is None else i * per + (base + u)

        @block.sync
        def _(sp):
            def load_in(g, n):
                source, view = (mem_raw, mem_v) if g < CPT else (x_raw, x_v)
                r = slice(g % CPT * KPC * P, (g % CPT + n) * KPC * P)
                sp.dma_start(source[:, :, r], view[:, :, r]).then_inc(in_landed[g], 16)

            def load(base, i, per, u, source):
                sp.wait_ge(chunk_split, nth(base, i, per, u) + 1)
                sp.sem_inc(passed_sp, 1)
                sp.dma_start(raw[:, u % RING, :, :], source).then_inc(raw_landed[u % RING], 16)

            def load_tile(base, i, per, u0, view, col, chunks):
                for c in range(chunks):
                    load(base, i, per, u0 + c, view[:, KPC * c:KPC * (c + 1), bass.ds(col, TILE)])

            wa_v = w_in_v[:, :, GLA_COLS:GLA_COLS + RANK]
            params = [(lam_v[:, k, :], v.partition_broadcast(P)) for k, v in
                      enumerate((diff_lambda_q1, diff_lambda_k1, diff_lambda_q2, diff_lambda_k2))]
            params += [(gla_gain[:, :], gla_norm_g.partition_broadcast(P)),
                       (sub_gain[:, :], diff_subln_g.partition_broadcast(P)),
                       (alpha_up[:, :], gla_w_alpha_up[0, :, :]),
                       (alpha_b[:, :], gla_b_alpha.partition_broadcast(P))]
            params += [(gain_rows2[g0 - NG1:g0 - NG1 + m, :], v.rearrange("o (k p) -> (o k) p", p=P))
                       for v, g0, m in ((norm_ffn_g, G_FFN, KT), (diff_q_norm_g, G_DQ, 1),
                                        (diff_k_norm_g, G_DK, 1), (mem_q_norm_g, G_MQ, 2),
                                        (mem_k_norm_g, G_MK, 2))]
            assert len(params) == PARAMS
            for u in range(MN * MP):
                c, col = u % CPT, u // CPT * TILE
                load(M0, None, 0, u, w_kv_v[:, KPC * c:KPC * (c + 1), col:col + TILE])
                if u == 0:
                    load_in(0, 1)
                    load_in(1, 1)
                elif u < CPT:
                    load_in(2 * u, 2)
                if u in (8, 9):
                    r = slice((u - 8) * KT // 2, (u - 7) * KT // 2)
                    sp.dma_start(wa_raw[:, r, :], wa_v[:, r, :]).then_inc(wa_landed, 16)
                if 10 <= u < 10 + PARAMS:
                    sp.dma_start(*params[u - 10]).then_inc(params_landed, 16)
            with sp.Fori(0, IN) as i:
                for t in range(2):
                    load_tile(I0, i, IP, t * CPT, w_in_v, i * (2 * TILE) + (DIFF_COL + t * TILE), CPT)
            with sp.Fori(0, LN) as i:
                for t in range(2):
                    load_tile(L0, i, LP, t * CPT, w_in_v, i * (2 * TILE) + t * TILE, CPT)
            with sp.Fori(0, GN) as i:
                for t in range(2):
                    sp.wait_ge(bias_used, i * 2 + (t + 1))
                    sp.sem_inc(passed_sp, 1)
                    col = i * (2 * TILE) + t * TILE
                    sp.dma_start(bias[:, t, :], b_gate[:, bass.ds(col, TILE)].partition_broadcast(P)
                                 ).then_inc(bias_landed[t], 16)
                    load_tile(G0, i, GP, t * CPT, w_gate_v, col, CPT)
            with sp.Fori(0, BN) as c:
                load_tile(B0, c, BP, 0, w_gate_v, c * TILE + 2 * D, CPT)
                sp.wait_ge(bias_used, c + (2 * GN + 2))
                sp.sem_inc(passed_sp, 1)
                sp.dma_start(bias[:, 0, :], b_gate[:, bass.ds(c * TILE + 2 * D, TILE)].partition_broadcast(P)
                             ).then_inc(bias_landed[0], 16)
                for b in range(3):
                    load_tile(B0, c, BP, CPT + b * CPB, w_br_v[:, b, :, :], c * TILE, CPB)
            with sp.Fori(0, ON) as i:
                for t in range(2):
                    load_tile(O0, i, OP, t * CPT, w_out_v, i * (2 * TILE) + t * TILE, CPT)
                    sp.wait_ge(chunk_used, nth(O0, i, OP, t * CPT) + RING)
                    sp.sem_inc(passed_sp, 1)
                    sp.wait_ge(res_ready, i * 2 + (BN + t - 1))
                    sp.sem_inc(passed_sp, 1)
                    sp.dma_start(xin[:, t, :, :], x_v[:, :, bass.ds(i * (2 * TILE) + t * TILE, TILE)]
                                 ).then_inc(xin_landed[t], 16)
            with sp.Fori(0, FN) as i:
                for t in range(2):
                    load_tile(F0, i, FP, t * CPT, w_fin_v, i * TILE + t * DFF, CPT)
            with sp.Fori(0, DN) as i:
                for t in range(2):
                    load_tile(D0, i, DP, t * CPD, w_down_v, i * (2 * TILE) + t * TILE, CPD)

        @block.tensor
        def _(pe):
            pe.sem_inc(chunk_used, RING)

            def multiply(base, i, per, u, psum, kt, st_hi, st_lo, first, last, by_half=False):
                slot = u % RING
                pe.wait_ge(chunk_split, nth(base, i, per, u) + (RING + 1))
                order = [(j, h) for j in range(KPC) for h in range(HALVES)]
                if by_half:
                    order.sort(key=lambda jh: jh[1])
                for j, h in order:
                    a_hi, a_lo = st_hi(kt + j, h), st_lo(kt + j, h)
                    nc.tensor.matmul(psum[:, h, :], a_hi, whi[:, slot, j, :],
                                     start=first and j == 0, stop=False)
                    nc.tensor.matmul(psum[:, h, :], a_hi, wlo[:, slot, j, :], start=False, stop=False)
                    mm = nc.tensor.matmul(psum[:, h, :], a_lo, whi[:, slot, j, :],
                                          start=False, stop=last and j == KPC - 1)
                    if by_half and (j, h) == (KPC - 1, 0):
                        mm.then_inc(half_done, 1)
                mm.then_inc(chunk_used, 1)

            def tokens(tensor):
                return lambda kt, h: tensor[:, kt, h * P:(h + 1) * P]

            X = tokens(xt_hi), tokens(xt_lo)
            GT = tokens(gt_hi), tokens(gt_lo)
            AT = tokens(act_hi), tokens(act_lo)

            def Y(branch):
                def hi(kt, h):
                    o = Y_OF[branch] + (kt % 2) * HALVES * P + h * P
                    return yt[:, kt // 2, o:o + P]

                def lo(kt, h):
                    o = Y_OF[branch] + (2 + kt % 2) * HALVES * P + h * P
                    return yt[:, kt // 2, o:o + P]
                return hi, lo

            def tile(base, i, per, u0, chunks, slot, tiles, st, hook=None, by_half=False):
                pe.wait_ge(acc_free[slot], tiles)
                for c in range(chunks):
                    multiply(base, i, per, u0 + c, acc[slot], KPC * c, *st, c == 0, c == chunks - 1,
                             by_half and c == chunks - 1)
                    if hook is not None:
                        hook(c)

            def turn_res(t):
                pe.wait_ge(res_ready, BN + t + 1)
                for b in range(2):
                    for j in range(2):
                        for h in range(HALVES):
                            t = nc.tensor.transpose(bank[b][:, j * 2 * P + h * P:j * 2 * P + (h + 1) * P],
                                                    res[:, h, (2 * b + j) * P:(2 * b + j + 1) * P], ident[:, :])
                t.then_inc(res_turned, 1)

            def turn_gains(rows, n, b, done):
                nc.tensor.transpose(bank[b][:, 0:n], rows[:, :], ident[0:n, 0:n]).then_inc(done, 1)

            def turn_in(g):
                source = mem_raw if g < KT // 2 else x_raw
                if g in in_landed:
                    pe.wait_ge(in_landed[g], 16)
                if g == 3:
                    pe.wait_ge(gains_ready, 1)
                if g >= 4:
                    pe.wait_ge(in_lo, g - 3)
                for j in range(2):
                    kt = 2 * (g % (KT // 2)) + j
                    for h in range(HALVES):
                        t = nc.tensor.transpose(bank[g % 4][:, j * 2 * P + h * P:j * 2 * P + (h + 1) * P],
                                                source[:, h, kt * P:(kt + 1) * P], ident[:, :])
                t.then_inc(in_turned, 1)

            def low_rank():
                pe.wait_ge(in_lo, 2 * KT // 2)
                pe.wait_ge(wa_split, 1)
                for kt in range(KT):
                    o = bank[0][0:RANK, 0:HALVES * P]
                    nc.tensor.matmul(o, wa_hi[:, kt, :], xt_hi[:, kt, :], start=kt == 0, stop=False)
                    nc.tensor.matmul(o, wa_hi[:, kt, :], xt_lo[:, kt, :], start=False, stop=False)
                    m = nc.tensor.matmul(o, wa_lo[:, kt, :], xt_hi[:, kt, :], start=False, stop=kt == KT - 1)
                m.then_inc(low_done, 1)

            def low_rank_up():
                pe.wait_ge(low_t_ready, 1)
                pe.wait_ge(params_landed, 16 * PARAMS)
                for h in range(HALVES):
                    m = nc.tensor.matmul(bank[2 + h][:, :], low_t[:, h * P:(h + 1) * P], alpha_up[:, :],
                                         start=True, stop=True)
                m.then_inc(lgate_done, 1)

            def keep_warm(n):
                for k in range(n):
                    nc.tensor.transpose(bank[2][:, k % 4 * P:(k % 4 + 1) * P], ident[:, :], ident[:, :])

            pe.wait_ge(ident_ready, 1)
            keep_warm(16)
            pe.wait_ge(gains_landed, 16 * 2)
            turn_gains(gain_rows, NG1, 3, gains_turned)
            turn_in(0)
            turn_in(1)
            keep_warm(9)

            def start(u):
                if u == 0:
                    turn_in(2)
                if u + IN_AHEAD < 2 * KT // 2:
                    turn_in(u + IN_AHEAD)
                if u == LOW_AT:
                    low_rank()
                if u == LOW_AT + 6:
                    low_rank_up()
                if u == LOW_AT + 7:
                    turn_gains(gain_rows2, NG - NG1, 1, gains_turned)

            for t in range(2 * MN):
                def hook(c, t=t):
                    if t == 0 and c < CPT - 1:
                        pe.wait_ge(in_lo, c + 2)
                    start(t * CPT + c)
                if t == 0:
                    pe.wait_ge(in_lo, 1)
                tile(M0, None, 0, t * CPT, CPT, t % 2, M_T + 1 + t // 2, GT, hook)
            with pe.Fori(0, IN) as i:
                for t in range(2):
                    tile(I0, i, IP, t * CPT, CPT, t, i + (I_T + 1), X)
            with pe.Fori(0, LN) as i:
                for t in range(2):
                    tile(L0, i, LP, t * CPT, CPT, t, i + (L_T + 1), X)
            pe.wait_ge(log_a_done, 1)
            pe.wait_ge(consts_ready, 1)
            for n in range(HEADS):
                for h in range(HALVES):
                    m = nc.tensor.matmul(bank[0][:, n * 4 + 2 * h:n * 4 + 2 * h + 2],
                                         log_a[:, h, n * DK:(n + 1) * DK], chunk_of[:, :], start=True, stop=True)
            m.then_inc(decay_sum, 1)

            with pe.Fori(0, GN) as n:
                def keys(place, j):
                    k = zh[:, n, place:place + 2 * DH].rearrange("p (h j t) -> p h j t", h=HALVES, j=2)
                    return k[:, :, j, :]

                def turn_y(y, ready, b, done):
                    pe.wait_ge(ready, n + 1)
                    for j in range(2):
                        for h in range(HALVES):
                            t = nc.tensor.transpose(bank[b][:, j * 2 * P + h * P:j * 2 * P + (h + 1) * P],
                                                    y[:, h, j * P:(j + 1) * P], ident[:, :])
                    t.then_inc(done, 1)

                def gla_sums():
                    for h in range(HALVES):
                        nc.tensor.matmul(bank[3][:, h * DK:(h + 1) * DK], upto[:, :],
                                         log_a[:, h, bass.ds(n * DK, DK)], start=True, stop=True)
                    for h in range(HALVES):
                        m = nc.tensor.matmul(bank[3][:, (2 + h) * DK:(3 + h) * DK], after[:, :],
                                             log_a[:, h, bass.ds(n * DK, DK)], start=True, stop=True)
                    m.then_inc(g_sums, 1)

                def gla_turn():
                    pe.wait_ge(gd_ready, n + 1)
                    for s, src in enumerate((qd, kd)):
                        for h in range(HALVES):
                            t = nc.tensor.transpose(bank[2][:, (2 * s + h) * P:(2 * s + h + 1) * P],
                                                    src[:, h, :], ident[:, :])
                    t.then_inc(g_turned, 1)
                    for c in range(2):
                        m = nc.tensor.matmul(bank[3][:, c * DH:(c + 1) * DH], k_tail[:, c, 0, :],
                                             zh[:, n, GV:GV + DH], start=True, stop=True)
                    m.then_inc(g_inc, 1)

                def gla_scores():
                    pe.wait_ge(gt_ready, n + 1)
                    for h in range(HALVES):
                        nc.tensor.matmul(bank[2][:, h * P:(h + 1) * P], g_t[:, 1, h * P:(h + 1) * P],
                                         g_t[:, 0, h * P:(h + 1) * P], start=True, stop=True)
                    m = nc.tensor.matmul(bank[2][:, DH:2 * DH], k_tail[:, 0, 1, :],
                                         zh[:, n, GV + DH:GV + 2 * DH], start=True, stop=True)
                    m.then_inc(g_att, 1)

                def gla_output():
                    pe.wait_ge(ga_ready, n + 1)
                    pe.wait_ge(gs_ready, n + 1)
                    for h in range(HALVES):
                        o = bank[2][:, h * DH:(h + 1) * DH]
                        nc.tensor.matmul(o, att[:, h, :], zh[:, n, GV + h * DH:GV + (h + 1) * DH],
                                         start=True, stop=True, skip_group_check=True)
                        for c in range(2):
                            if 2 * h + c == 0:
                                continue
                            r = slice(c * CHUNK, (c + 1) * CHUNK)
                            m = nc.tensor.matmul(bank[2][r, h * DH:(h + 1) * DH],
                                                 g_t[:, 0, h * P + c * CHUNK:h * P + (c + 1) * CHUNK],
                                                 state[:, 2 * h + c - 1, :], start=False, stop=True,
                                                 skip_group_check=True)
                    m.then_inc(g_out, 1)

                def diff_scores():
                    pe.wait_ge(dqt_ready, n + 1)
                    pe.wait_ge(qk_back, 2 * HEADS + 2)
                    for j in range(2):
                        nc.tensor.matmul(bank[0][:, j * 2 * P:(j + 1) * 2 * P], dq_t[:, 1, j, :],
                                         keys(DKO, j), start=True, stop=True)
                    for j in range(2):
                        m = nc.tensor.matmul(bank[1][:, j * P:(j + 1) * P], dq_t[:, 0, j, :],
                                             zh[:, n, DKO + j * P:DKO + (j + 1) * P], start=True, stop=True)
                    m.then_inc(d_scores, 1)

                def diff_turn():
                    pe.wait_ge(da_ready, n + 1)
                    for s, at in enumerate((512, 0, P)):
                        t = nc.tensor.transpose(bank[0][:, s * P:(s + 1) * P], prob[:, at:at + P], ident[:, :])
                    t.then_inc(dp_turned, 1)

                def diff_output():
                    pe.wait_ge(dpt_ready, n + 1)
                    nc.tensor.matmul(bank[0][:, 0:DH], prob_t[:, 0:P], zh[:, n, DV:DV + DH],
                                     start=True, stop=True)
                    nc.tensor.matmul(bank[0][:, DH:2 * DH], prob_t[:, P:2 * P], zh[:, n, DV:DV + DH],
                                     start=True, stop=False)
                    nc.tensor.matmul(bank[0][:, DH:2 * DH], prob_t[:, 2 * P:3 * P],
                                     zh[:, n, DV + DH:DV + 2 * DH], start=False, stop=True).then_inc(d_out, 1)

                def mem_scores():
                    pe.wait_ge(mqt_ready, n + 1)
                    for h in range(HALVES):
                        for j in range(2):
                            m = nc.tensor.matmul(bank[1][:, h * 2 * P:(h + 1) * 2 * P],
                                                 mq_t[:, h, j, :], keys(MK, j),
                                                 start=j == 0, stop=j == 1)
                    m.then_inc(m_scores, 1)

                def mem_turn():
                    pe.wait_ge(mp_ready, n + 1)
                    for h in range(HALVES):
                        for j in range(2):
                            t = nc.tensor.transpose(bank[1][:, (2 * h + j) * P:(2 * h + j + 1) * P],
                                                    prob[:, (2 * h + j) * P:(2 * h + j + 1) * P], ident[:, :])
                    t.then_inc(mp_turned, 1)

                def mem_output():
                    pe.wait_ge(mpt_ready, n + 1)
                    for h in range(HALVES):
                        for j in range(2):
                            m = nc.tensor.matmul(bank[1][:, h * DH:(h + 1) * DH],
                                                 prob_t[:, (2 * h + j) * P:(2 * h + j + 1) * P],
                                                 zh[:, n, MV + j * DH:MV + (j + 1) * DH],
                                                 start=j == 0, stop=j == 1)
                    m.then_inc(m_out, 1)

                def heads(c):
                    if c == 0:
                        gla_sums()

                    if c == 6:
                        gla_turn()
                    if c == 7:
                        diff_scores()
                    if c == 8:
                        gla_scores()
                    if c == 9:
                        diff_turn()
                    if c == 10:
                        gla_output()
                    if c == 11:
                        diff_output()
                        mem_scores()
                    if c == 13:
                        turn_y(sg, gy_ready, 2, gy_turned)
                        turn_y(kn, dy_ready, 0, dy_turned)
                        mem_turn()
                    if c == 14:
                        mem_output()
                    if c == 15:
                        turn_y(qn, my_ready, 1, my_turned)

                for t in range(2):
                    tile(G0, n, GP, t * CPT, CPT, t, n + (G_T + 1), X,
                         lambda c, t=t: heads(t * CPT + c))

            with pe.Fori(0, BN) as c:
                tile(B0, c, BP, 0, CPT, 0, c * 2 + (B_T + 1), X)
                for y_lo in (dy_lo, my_lo, gy_lo):
                    pe.wait_ge(y_lo, HEADS)
                tile(B0, c, BP, CPT, CPB, 1, c * 2 + (B_T + 1), Y(0))
                tile(B0, c, BP, CPT + CPB, CPB, 0, c * 2 + (B_T + 2), Y(1))
                tile(B0, c, BP, CPT + 2 * CPB, CPB, 1, c * 2 + (B_T + 2), Y(2))

            for t in range(COLS):
                def hook(c, t=t):
                    if c == 3 and t > 0:
                        turn_res(t - 1)
                    if c == 5 and t == 0:
                        pe.wait_ge(res_lo, 2 * BN)
                tile(O0, None, 0, t * CPT, CPT, t % 2, O_T + 1 + t // 2, GT, hook)

            def last_turn(c):
                if c == 3:
                    turn_res(COLS - 1)
                if c == 5:
                    pe.wait_ge(res_lo, 2 * (BN + COLS))
            tile(F0, None, 0, 0, CPT, 0, F_T + 1, X, last_turn)
            tile(F0, None, 0, CPT, CPT, 1, F_T + 1, X)
            with pe.Fori(1, FN) as i:
                tile(F0, i, FP, 0, CPT, 0, i + (F_T + 1), X)
                tile(F0, i, FP, CPT, CPT, 1, i + (F_T + 1), X)

            def last_act(c):
                if c == CPD - 3:
                    pe.wait_ge(res_lo, 2 * (BN + COLS + FT))
            for t in range(COLS):
                tile(D0, None, 0, t * CPD, CPD, t % 2, D_T + 1 + t // 2, AT, last_act if t == 0 else None,
                     by_half=t == COLS - 1)

        @block.scalar
        def _(act):
            own = Tally(act, act_step)
            for v, g0 in ((norm_mem_g, G_MEM), (norm_mix_g, G_MIX)):
                act.dma_start(gain_rows[g0:g0 + KT, :], v.rearrange("o (k p) -> (o k) p", p=P)
                              ).then_inc(gains_landed, 16)

            def split(base, i, per, u):
                s = u % RING
                act.wait_ge(raw_landed[s], 16 * nth(base // RING, i, per // RING, u // RING + 1))
                act.wait_ge(chunk_used, nth(base, i, per, u) + 1)
                nc.scalar.activation(whi[:, s, :, :], raw[:, s, :, :], ACT.Copy).then_inc(chunk_hi, 1)

            def split_some(base, i, per, u, count):
                for k in range(count):
                    split(base, i, per, u + k)

            def store_z(base, i, per, t, src, dest):
                act.wait_ge(chunk_used, nth(base, i, per, (t + 1) * CPT) + RING)
                for h in range(HALVES):
                    a = nc.scalar.activation(dest(h), acc[t][:, h, :].rearrange("p (n c) -> p n c", c=dest(h).shape[2]),
                                             ACT.Copy, scale=rstd_in[:, src, h:h + 1])
                a.then_inc(acc_free[t], 1)

            def two_heads(i, item, t):
                return lambda h: zh[:, 2 * t:2 * t + 2, bass.ds(i * TILE + (item + h * DH), DH)]

            def in_group(g):
                act.wait_ge(in_turned, g + 1)
                hi, g0 = (gt_hi, G_MEM) if g < KT // 2 else (xt_hi, G_MIX)
                for j in range(2):
                    kt = 2 * (g % (KT // 2)) + j
                    a = nc.scalar.activation(hi[:, kt, :], bank[g % 4][:, j * 2 * P:(j + 1) * 2 * P], ACT.Copy,
                                             scale=gains[:, g0 + kt:g0 + kt + 1])
                a.then_inc(in_hi, 1)

            def in_squares(k, h):
                source = (mem_raw, x_raw)[k]
                own.step(nc.scalar.activation(junk[:, :], source[:, h, :], ACT.Square,
                                              accum_out=ssq_in[:, k, h:h + 1]))

            def in_rms(k):
                nc.scalar.activation(rms_in[:, k, :], ssq_in[:, k, :], ACT.Sqrt, scale=1.0 / D,
                                     bias=eps[:, :]).then_inc(rms_in_done, 1)

            act.wait_ge(eps_ready, 1)
            own.step(nc.scalar.activation(rms_o[:, 0:1], eps[:, :], ACT.Sqrt))
            for u in range(MN * MP + LEAD):
                split(M0, None, 0, u)
                if u == 0:
                    act.wait_ge(gains_ready, 1)
                if u < 2 * KT // 2:
                    in_group(u)
                if u in (8, 9):
                    in_squares(0, u - 8)
                if u == 10:
                    in_rms(0)
                if u == 12:
                    act.wait_ge(wa_landed, 16 * 2)
                    nc.scalar.activation(wa_hi[:, :, :], wa_raw[:, :, :], ACT.Copy).then_inc(wa_hi_done, 1)
                if u in (16, 17):
                    in_squares(1, u - 16)
                if u == 18:
                    in_rms(1)
                if u == LOW_AT + 4:
                    act.wait_ge(low_done, 1)
                    nc.scalar.activation(low_t[:, :], bank[0][0:RANK, 0:HALVES * P], ACT.Copy
                                         ).then_inc(low_t_ready, 1)
                if u == LOW_AT + 12:
                    act.wait_ge(larg_done, 1)
                    own.step(nc.scalar.activation(labs[:, :, :], log_a[:, :, :], ACT.Abs))
                if u == LOW_AT + 13:
                    own.step(nc.scalar.activation(lexp[:, :, :], labs[:, :, :], ACT.Exp, scale=-1.0))
                if u == LOW_AT + 15:
                    nc.scalar.activation(labs[:, :, :], lexp[:, :, :], ACT.Ln, bias=1.0).then_inc(lln_done, 1)
                if u >= LEAD and (u - LEAD) % CPT == 3:
                    t = (u - LEAD) // CPT
                    if t == 0:
                        act.wait_ge(rstd_in_done, 1)
                    store_z(M0, t // 2, MP, t % 2, 0, two_heads(t // 2, MK, t % 2))
            act.wait_ge(rstd_in_done, 2)
            act.wait_ge(gains_ready, 2)
            with act.Fori(0, IN) as i:
                for t in range(2):
                    split_some(I0, i, IP, LEAD + t * CPT, 4)
                    store_z(I0, i, IP, t, 1, two_heads(i, DQ, t))
                    split_some(I0, i, IP, LEAD + t * CPT + 4, CPT - 4)
            act.wait_ge(lam_dot_done, 1)
            nc.scalar.activation(lam_exp[:, :], lam_dot[:, :], ACT.Exp).then_inc(lam_exp_done, 1)
            for t, item in enumerate((GQ, GK)):
                split_some(L0, None, 0, LEAD + t * CPT, 4)
                if t == 0:
                    act.wait_ge(ms_z_done, 1)
                    nc.scalar.activation(rstd_z[:, :, :], ms_z[:, :, :], ACT.Sqrt, bias=eps[:, :]
                                         ).then_inc(rms_z_done, 1)
                store_z(L0, None, 0, t, 1, lambda h: zh[:, :, item + h * DK:item + (h + 1) * DK])
                split_some(L0, None, 0, LEAD + t * CPT + 4, CPT - 4)
            with act.Fori(1, LN) as i:
                for s in range(LP):
                    split(L0, i, LP, LEAD + s)
                    if s % CPT == 3:
                        store_z(L0, i, LP, s // CPT, 1, two_heads(i, GV - TILE, s // CPT))
                    if s in QK_BACK_AT:
                        unit = QK_BACK_AT.index(s)
                        act.wait_ge(qk_turned, i * 4 + (unit - 3))
                        act.sem_inc(passed_act, 1)
                        place = (DQ, MQ)[unit % 2]
                        nc.scalar.activation(zh[:, i * 2 + (unit // 2 - 2), place:place + 4 * DH],
                                             turned[:, unit % 2, :, :].rearrange("p b t -> p (b t)"), ACT.Copy
                                             ).then_inc(qk_back, 1)
            act.wait_ge(decay_sum, 1)
            nc.scalar.activation(decay[:, :, :], bank[0][:, 0:HEADS * 4].rearrange("p (n c) -> p n c", c=4),
                                 ACT.Exp, scale=1.0 / GATE_NORM).then_inc(decay_done, 1)

            with act.Fori(0, GN) as n:
                own.enter(n, ACT_HEAD_STEPS)

                def gla_decays():
                    act.wait_ge(g_sums, n + 1)
                    nc.scalar.activation(qd[:, :, :], bank[3][:, 0:2 * DK], ACT.Exp, scale=1.0 / GATE_NORM)
                    nc.scalar.activation(kd[:, :, :], bank[3][:, 0:2 * DK], ACT.Exp, scale=-1.0 / GATE_NORM)
                    nc.scalar.activation(e_tail[:, :, :], bank[3][:, 2 * DK:4 * DK], ACT.Exp,
                                         scale=1.0 / GATE_NORM).then_inc(ge_ready, 1)

                def queries():
                    act.wait_ge(qk_back, 2 * HEADS + 2)
                    nc.scalar.activation(dq_t[:, :, :, :], zh[:, n, DQ:DQ + 2 * DH], ACT.Copy,
                                         scale=gains[:, G_DQ:G_DQ + 1]).then_inc(dqt_ready, 1)
                    q = zh[:, n, MQ:MQ + 2 * DH].rearrange("p (h j t) -> p h j t", h=HALVES, j=2)
                    for j in range(2):
                        a = nc.scalar.activation(mq_t[:, :, j, :], q[:, :, j, :], ACT.Copy,
                                                 scale=gains[:, G_MQ + j:G_MQ + j + 1])
                    a.then_inc(mqt_ready, 1)

                def gla_qk():
                    act.wait_ge(g_turned, n + 1)
                    nc.scalar.activation(g_t[:, :, :], bank[2][:, :], ACT.Copy).then_inc(gt_ready, 1)

                def gla_silu():
                    nc.scalar.activation(sg[:, :, :], zh[:, n, GG:GG + 2 * DH], ACT.Exp, scale=-1.0
                                         ).then_inc(gg_exp, 1)

                def diff_exp():
                    act.wait_ge(dmax_ready, n + 1)
                    for k, (b, at, src, w) in enumerate(((0, 0, 0, 2 * P), (0, 2 * P, 2 * P, 2 * P),
                                                         (1, 4 * P, 0, P), (1, 5 * P, P, P))):
                        a = nc.scalar.activation(prob[:, at:at + w], bank[b][:, src:src + w], ACT.Exp,
                                                 scale=DK ** -0.5, bias=nmax[:, k:k + 1],
                                                 accum_out=psum_exp[:, k:k + 1])
                    a.then_inc(dp_ready, 1)

                def gla_copy():
                    act.wait_ge(g_att, n + 1)
                    scores = bank[2][:, 0:2 * P].rearrange("p (h t) -> p h t", t=P)
                    for c in range(2):
                        r = slice(c * CHUNK, (c + 1) * CHUNK)
                        a = nc.scalar.activation(att[r, :, r], scores[r, :, r], ACT.Copy)
                    a.then_inc(ga_copied, 1)

                def diff_weights():
                    act.wait_ge(dp_turned, n + 1)
                    nc.scalar.activation(prob_t[:, 0:3 * P], bank[0][:, 0:3 * P], ACT.Copy).then_inc(dpt_ready, 1)

                def mem_exp():
                    act.wait_ge(mmax_ready, n + 1)
                    for h in range(HALVES):
                        r = slice(h * 2 * P, (h + 1) * 2 * P)
                        a = nc.scalar.activation(prob[:, r], bank[1][:, r], ACT.Exp, scale=DH ** -0.5,
                                                 bias=nmax[:, 4 + h:5 + h], accum_out=psum_exp[:, 4 + h:5 + h])
                    a.then_inc(mp_ready, 1)

                def output_rms():
                    act.wait_ge(g_out, n + 1)
                    for h in range(HALVES):
                        nc.scalar.activation(g_t[:, h, :], bank[2][:, h * DH:(h + 1) * DH], ACT.Square,
                                             accum_out=ssq_o[:, 2 + h:3 + h])
                    act.wait_ge(d_out, n + 1)
                    for h in range(HALVES):
                        a = nc.scalar.activation(kn[:, h, :], bank[0][:, h * DH:(h + 1) * DH], ACT.Square,
                                                 accum_out=ssq_o[:, h:h + 1])
                    own.step(a)
                    nc.scalar.activation(rms_o[:, :], ssq_o[:, :], ACT.Sqrt, scale=1.0 / DH, bias=eps[:, :]
                                         ).then_inc(go_rms, 1)

                def mem_weights():
                    act.wait_ge(mp_turned, n + 1)
                    nc.scalar.activation(prob_t[:, :], bank[1][:, :], ACT.Copy).then_inc(mpt_ready, 1)

                def y_hi(turned, b, place, done):
                    act.wait_ge(turned, n + 1)
                    act.sem_inc(passed_act, 1)
                    nc.scalar.activation(yt[:, n, place:place + 2 * DH], bank[b][:, :], ACT.Copy).then_inc(done, 1)

                for s in range(GP):
                    split(G0, n, GP, LEAD + s)
                    if s == 0:
                        gla_decays()
                    if s == 1:
                        queries()
                    if s == 2:
                        gla_qk()
                        gla_silu()
                    if s == 3:
                        diff_exp()
                    if s == 4:
                        gla_copy()
                    if s == 5:
                        diff_weights()
                    if s == 7:
                        output_rms()
                        mem_exp()
                    if s == 9:
                        mem_weights()
                        y_hi(gy_turned, 2, GQ, gy_hi)
                        y_hi(dy_turned, 0, DQ, dy_hi)
                    if s == 13:
                        y_hi(my_turned, 1, MQ, my_hi)
                own.leave(GN)

            def turned_hi(k, turned, hi, first):
                for h in range(HALVES):
                    act.wait_ge(res_turned_v, turned * 2 + (h + 1))
                    cols = slice(h * P, (h + 1) * P)
                    nc.scalar.activation(hi[:, bass.ds(first, 4), cols], res_t[:, :, cols], ACT.Copy
                                         ).then_inc(res_hi, 1)

            with act.Fori(0, BN) as c:
                split_some(B0, c, BP, LEAD, 4)
                act.wait_ge(bias_used, 2 * GN + 2)
                for b in range(2):
                    a = nc.scalar.activation(gates[:, c + b * COLS, :, :], gates[:, c + b * COLS, :, :], ACT.Sigmoid)
                a.then_inc(sig_g01, 1)
                split_some(B0, c, BP, LEAD + 4, 4)
                act.wait_ge(g2_ready, c + 1)
                nc.scalar.activation(g2[:, :, :], g2[:, :, :], ACT.Sigmoid).then_inc(sig_g2, 1)
                split_some(B0, c, BP, LEAD + 8, BP - 9)
                turned_hi(c, c, gt_hi, c * 4)
                split(B0, c, BP, LEAD + BP - 1)

            for t in range(COLS):
                split_some(O0, None, 0, LEAD + t * CPT, 4)
                k = BN + t
                act.wait_ge(res_ready, k + 1)
                nc.scalar.activation(x1[:, :, t * TILE:(t + 1) * TILE], res[:, :, :], ACT.Copy)
                for h in range(HALVES):
                    a = nc.scalar.activation(sq1[:, h, :], res[:, h, :], ACT.Square,
                                             accum_out=ssq_x1[:, h, t:t + 1])
                a.then_inc(x1_squared, 1)
                if t == COLS - 1:
                    act.wait_ge(x1_sum, 1)
                    nc.scalar.activation(rms_x1[:, :], sum_x1[:, :], ACT.Sqrt, scale=1.0 / D, bias=eps[:, :]
                                         ).then_inc(x1_rms, 1)
                split_some(O0, None, 0, LEAD + t * CPT + 4, 4)
                act.wait_ge(res_turned, t + 1)
                for b in range(2):
                    for j in range(2):
                        kt = 4 * t + 2 * b + j
                        a = nc.scalar.activation(xt_hi[:, kt, :], bank[b][:, j * 2 * P:(j + 1) * 2 * P], ACT.Copy,
                                                 scale=gains[:, G_FFN + kt:G_FFN + kt + 1])
                    a.then_inc(res_hi, 1)
                if t < COLS - 1:
                    act.wait_ge(x1_squared, t + 1)

            act.wait_ge(x1_rstd, 1)
            with act.Fori(0, FN) as i:
                split_some(F0, i, FP, LEAD, 4)
                act.wait_ge(chunk_used, nth(F0, i, FP, CPT) + RING)
                act.wait_ge(res_ready, i + (BN + COLS))
                for h in range(HALVES):
                    a = nc.scalar.activation(g2[:, h, :], acc[0][:, h, :], ACT.Silu, scale=rstd_x1[:, h:h + 1])
                a.then_inc(acc_free[0], 1)
                split_some(F0, i, FP, LEAD + 4, FP - 5)
                turned_hi(i + (BN + COLS), i + BN, act_hi, i * 4)
                split(F0, i, FP, LEAD + FP - 1)

            def store(t, h, ready):
                act.wait_ge(fin_ready, ready)
                act.dma_start(out_v[:, h, t * TILE:(t + 1) * TILE], fin[:, t, h, :]).then_inc(out_stored, 16)

            for t in range(COLS):
                u = LEAD + t * CPD
                last = t == COLS - 1
                split_some(D0, None, 0, u, CPD - LEAD if last else CPD - 4)
                if not last:
                    split_some(D0, None, 0, u + CPD - 4, 4)
                for h in range(HALVES):
                    store(t, h, t + 1 + (last and h))
            act.wait_ge(out_stored, 16 * COLS * HALVES)

        @block.vector
        def _(dve):
            own = Tally(dve, dve_step)
            V = nc.vector
            dve.sem_inc(chunk_split, RING)
            dve.sem_inc(acc_free[0], 1)
            dve.sem_inc(acc_free[1], 1)
            dve.sem_inc(bias_used, 2)
            dve.sem_inc(qk_back, 2)

            def f32(ap):
                return ap.bitcast(FP32)

            def split(base, i, per, u):
                s = u % RING
                dve.wait_ge(chunk_hi, nth(base, i, per, u) + 1)
                V.tensor_tensor(wlo[:, s, :, :], raw[:, s, :, :], f32(whi[:, s, :, :]), ALU.subtract
                                ).then_inc(chunk_split, 1)

            def split_some(base, i, per, u, count):
                for k in range(count):
                    split(base, i, per, u + k)

            def squares(tiles_before, i, t, item, place):
                dve.wait_ge(acc_free[t], nth(tiles_before, i, 1, 2))
                off = i * TILE + place
                for h in range(HALVES):
                    z = zh[:, 2 * t:2 * t + 2, bass.ds(off + h * DH, DH)]
                    v = V.tensor_tensor(sq[:, h, :].rearrange("p (n c) -> p n c", n=2), z, z, ALU.mult)
                own.step(v)
                for h in range(HALVES):
                    v = V.reduce_sum(ssq_z[:, 2 * t:2 * t + 2, i + item, 2 * h:2 * h + 2],
                                     sq[:, h, :].rearrange("p (n j c) -> p n j c", n=2, c=DK), AX.X)
                own.step(v)

            def in_group(g):
                dve.wait_ge(in_hi, g + 1)
                hi, lo, g0 = (gt_hi, gt_lo, G_MEM) if g < KT // 2 else (xt_hi, xt_lo, G_MIX)
                for j in range(2):
                    kt = 2 * (g % (KT // 2)) + j
                    v = V.scalar_tensor_tensor(lo[:, kt, :], bank[g % 4][:, j * 2 * P:(j + 1) * 2 * P],
                                               gains[:, g0 + kt:g0 + kt + 1], f32(hi[:, kt, :]),
                                               ALU.mult, ALU.subtract)
                v.then_inc(in_lo, 1)

            V.memset(lam_dot[:, :], 0.0)
            dve.wait_ge(gains_turned, 1)
            own.step(V.tensor_copy(gains[:, 0:NG1], bank[3][:, 0:NG1]))
            dve.sem_inc(gains_ready, 1)
            for u in range(MN * MP + LEAD):
                split(M0, None, 0, u)
                if u < 2 * KT // 2:
                    in_group(u)
                if u in (10, 18):
                    k = (u - 10) // 8
                    dve.wait_ge(rms_in_done, k + 1)
                    V.reciprocal(rstd_in[:, k, :], rms_in[:, k, :]).then_inc(rstd_in_done, 1)
                if u == 13:
                    dve.wait_ge(wa_hi_done, 1)
                    V.tensor_tensor(wa_lo[:, :, :], wa_raw[:, :, :], f32(wa_hi[:, :, :]), ALU.subtract
                                    ).then_inc(wa_split, 1)
                if u == LOW_AT + 10:
                    dve.wait_ge(params_landed, 16 * PARAMS)
                    prod = sq[:, 0, 0:2 * DK].rearrange("p (a b) -> p a b", a=2)
                    own.step(V.tensor_tensor(prod, lam_v[:, 0:4:2, :], lam_v[:, 1:4:2, :], ALU.mult))
                    V.reduce_sum(lam_dot[:, :], prod, AX.X).then_inc(lam_dot_done, 1)
                    own.step(V.tensor_scalar(sub_gain[:, :], sub_gain[:, :], 1.0 - LAM_INIT, None, ALU.mult))
                if u == LOW_AT + 11:
                    dve.wait_ge(rstd_in_done, 2)
                    dve.wait_ge(lgate_done, 1)
                    for h in range(HALVES):
                        v = V.scalar_tensor_tensor(log_a[:, h, :], bank[2 + h][:, :], rstd_in[:, 1, h:h + 1],
                                                   alpha_b[:, :], ALU.mult, ALU.add)
                    v.then_inc(larg_done, 1)
                    dve.wait_ge(gains_turned, 2)
                    own.step(V.tensor_copy(gains[:, NG1:NG], bank[1][:, 0:NG - NG1]))
                    V.tensor_tensor(gains[:, G_DQ:G_DQ + 1], gains[:, G_DQ:G_DQ + 1],
                                    gains[:, G_DK:G_DK + 1], ALU.mult)
                    V.tensor_tensor(gains[:, G_MQ:G_MQ + 2], gains[:, G_MQ:G_MQ + 2],
                                    gains[:, G_MK:G_MK + 2], ALU.mult).then_inc(gains_ready, 1)
                if u == LOW_AT + 17:
                    dve.wait_ge(lln_done, 1)
                    V.scalar_tensor_tensor(log_a[:, :, :], log_a[:, :, :], 0.0, labs[:, :, :],
                                           ALU.min, ALU.subtract).then_inc(log_a_done, 1)
                if u >= LEAD and (u - LEAD) % CPT == 7:
                    t = (u - LEAD) // CPT
                    squares(M_T, t // 2, t % 2, 0, MK)
            with dve.Fori(0, IN) as i:
                own.enter(i, 4)
                for t in range(2):
                    split_some(I0, i, IP, LEAD + t * CPT, CPT)
                    squares(I_T, i, t, 2, DQ)
                own.leave(IN)

            V.tensor_scalar(ms_z[:, :, 0:8].rearrange("p n (a b) -> p n a b", a=2), ssq_z[:, :, 2:4, :],
                            1.0 / DK, None, ALU.mult)
            for place, item in ((8, 5), (10, 0)):
                v = V.tensor_tensor(ms_z[:, :, place:place + 2], ssq_z[:, :, item, 0:4:2],
                                    ssq_z[:, :, item, 1:4:2], ALU.add)
            own.step(v)
            V.tensor_scalar(ms_z[:, :, 8:12], ms_z[:, :, 8:12], 1.0 / DH, None, ALU.mult).then_inc(ms_z_done, 1)
            dve.wait_ge(log_a_done, 1)
            V.memset(k_tail[CHUNK:P, 0, :, :], 0.0)
            V.memset(k_tail[0:CHUNK, 1, :, :], 0.0)
            V.memset(att[0:CHUNK, :, CHUNK:P], 0.0)
            own.step(V.memset(att[CHUNK:P, :, 0:CHUNK], 0.0))
            dve.wait_ge(lam_exp_done, 1)
            V.tensor_scalar(neg_lam[:, :], lam_exp[:, 1:2], lam_exp[:, 0:1], -LAM_INIT, ALU.subtract, ALU.add)
            split_some(L0, None, 0, LEAD, 6)
            dve.wait_ge(rms_z_done, 1)
            own.step(V.reciprocal(rstd_z[:, :, :], rstd_z[:, :, :]))
            for s in range(6, LP):
                split(L0, None, 0, LEAD + s)
                if s - 6 < 2 * HEADS:
                    n, branch = (s - 6) // 2, (s - 6) % 2
                    width = (DK, DH)[branch]
                    place, r, m = (DQ, MQ)[branch], (0, 8)[branch], 4 * DH // width
                    z = zh[:, n, place:place + 4 * DH].rearrange("p (g c) -> p g c", c=width)
                    own.step(V.tensor_tensor(z, z, rstd_z[:, n, r:r + m].unsqueeze(2).to_broadcast([P, m, width]),
                                             ALU.mult))
            for i in range(1, LN):
                B, per_unit, slots = 32, (P // 32) ** 2, LP - 2
                for s in range(LP):
                    split(L0, i, LP, LEAD + s)
                    for k in range(4 * per_unit):
                        if k * slots // (4 * per_unit) != s:
                            continue
                        unit, r, q = k // per_unit, k % per_unit // 4, k % 4
                        if k % per_unit == 0:
                            dve.wait_ge(qk_back, i * 4 + (unit - 3))
                        place = (DQ, MQ)[unit % 2]
                        z = zh[r * B:(r + 1) * B, i * 2 + (unit // 2 - 2), place:place + 4 * DH]
                        v = V.transpose(turned[q * B:(q + 1) * B, unit % 2, :, r * B:(r + 1) * B],
                                        z.rearrange("p (b c) -> p b c", c=P)[:, :, q * B:(q + 1) * B])
                        if k % per_unit == per_unit - 1:
                            v.then_inc(qk_turned, 1)
            dve.wait_ge(decay_done, 1)
            dve.wait_ge(acc_free[1], L_T + LN + 1)

            with dve.Fori(0, GN) as n:
                own.enter(n, DVE_HEAD_STEPS)

                def store_gates(t):
                    dve.wait_ge(chunk_used, nth(G0, n, GP, (t + 1) * CPT) + RING)
                    dve.wait_ge(bias_landed[t], 16 * (n + 1))
                    for h in range(HALVES):
                        v = V.scalar_tensor_tensor(gates[:, n * 2 + t, h, :], acc[t][:, h, :],
                                                   rstd_in[:, 1, h:h + 1], bias[:, t, :], ALU.mult, ALU.add)
                    own.step(v)
                    dve.sem_inc(acc_free[t], 1)
                    dve.sem_inc(bias_used, 1)

                def gla_decayed():
                    dve.wait_ge(ge_ready, n + 1)
                    zq, zk = zh[:, n, GQ:GQ + 2 * DK], zh[:, n, GK:GK + 2 * DK]
                    flat = lambda a: a.rearrange("p h c -> p (h c)")
                    V.scalar_tensor_tensor(flat(qd[:, :, :]), zq, DK ** -0.5, flat(qd[:, :, :]), ALU.mult, ALU.mult)
                    V.tensor_tensor(flat(kd[:, :, :]), zk, flat(kd[:, :, :]), ALU.mult)
                    V.tensor_copy(decay_h[:, :], decay[:, n, :])
                    for c in range(2):
                        r = slice(c * CHUNK, (c + 1) * CHUNK)
                        v = V.tensor_tensor(flat(k_tail[r, c, :, :]), zk[r, :], flat(e_tail[r, :, :]), ALU.mult)
                    own.step(v)
                    dve.sem_inc(gd_ready, 1)

                def gla_states():
                    dve.wait_ge(g_inc, n + 1)
                    own.step(V.tensor_copy(state[:, 0, :], bank[3][:, 0:DH]))
                    own.step(V.scalar_tensor_tensor(state[:, 1, :], state[:, 0, :], decay_h[:, 1:2],
                                                    bank[3][:, DH:2 * DH], ALU.mult, ALU.add))

                def gla_last_state():
                    dve.wait_ge(g_att, n + 1)
                    dve.wait_ge(ga_copied, n + 1)
                    V.scalar_tensor_tensor(state[:, 2, :], state[:, 1, :], decay_h[:, 2:3],
                                           bank[2][:, DH:2 * DH], ALU.mult, ALU.add).then_inc(gs_ready, 1)

                def diff_max():
                    dve.wait_ge(d_scores, n + 1)
                    s1 = bank[0][:, :].rearrange("p (j k) -> p j k", j=2)
                    s0 = bank[1][:, 0:2 * P].rearrange("p (j k) -> p j k", j=2)
                    V.memset(s1[0:CHUNK, :, 3 * CHUNK:4 * CHUNK], NEG)
                    own.step(V.memset(s0[0:CHUNK, :, CHUNK:2 * CHUNK], NEG))
                    V.reduce_max(rmax[:, 0:2], s1, AX.X)
                    own.step(V.reduce_max(rmax[:, 2:4], s0, AX.X))
                    V.tensor_scalar(nmax[:, 0:4], rmax[:, 0:4], -DK ** -0.5, None, ALU.mult).then_inc(dmax_ready, 1)

                def diff_weights():
                    dve.wait_ge(dp_ready, n + 1)
                    own.step(V.reciprocal(rsum[:, 0:4], psum_exp[:, 0:4]))
                    own.step(V.tensor_scalar(lam_r[:, :], rsum[:, 1:4:2], neg_lam[:, :], None, ALU.mult))
                    V.tensor_scalar(prob[:, 2 * P:4 * P], prob[:, 2 * P:4 * P], lam_r[:, 0:1], None, ALU.mult)
                    own.step(V.tensor_scalar(prob[:, 5 * P:6 * P], prob[:, 5 * P:6 * P], lam_r[:, 1:2], None, ALU.mult))
                    V.scalar_tensor_tensor(prob[:, 0:2 * P], prob[:, 0:2 * P], rsum[:, 0:1],
                                           prob[:, 2 * P:4 * P], ALU.mult, ALU.add)
                    V.scalar_tensor_tensor(prob[:, 4 * P:5 * P], prob[:, 4 * P:5 * P], rsum[:, 2:3],
                                           prob[:, 5 * P:6 * P], ALU.mult, ALU.add).then_inc(da_ready, 1)

                def mem_max():
                    dve.wait_ge(m_scores, n + 1)
                    own.step(V.reduce_max(rmax[:, 4:6], bank[1][:, :].rearrange("p (h k) -> p h k", h=2), AX.X))
                    V.tensor_scalar(nmax[:, 4:6], rmax[:, 4:6], -DH ** -0.5, None, ALU.mult).then_inc(mmax_ready, 1)

                def gla_silu():
                    dve.wait_ge(gg_exp, n + 1)
                    own.step(V.tensor_scalar(sg[:, :, :], sg[:, :, :], 1.0, None, ALU.add))
                    own.step(V.reciprocal(sg[:, :, :], sg[:, :, :]))
                    flat = sg[:, :, :].rearrange("p h c -> p (h c)")
                    own.step(V.tensor_tensor(flat, flat, zh[:, n, GG:GG + 2 * DH], ALU.mult))
                    own.step(V.tensor_tensor(sg[:, :, :], sg[:, :, :],
                                             gla_gain[:, :].unsqueeze(1).to_broadcast([P, HALVES, DH]), ALU.mult))

                def outputs():
                    dve.wait_ge(go_rms, n + 1)
                    own.step(V.reciprocal(rstd_o[:, :], rms_o[:, :]))
                    for h in range(HALVES):
                        v = V.scalar_tensor_tensor(sg[:, h, :], bank[2][:, h * DH:(h + 1) * DH],
                                                   rstd_o[:, 2 + h:3 + h], sg[:, h, :], ALU.mult, ALU.mult)
                    v.then_inc(gy_ready, 1)
                    for h in range(HALVES):
                        v = V.scalar_tensor_tensor(kn[:, h, :], bank[0][:, h * DH:(h + 1) * DH],
                                                   rstd_o[:, h:h + 1], sub_gain[:, :], ALU.mult, ALU.mult)
                    v.then_inc(dy_ready, 1)

                def mem_output():
                    dve.wait_ge(m_out, n + 1)
                    own.step(V.reciprocal(rsum[:, 4:6], psum_exp[:, 4:6]))
                    for h in range(HALVES):
                        v = V.tensor_scalar(qn[:, h, :], bank[1][:, h * DH:(h + 1) * DH], rsum[:, 4 + h:5 + h],
                                            None, ALU.mult)
                    v.then_inc(my_ready, 1)

                def y_lo(hi_done, b, place, done):
                    dve.wait_ge(hi_done, n + 1)
                    V.tensor_tensor(yt[:, n, place + 2 * DH:place + 4 * DH], bank[b][:, :],
                                    f32(yt[:, n, place:place + 2 * DH]), ALU.subtract).then_inc(done, 1)

                for s in range(GP):
                    if s == 4:
                        gla_last_state()
                    split(G0, n, GP, LEAD + s)
                    if s == 0:
                        gla_decayed()

                    if s == 2:
                        gla_states()
                    if s == 3:
                        diff_max()
                        diff_weights()
                        store_gates(0)
                    if s == 5:
                        gla_silu()
                    if s == 7:
                        outputs()
                        mem_max()
                    if s == 9:
                        y_lo(gy_hi, 2, GQ, gy_lo)
                        y_lo(dy_hi, 0, DQ, dy_lo)
                    if s == 10:
                        mem_output()
                    if s == 11:
                        store_gates(1)
                    if s == 13:
                        y_lo(my_hi, 1, MQ, my_lo)
                own.leave(GN)

            def turn_res_split(base, i, per, u):
                B = 32
                for h in range(HALVES):
                    for r in range(P // B):
                        if r % 2 == 0 and (h, r) != (1, 2):
                            split(base, i, per, u + 2 * h + r // 2)
                        for q in range(P // B):
                            block = res[r * B:(r + 1) * B, h, :].rearrange("p (k c) -> p k c", c=P)
                            v = V.transpose(res_t[q * B:(q + 1) * B, :, h * P + r * B:h * P + (r + 1) * B],
                                            block[:, :, q * B:(q + 1) * B])
                    v.then_inc(res_turned_v, 1)

            def turned_lo(k, lo, hi, first):
                for h in range(HALVES):
                    dve.wait_ge(res_hi, k * 2 + (h + 1))
                    t, cols = bass.ds(first, 4), slice(h * P, (h + 1) * P)
                    V.tensor_tensor(lo[:, t, cols], res_t[:, :, cols], f32(hi[:, t, cols]), ALU.subtract
                                    ).then_inc(res_lo, 1)

            with dve.Fori(0, BN) as c:
                own.enter(c, 3)
                split_some(B0, c, BP, LEAD, 4)
                dve.wait_ge(chunk_used, nth(B0, c, BP, CPT) + RING)
                dve.wait_ge(bias_landed[0], 16 * (c + (GN + 1)))
                for h in range(HALVES):
                    v = V.scalar_tensor_tensor(g2[:, h, :], acc[0][:, h, :], rstd_in[:, 1, h:h + 1],
                                               bias[:, 0, :], ALU.mult, ALU.add)
                own.step(v)
                dve.sem_inc(g2_ready, 1)
                dve.sem_inc(acc_free[0], 1)
                dve.sem_inc(bias_used, 1)
                for b in range(3):
                    split_some(B0, c, BP, LEAD + 4 * (b + 1), 4)
                    slot = (b + 1) % 2
                    dve.wait_ge(chunk_used, nth(B0, c, BP, CPT + (b + 1) * CPB) + RING)
                    dve.wait_ge((sig_g01, sig_g01, sig_g2)[b], c + 1)
                    g = (gates[:, c, :, :], gates[:, c + COLS, :, :], g2[:, :, :])[b]
                    v = V.tensor_tensor(g, g, acc[slot][:, :, :], ALU.mult)
                    v.then_inc(acc_free[slot], 1)
                    if b > 0:
                        dve.wait_ge(acc_free[slot], nth(B_T, c, 2, 3))
                        sums = gates[:, c, :, :]
                        if b == 1:
                            own.step(V.tensor_tensor(sums, sums, gates[:, c + COLS, :, :], ALU.add))
                        else:
                            own.step(V.tensor_tensor(res[:, :, :], sums, g2[:, :, :], ALU.add))
                            dve.sem_inc(res_ready, 1)
                turn_res_split(B0, c, BP, LEAD + 16)
                turned_lo(c, gt_lo, gt_hi, c * 4)
                split(B0, c, BP, LEAD + BP - 1)
                own.leave(BN)

            for t in range(COLS):
                split_some(O0, None, 0, LEAD + t * CPT, 4)
                k = BN + t
                s = t % 2
                dve.wait_ge(chunk_used, O0 + (t + 1) * CPT + RING)
                dve.wait_ge(xin_landed[s], 16 * (t // 2 + 1))
                if t > 0:
                    dve.wait_ge(x1_squared, t)
                V.tensor_tensor(res[:, :, :], acc[s][:, :, :], xin[:, s, :, :], ALU.add).then_inc(acc_free[s], 1)
                dve.wait_ge(acc_free[s], O_T + t // 2 + 2)
                dve.sem_inc(res_ready, 1)
                if t == COLS - 1:
                    dve.wait_ge(x1_squared, COLS)
                    V.reduce_sum(sum_x1[:, :], ssq_x1[:, :, :], AX.X).then_inc(x1_sum, 1)
                split_some(O0, None, 0, LEAD + t * CPT + 4, 4)
                for b in range(2):
                    dve.wait_ge(res_hi, 2 * k + b + 1)
                    for j in range(2):
                        kt = 4 * t + 2 * b + j
                        v = V.scalar_tensor_tensor(xt_lo[:, kt, :], bank[b][:, j * 2 * P:(j + 1) * 2 * P],
                                                   gains[:, G_FFN + kt:G_FFN + kt + 1], f32(xt_hi[:, kt, :]),
                                                   ALU.mult, ALU.subtract)
                    v.then_inc(res_lo, 1)
            dve.wait_ge(x1_rms, 1)
            V.reciprocal(rstd_x1[:, :], rms_x1[:, :]).then_inc(x1_rstd, 1)
            dve.wait_ge(x1_rstd, 1)
            with dve.Fori(0, FN) as i:
                split_some(F0, i, FP, LEAD, 12)
                dve.wait_ge(chunk_used, nth(F0, i, FP, FP) + RING)
                dve.wait_ge(acc_free[0], i + (F_T + 2))
                own.enter(i, 1)
                for h in range(HALVES):
                    v = V.scalar_tensor_tensor(res[:, h, :], acc[1][:, h, :], rstd_x1[:, h:h + 1], g2[:, h, :],
                                               ALU.mult, ALU.mult)
                own.step(v)
                dve.sem_inc(acc_free[1], 1)
                dve.sem_inc(res_ready, 1)
                turn_res_split(F0, i, FP, LEAD + 12)
                turned_lo(i + (BN + COLS), act_lo, act_hi, i * 4)
                split(F0, i, FP, LEAD + FP - 1)
                own.leave(FN)
            for t in range(COLS):
                u = LEAD + t * CPD
                last = t == COLS - 1
                split_some(D0, None, 0, u, CPD - LEAD if last else CPD - 4)
                cols = slice(t * TILE, (t + 1) * TILE)
                if last:
                    for h in range(HALVES):
                        if h == 0:
                            dve.wait_ge(half_done, 1)
                        else:
                            dve.wait_ge(chunk_used, END + RING)
                        V.tensor_tensor(fin[:, t, h, :], acc[t % 2][:, h, :], x1[:, h, cols], ALU.add
                                        ).then_inc(fin_ready, 1)
                    continue
                dve.wait_ge(chunk_used, D0 + (t + 1) * CPD + RING)
                V.tensor_tensor(fin[:, t, :, :], acc[t % 2][:, :, :], x1[:, :, cols], ALU.add
                                ).then_inc(acc_free[t % 2], 1)
                dve.wait_ge(acc_free[t % 2], D_T + t // 2 + 2)
                dve.sem_inc(fin_ready, 1)
                split_some(D0, None, 0, u + CPD - 4, 4)

        @block.gpsimd
        def _(pool):
            own = Tally(pool, pool_step)
            G = nc.gpsimd
            G.memset(eps[:, :], EPS).then_inc(eps_ready, 1)
            own.step(G.memset(ident[:, :], 0.0))
            G.affine_select(out=ident[:, :], in_=ident[:, :], compare_op=ALU.not_equal, fill=1.0, base=0,
                            pattern=[[-1, P]], channel_multiplier=1).then_inc(ident_ready, 1)
            G.memset(chunk_of[:, :], 0.0)
            G.memset(upto[:, :], 0.0)
            own.step(G.memset(after[:, :], 0.0))
            for c in range(2):
                r = slice(c * CHUNK, (c + 1) * CHUNK)
                G.memset(chunk_of[r, c:c + 1], 1.0)
                G.memset(upto[r, r], 1.0)
                m = G.memset(after[r, r], 1.0)
            own.step(m)
            G.affine_select(out=upto[:, :], in_=upto[:, :], compare_op=ALU.is_ge, fill=0.0, base=0,
                            pattern=[[1, P]], channel_multiplier=-1)
            G.affine_select(out=after[:, :], in_=after[:, :], compare_op=ALU.is_gt, fill=0.0, base=0,
                            pattern=[[-1, P]], channel_multiplier=1).then_inc(consts_ready, 1)
            with pool.Fori(0, GN) as n:
                pool.wait_ge(ga_copied, n + 1)
                pool.sem_inc(passed_pool, 1)
                for c in range(2):
                    r = slice(c * CHUNK, (c + 1) * CHUNK)
                    m = G.affine_select(out=att[r, :, r], in_=att[r, :, r], compare_op=ALU.is_ge, fill=0.0,
                                        base=0, pattern=[[0, HALVES], [1, CHUNK]], channel_multiplier=-1)
                m.then_inc(ga_ready, 1)


_INS = ["x", "mem", "norm_mix_g", "norm_mem_g", "w_in", "gla_w_alpha_up", "gla_b_alpha", "gla_norm_g",
        "diff_q_norm_g", "diff_k_norm_g", "diff_lambda_q1", "diff_lambda_k1", "diff_lambda_q2",
        "diff_lambda_k2", "diff_subln_g", "mem_q_norm_g", "mem_k_norm_g", "w_mem_kv", "w_branch",
        "w_gate", "b_gate", "w_out", "norm_ffn_g", "w_ffn_in", "w_ffn_down"]


def kernel(**inputs):
    import numpy as np
    import concourse.bacc as bacc
    from concourse.bass_utils import run_bass_kernel_spmd

    nc = bacc.Bacc("TRN2", target_bir_lowering=False, num_devices=1, dynamic_dma_scratch_size=1024)
    arrays, args = {}, []
    for name in _INS:
        a = np.ascontiguousarray(inputs[name])
        arrays[f"in_{name}"] = a
        args.append(nc.dram_tensor(f"in_{name}", a.shape, mybir.dt.from_np(a.dtype), kind="ExternalInput").ap())
    shape = inputs["x"].shape
    out = nc.dram_tensor("out", shape, FP32, kind="ExternalOutput").ap()
    hybrid_layer(nc, *args, out)
    result = run_bass_kernel_spmd(nc, [arrays], core_ids=[0])
    return result.results[0]["out"]
```
